# Optimizing a Trainium2 kernel written in Bass

```python
import jax, jax.numpy as jnp
from jax import lax
import numpy as np
import math
import jax
import jax.numpy as jnp

D_MODEL = 1024
BATCH = 1
SEQ = 512
DEPTH = 1

D_MIX = D_MODEL
D_REC = D_MIX // 2
D_ATT = D_MIX - D_REC
N_LRU_BLOCKS = 8
LRU_BLOCK = D_REC // N_LRU_BLOCKS
LRU_C = 8.0
CONV_WIDTH = 4
HEAD_DIM = 64
N_HEADS = D_ATT // HEAD_DIM
DILATED_PATTERNS = ((128, 1), (512, 4), (2048, 16))
ROPE_THETA = 10000.0
NORM_EPS = 1e-6
NEG_INF = -1e30
D_IN_PROJ = 2 * D_REC + 4 * D_ATT
SPLIT_IDX = (D_REC, 2 * D_REC, 2 * D_REC + D_ATT, 2 * D_REC + 2 * D_ATT, 2 * D_REC + 3 * D_ATT)


def rms_norm(x, g):
    xf = x.astype(jnp.float32)
    y = xf * lax.rsqrt(jnp.mean(xf * xf, axis=-1, keepdims=True) + NORM_EPS)
    return (y * g.astype(jnp.float32)).astype(x.dtype)

def rotary(x, positions):
    half = HEAD_DIM // 2
    inv_freq = ROPE_THETA ** (-jnp.arange(half, dtype=jnp.float32) / half)
    ang = positions.astype(jnp.float32)[..., None] * inv_freq
    cos = jnp.cos(ang)[:, :, None, :]
    sin = jnp.sin(ang)[:, :, None, :]
    xf = x.astype(jnp.float32)
    x1, x2 = xf[..., :half], xf[..., half:]
    out = jnp.concatenate([x1 * cos - x2 * sin, x2 * cos + x1 * sin], axis=-1)
    return out.astype(x.dtype)

def causal_depthwise_conv(x, w, b):
    S = x.shape[1]
    xp = jnp.pad(x, ((0, 0), (CONV_WIDTH - 1, 0), (0, 0)))
    return sum(xp[:, k:k + S, :] * w[k] for k in range(CONV_WIDTH)) + b

def rg_lru(x, w_a, b_a, w_x, b_x, lam):
    B, S, C = x.shape
    xb = x.reshape(B, S, N_LRU_BLOCKS, LRU_BLOCK)
    r = jax.nn.sigmoid(jnp.einsum('bshi,hij->bshj', xb, w_a).reshape(B, S, C) + b_a)
    i = jax.nn.sigmoid(jnp.einsum('bshi,hij->bshj', xb, w_x).reshape(B, S, C) + b_x)
    log_a = -LRU_C * r.astype(jnp.float32) * jax.nn.softplus(-lam.astype(jnp.float32))
    a = jnp.exp(log_a)
    mult = jnp.sqrt(-jnp.expm1(2.0 * log_a))
    u = mult * (i * x).astype(jnp.float32)

    def combine(left, right):
        a_l, b_l = left
        a_r, b_r = right
        return a_l * a_r, a_r * b_l + b_r

    _, h = lax.associative_scan(combine, (a, u), axis=1)
    return h.astype(x.dtype)

def dilated_attention(q, k, v, window, dilation):
    B, H, S, Dh = q.shape
    L = S // dilation
    blk = window // dilation
    n_blk = -(-L // blk)
    pad = n_blk * blk - L

    def to_blocks(t):
        t = t.reshape(B, H, L, dilation, Dh).transpose(0, 1, 3, 2, 4)
        t = jnp.pad(t, ((0, 0), (0, 0), (0, 0), (0, pad), (0, 0)))
        return t.reshape(B, H, dilation, n_blk, blk, Dh)

    def with_prev(t):
        prev = jnp.pad(t, ((0, 0), (0, 0), (0, 0), (1, 0), (0, 0), (0, 0)))[:, :, :, :-1]
        return jnp.concatenate([prev, t], axis=4)

    qb = to_blocks(q)
    kc = with_prev(to_blocks(k))
    vc = with_prev(to_blocks(v))
    scores = jnp.einsum('bhrnqd,bhrnkd->bhrnqk', qb, kc, preferred_element_type=jnp.float32)
    qi = jnp.arange(blk)[:, None]
    ki = jnp.arange(2 * blk)[None, :]
    dist = qi + blk - ki
    blk_idx = jnp.arange(n_blk)[:, None, None]
    valid = ((dist >= 0) & (dist <= blk))[None] & (blk_idx * blk + ki[None] - blk >= 0)
    scores = jnp.where(valid, scores, NEG_INF)
    m = jnp.max(scores, axis=-1, keepdims=True)
    p = jnp.exp(scores - m)
    denom = jnp.sum(p, axis=-1, keepdims=True)
    out = jnp.einsum('bhrnqk,bhrnkd->bhrnqd', p, vc.astype(jnp.float32)) / denom
    lse = (m + jnp.log(denom))[..., 0]

    def from_blocks(t):
        t = t.reshape(B, H, dilation, n_blk * blk, *t.shape[5:])[:, :, :, :L]
        t = jnp.moveaxis(t, 2, 3)
        return t.reshape(B, H, S, *t.shape[4:])

    return from_blocks(out), from_blocks(lse)

def first_inputs(seed: int = 0) -> dict:
    key = jax.random.key(seed)
    ks = jax.random.split(key, 20)
    D = D_MODEL
    nrm = lambda k, shape, fan_in: jax.random.normal(k, shape, jnp.float32) * fan_in ** -0.5
    x = jax.random.normal(ks[0], (BATCH, SEQ, D), jnp.float32)
    c = jax.random.normal(ks[1], (BATCH, D), jnp.float32)
    offsets = jax.random.randint(ks[2], (BATCH, 1), 0, 4096, dtype=jnp.int32)
    positions = offsets + jnp.arange(SEQ, dtype=jnp.int32)[None, :]
    w_ada = nrm(ks[3], (DEPTH, D, 3 * D), D) * 0.5
    b_ada = 0.02 * jax.random.normal(ks[4], (DEPTH, 3 * D), jnp.float32)
    norm_pre = 1.0 + 0.1 * jax.random.normal(ks[5], (DEPTH, D), jnp.float32)
    norm_post = 1.0 + 0.1 * jax.random.normal(ks[6], (DEPTH, D), jnp.float32)
    w_in = nrm(ks[7], (DEPTH, D, D_IN_PROJ), D)
    conv_w = nrm(ks[8], (DEPTH, CONV_WIDTH, D_REC), CONV_WIDTH)
    conv_b = 0.02 * jax.random.normal(ks[9], (DEPTH, D_REC), jnp.float32)
    w_rg_a = nrm(ks[10], (DEPTH, N_LRU_BLOCKS, LRU_BLOCK, LRU_BLOCK), LRU_BLOCK)
    b_rg_a = 0.02 * jax.random.normal(ks[11], (DEPTH, D_REC), jnp.float32)
    w_rg_x = nrm(ks[12], (DEPTH, N_LRU_BLOCKS, LRU_BLOCK, LRU_BLOCK), LRU_BLOCK)
    b_rg_x = 0.02 * jax.random.normal(ks[13], (DEPTH, D_REC), jnp.float32)
    a_c = jax.random.uniform(ks[14], (DEPTH, D_REC), jnp.float32, 0.9, 0.999)
    a_base = a_c ** (1.0 / LRU_C)
    lru_lambda = jnp.log(a_base) - jnp.log1p(-a_base)
    norm_rec = 1.0 + 0.1 * jax.random.normal(ks[15], (DEPTH, D_REC), jnp.float32)
    norm_att = 1.0 + 0.1 * jax.random.normal(ks[16], (DEPTH, D_ATT), jnp.float32)
    w_out = nrm(ks[17], (DEPTH, D_MIX, D), D_MIX)
    return {'x': x, 'c': c, 'positions': positions, 'w_ada': w_ada, 'b_ada': b_ada,
            'norm_pre': norm_pre, 'norm_post': norm_post, 'w_in': w_in, 'conv_w': conv_w,
            'conv_b': conv_b, 'w_rg_a': w_rg_a, 'b_rg_a': b_rg_a, 'w_rg_x': w_rg_x,
            'b_rg_x': b_rg_x, 'lru_lambda': lru_lambda, 'norm_rec': norm_rec,
            'norm_att': norm_att, 'w_out': w_out}

def first_block(x, c, positions, w_ada, b_ada, norm_pre, norm_post, w_in, conv_w, conv_b,
              w_rg_a, b_rg_a, w_rg_x, b_rg_x, lru_lambda, norm_rec, norm_att, w_out):
    B, S, _ = x.shape
    for l in range(DEPTH):
        mod = jnp.einsum('bd,de->be', jax.nn.silu(c), w_ada[l]) + b_ada[l]
        shift, scale, gate = jnp.split(mod, 3, axis=-1)
        h = rms_norm(x, norm_pre[l]) * (1.0 + scale[:, None, :]) + shift[:, None, :]

        proj = jnp.einsum('bsd,de->bse', h, w_in[l])
        xa, ga, q, k, v, gb = jnp.split(proj, SPLIT_IDX, axis=-1)

        xa = causal_depthwise_conv(xa, conv_w[l], conv_b[l])
        ya = rg_lru(xa, w_rg_a[l], b_rg_a[l], w_rg_x[l], b_rg_x[l], lru_lambda[l]) * jax.nn.silu(ga)
        ya = rms_norm(ya, norm_rec[l])

        heads = lambda t: t.reshape(B, S, N_HEADS, HEAD_DIM)
        qh = (rotary(heads(q), positions) * HEAD_DIM ** -0.5).transpose(0, 2, 1, 3)
        kh = rotary(heads(k), positions).transpose(0, 2, 1, 3)
        vh = heads(v).transpose(0, 2, 1, 3)
        outs, lses = zip(*[dilated_attention(qh, kh, vh, w, d) for (w, d) in DILATED_PATTERNS])
        wts = jax.nn.softmax(jnp.stack(lses, axis=0), axis=0)
        att = jnp.einsum('pbhs,pbhsd->bhsd', wts, jnp.stack(outs, axis=0))
        yb = att.transpose(0, 2, 1, 3).reshape(B, S, D_ATT).astype(x.dtype) * jax.nn.silu(gb)
        yb = rms_norm(yb, norm_att[l])

        mix = jnp.einsum('bse,ed->bsd', jnp.concatenate([ya, yb], axis=-1), w_out[l])
        x = x + gate[:, None, :] * rms_norm(mix, norm_post[l])
    return x


GRID_W = 64
CTX_LEN = 256
N_BRANCH = 3
BRANCH_WIDTH = D_MODEL // 2
POOL_WINDOWS = (2, 4, 8, 16)
POOL_GROUPS = len(POOL_WINDOWS)
POOL_GROUP_DIM = BRANCH_WIDTH // POOL_GROUPS
DIFF_HEAD_DIM = 64
DIFF_HEADS = BRANCH_WIDTH // (2 * DIFF_HEAD_DIM)
DIFF_V_DIM = 2 * DIFF_HEAD_DIM
DIFF_QK_WIDTH = DIFF_HEADS * 2 * DIFF_HEAD_DIM
DIFF_V_WIDTH = DIFF_HEADS * DIFF_V_DIM
ROPE_AXIS_FREQS = DIFF_HEAD_DIM // 4
Q_BLOCK = 128
RWKV_HEAD = 64
RWKV_HEADS = BRANCH_WIDTH // RWKV_HEAD
RWKV_WIDTH = RWKV_HEADS * RWKV_HEAD
DECAY_LORA = 64
AAA_LORA = 64
GATE_LORA = 128
RWKV_SPLITS = (RWKV_WIDTH, RWKV_WIDTH, RWKV_WIDTH, 2 * DECAY_LORA, 2 * AAA_LORA, GATE_LORA)
RWKV_IN = 3 * RWKV_WIDTH + 2 * DECAY_LORA + 2 * AAA_LORA + GATE_LORA
IN_SPLITS = (BRANCH_WIDTH, DIFF_QK_WIDTH, DIFF_QK_WIDTH, DIFF_V_WIDTH, RWKV_IN, N_BRANCH * D_MODEL)
IN_WIDTH = BRANCH_WIDTH + 2 * DIFF_QK_WIDTH + DIFF_V_WIDTH + RWKV_IN + N_BRANCH * D_MODEL
N_GROUPS = 4
EXPERTS_PER_GROUP = 8
N_EXPERTS = N_GROUPS * EXPERTS_PER_GROUP
TOP_K = 2
EXPERT_FF = D_MODEL // 2
MOE_BLOCK = 128
N_MOD = 6
GN_EPS = 64e-5


def split_cols(p, sizes):
    return jnp.split(p, [int(s) for s in np.cumsum(sizes)[:-1]], axis=-1)

def rms_norm_2(x, g):
    xf = x.astype(jnp.float32)
    y = xf * lax.rsqrt(jnp.mean(xf * xf, axis=-1, keepdims=True) + NORM_EPS)
    return (y * g.astype(jnp.float32)).astype(x.dtype)

def modulate(x, g, shift, scale):
    return rms_norm_2(x, g) * (1 + scale) + shift

def centred_window_mean(u, win):
    L = u.shape[1]
    cs = jnp.pad(jnp.cumsum(u.astype(jnp.float32), axis=1), ((0, 0), (1, 0), (0, 0)))
    t = jnp.arange(L)
    lo = jnp.clip(t - win // 2, 0, L - 1)
    hi = jnp.clip(t + win // 2 - 1, 0, L - 1)
    cnt = (hi - lo + 1).astype(jnp.float32)
    return (cs[:, hi + 1] - cs[:, lo]) / cnt[None, :, None]

def pool_mixer(u, w_pool, pool_scale):
    B, L, _ = u.shape
    ug = u.reshape(B, L, POOL_GROUPS, POOL_GROUP_DIM)
    pooled = jnp.stack([centred_window_mean(ug[:, :, i], w) for i, w in enumerate(POOL_WINDOWS)], axis=2)
    diff = pooled.astype(u.dtype) - ug
    y = jnp.einsum('blgc,gcd->blgd', diff, w_pool)
    return y.reshape(B, L, BRANCH_WIDTH) * pool_scale

def rope_rotate(u, ang):
    u1, u2 = jnp.split(u, 2, axis=-1)
    cs = jnp.cos(ang).astype(u.dtype)
    sn = jnp.sin(ang).astype(u.dtype)
    return jnp.concatenate([u1 * cs - u2 * sn, u2 * cs + u1 * sn], axis=-1)

def axial_rope(x, ang_r, ang_c):
    xr, xc = jnp.split(x, 2, axis=-1)
    ar = ang_r[None, :, None, None, :]
    ac = ang_c[None, :, None, None, :]
    return jnp.concatenate([rope_rotate(xr, ar), rope_rotate(xc, ac)], axis=-1)

def diff_qkv(pq, pk, pv, qn_g, kn_g):
    B, L, _ = pq.shape
    q = rms_norm_2(pq.reshape(B, L, DIFF_HEADS, 2, DIFF_HEAD_DIM), qn_g)
    k = rms_norm_2(pk.reshape(B, L, DIFF_HEADS, 2, DIFF_HEAD_DIM), kn_g)
    v = pv.reshape(B, L, DIFF_HEADS, DIFF_V_DIM)
    return q, k, v

def diff_attn_block(qb, keys, vals, lam):
    s = jnp.einsum('bqhmd,bkhmd->bhmqk', qb, keys).astype(jnp.float32) * (DIFF_HEAD_DIM ** -0.5)
    p = jax.nn.softmax(s, axis=-1)
    a = p[:, :, 0] - lam * p[:, :, 1]
    return jnp.einsum('bhqk,bkhv->bqhv', a.astype(vals.dtype), vals)

def diff_attn_latent(q, keys, vals, lam):
    B, L = q.shape[:2]
    nb = L // Q_BLOCK
    qb = jnp.moveaxis(q.reshape(B, nb, Q_BLOCK, DIFF_HEADS, 2, DIFF_HEAD_DIM), 1, 0)
    out = lax.map(lambda blk: diff_attn_block(blk, keys, vals, lam), qb)
    return jnp.moveaxis(out, 0, 1).reshape(B, L, DIFF_HEADS, DIFF_V_DIM)

def diff_post(o, subln_g, lam_init):
    B, L = o.shape[:2]
    return (rms_norm_2(o, subln_g) * (1 - lam_init)).reshape(B, L, DIFF_V_WIDTH)

def token_shift_centred(u, mu):
    prev = jnp.pad(u, ((0, 0), (1, 0), (0, 0)))[:, :-1]
    nxt = jnp.pad(u, ((0, 0), (0, 1), (0, 0)))[:, 1:]
    return u + (prev - u) * mu[0] + (nxt - u) * mu[1]

def rwkv_prepare(pr, shift_mu, w0, w2, a0, a2, g2, k_k, k_a):
    B, L, _ = pr.shape
    u = token_shift_centred(pr, shift_mu)
    r, k, v, wl, al, gl = split_cols(u, RWKV_SPLITS)
    wl = wl.reshape(B, L, 2, DECAY_LORA)
    al = al.reshape(B, L, 2, AAA_LORA)
    w_log = -jax.nn.softplus(-(w0 + jnp.einsum('bldr,drc->bldc', jnp.tanh(wl), w2))) - 0.5
    decay = jnp.exp(-jnp.exp(w_log.astype(jnp.float32)))
    a = jax.nn.sigmoid(a0 + jnp.einsum('bldr,drc->bldc', al, a2))
    g = jax.nn.sigmoid(gl) @ g2
    kk = (k * k_k).reshape(B, L, RWKV_HEADS, RWKV_HEAD).astype(jnp.float32)
    kk = kk / jnp.maximum(jnp.sqrt(jnp.sum(kk * kk, axis=-1, keepdims=True)), 1e-12)
    kk = kk.reshape(B, L, RWKV_WIDTH).astype(k.dtype)
    k_mod = k[:, :, None] * (1 + (a - 1) * k_a)
    b_vec = kk[:, :, None] * a
    return r, k_mod, v, decay, -kk, b_vec, g

def to_scan(u):
    B, L = u.shape[:2]
    u = jnp.stack([u[:, :, 0], jnp.flip(u[:, :, 1], axis=1)], axis=0)
    return jnp.moveaxis(u.reshape(2, B, L, RWKV_HEADS, RWKV_HEAD), 2, 0).astype(jnp.float32)

def wkv_step(S, inp):
    r, w, k, v, a, b = inp
    sa = jnp.einsum('dbhvk,dbhk->dbhv', S, a)
    S = S * w[..., None, :] + sa[..., None] * b[..., None, :] + v[..., None] * k[..., None, :]
    return S, jnp.einsum('dbhvk,dbhk->dbhv', S, r)

def wkv_bidir(S0, r, k_mod, v, decay, a_vec, b_vec):
    B, L, C = r.shape
    both = lambda u: jnp.broadcast_to(u[:, :, None], (B, L, 2, C))
    xs = tuple(to_scan(u) for u in (both(r), decay, k_mod, both(v), both(a_vec), b_vec))
    S, ys = lax.scan(wkv_step, S0, xs)
    y = ys[:, 0] + jnp.flip(ys[:, 1], axis=0)
    return S, jnp.moveaxis(y, 0, 1)

def rwkv_output(y, prep, r_k, gn_w, gn_b):
    r, k_mod, v, g = prep[0], prep[1], prep[2], prep[6]
    B, L, _ = r.shape
    mu = jnp.mean(y, axis=-1, keepdims=True)
    var = jnp.mean(jnp.square(y - mu), axis=-1, keepdims=True)
    yn = ((y - mu) * lax.rsqrt(var + GN_EPS)).reshape(B, L, RWKV_WIDTH) * gn_w + gn_b
    coef = jnp.sum((r[:, :, None] * k_mod * r_k.reshape(-1)).reshape(B, L, 2, RWKV_HEADS, RWKV_HEAD), axis=(2, 4))
    bonus = (coef[..., None] * v.reshape(B, L, RWKV_HEADS, RWKV_HEAD)).reshape(B, L, RWKV_WIDTH)
    return (yn.astype(r.dtype) + bonus) * g

def merge_branches(branches, gates, w_br, w_out):
    B, L, _ = gates.shape
    g = jax.nn.sigmoid(gates.reshape(B, L, N_BRANCH, D_MODEL))
    merged = g[:, :, 0] * (branches[0] @ w_br[0])
    for n in range(1, N_BRANCH):
        merged = merged + g[:, :, n] * (branches[n] @ w_br[n])
    return merged @ w_out

def expert_dispatch(h, eid, gates, w_g, w_u, w_d):
    T, D = h.shape
    A = T * TOP_K
    flat_e = eid.reshape(A)
    flat_tok = jnp.repeat(jnp.arange(T, dtype=jnp.int32), TOP_K)
    order = jnp.argsort(flat_e)
    e_sorted = flat_e[order]
    counts = jnp.bincount(flat_e, length=N_EXPERTS)
    padded = (counts + MOE_BLOCK - 1) // MOE_BLOCK * MOE_BLOCK
    start = jnp.cumsum(counts) - counts
    pend = jnp.cumsum(padded)
    pstart = pend - padded
    slot = pstart[e_sorted] + jnp.arange(A, dtype=jnp.int32) - start[e_sorted]
    P = -(-A // MOE_BLOCK) * MOE_BLOCK + N_EXPERTS * MOE_BLOCK
    n_blk = P // MOE_BLOCK
    slot_tok = jnp.full((P,), T, jnp.int32).at[slot].set(flat_tok[order])
    slot_gate = jnp.zeros((P,), h.dtype).at[slot].set(gates.reshape(A)[order])
    blk_e = jnp.minimum(jnp.searchsorted(pend, jnp.arange(n_blk, dtype=jnp.int32) * MOE_BLOCK, side='right'), N_EXPERTS - 1)
    xb = jnp.concatenate([h, jnp.zeros((1, D), h.dtype)], axis=0)[slot_tok].reshape(n_blk, MOE_BLOCK, D)

    def block_ffn(args):
        xblk, e = args
        return (jax.nn.silu(xblk @ w_g[e]) * (xblk @ w_u[e])) @ w_d[e]

    yb = lax.map(block_ffn, (xb, blk_e)).reshape(P, D)
    return jax.ops.segment_sum(yb * slot_gate[:, None], slot_tok, num_segments=T + 1)[:T]

def hier_moe(h, w_rg, w_re, w_g, w_u, w_d):
    T = h.shape[0]
    lg = (h @ w_rg).astype(jnp.float32)
    grp = jnp.argmax(lg, axis=-1)
    p_grp = jnp.take_along_axis(jax.nn.softmax(lg, axis=-1), grp[:, None], axis=-1)
    le = (h @ w_re).astype(jnp.float32).reshape(T, N_GROUPS, EXPERTS_PER_GROUP)
    le = jnp.take_along_axis(le, grp[:, None, None], axis=1)[:, 0]
    top_v, top_i = lax.top_k(le, TOP_K)
    gates = p_grp * jax.nn.softmax(top_v, axis=-1)
    eid = (grp[:, None] * EXPERTS_PER_GROUP + top_i).astype(jnp.int32)
    return expert_dispatch(h, eid, gates.astype(h.dtype), w_g, w_u, w_d)

def second_inputs(seed: int = 0) -> dict:
    key = jax.random.key(seed)
    keys = jax.random.split(key, 40)
    cnt = [0]

    def nk():
        cnt[0] += 1
        return keys[cnt[0] - 1]

    def nrm(shape, scale):
        return scale * jax.random.normal(nk(), shape, jnp.float32)

    def uni(shape, lo, hi):
        return jax.random.uniform(nk(), shape, jnp.float32, lo, hi)

    D = D_MODEL
    return {
        'x': nrm((BATCH, SEQ, D), 1.0),
        'c': nrm((BATCH, D), 1.0),
        'ctx': nrm((BATCH, CTX_LEN, D), 1.0),
        'c_ctx': nrm((D,), 1.0),
        'w_ada': nrm((DEPTH, D, N_MOD * D), 0.5 * D ** -0.5),
        'b_ada': nrm((DEPTH, N_MOD * D), 0.02),
        'norm1_g': 1.0 + nrm((DEPTH, D), 0.05),
        'norm2_g': 1.0 + nrm((DEPTH, D), 0.05),
        'w_in': nrm((DEPTH, D, IN_WIDTH), D ** -0.5),
        'pool_w': nrm((DEPTH, POOL_GROUPS, POOL_GROUP_DIM, POOL_GROUP_DIM), POOL_GROUP_DIM ** -0.5),
        'pool_scale': 1.0 + nrm((DEPTH, BRANCH_WIDTH), 0.1),
        'q_norm_g': 1.0 + nrm((DEPTH, DIFF_HEAD_DIM), 0.05),
        'k_norm_g': 1.0 + nrm((DEPTH, DIFF_HEAD_DIM), 0.05),
        'lambda_qk': nrm((DEPTH, 4, DIFF_HEAD_DIM), 0.1),
        'subln_g': 1.0 + nrm((DEPTH, DIFF_V_DIM), 0.05),
        'shift_mu': uni((DEPTH, 2, RWKV_IN), 0.0, 0.5),
        'decay_w0': uni((DEPTH, 2, RWKV_WIDTH), -4.0, 1.0),
        'decay_w2': nrm((DEPTH, 2, DECAY_LORA, RWKV_WIDTH), 0.5 * DECAY_LORA ** -0.5),
        'aaa_a0': nrm((DEPTH, 2, RWKV_WIDTH), 0.5),
        'aaa_a2': nrm((DEPTH, 2, AAA_LORA, RWKV_WIDTH), 0.5 * AAA_LORA ** -0.5),
        'gate_w2': nrm((DEPTH, GATE_LORA, RWKV_WIDTH), GATE_LORA ** -0.5),
        'k_k': 0.85 + nrm((DEPTH, RWKV_WIDTH), 0.1),
        'k_a': 1.0 + nrm((DEPTH, RWKV_WIDTH), 0.1),
        'r_k': nrm((DEPTH, RWKV_HEADS, RWKV_HEAD), 0.1),
        'gn_w': 1.0 + nrm((DEPTH, RWKV_WIDTH), 0.05),
        'gn_b': nrm((DEPTH, RWKV_WIDTH), 0.02),
        'w_br': nrm((DEPTH, N_BRANCH, BRANCH_WIDTH, D), BRANCH_WIDTH ** -0.5),
        'w_out': nrm((DEPTH, D, D), D ** -0.5),
        'w_router_group': nrm((DEPTH, D, N_GROUPS), D ** -0.5),
        'w_router_expert': nrm((DEPTH, D, N_EXPERTS), D ** -0.5),
        'w_exp_gate': nrm((DEPTH, N_EXPERTS, D, EXPERT_FF), D ** -0.5),
        'w_exp_up': nrm((DEPTH, N_EXPERTS, D, EXPERT_FF), D ** -0.5),
        'w_exp_down': nrm((DEPTH, N_EXPERTS, EXPERT_FF, D), EXPERT_FF ** -0.5),
    }

def second_block(x, c, ctx, c_ctx, w_ada, b_ada, norm1_g, norm2_g, w_in, pool_w, pool_scale, q_norm_g, k_norm_g,
              lambda_qk, subln_g, shift_mu, decay_w0, decay_w2, aaa_a0, aaa_a2, gate_w2, k_k, k_a, r_k, gn_w, gn_b,
              w_br, w_out, w_router_group, w_router_expert, w_exp_gate, w_exp_up, w_exp_down):
    B, L, D = x.shape
    C = ctx.shape[1]
    rows = L // GRID_W
    row_idx = jnp.repeat(jnp.arange(rows), GRID_W).astype(jnp.float32)
    col_idx = jnp.tile(jnp.arange(GRID_W), rows).astype(jnp.float32)
    inv_freq = ROPE_THETA ** (-jnp.arange(ROPE_AXIS_FREQS, dtype=jnp.float32) / ROPE_AXIS_FREQS)
    ang_r = row_idx[:, None] * inv_freq
    ang_c = col_idx[:, None] * inv_freq
    s_lat = jax.nn.silu(c)
    s_ctx = jax.nn.silu(c_ctx)
    S0 = jnp.zeros((2, B, RWKV_HEADS, RWKV_HEAD, RWKV_HEAD), jnp.float32)

    for l in range(DEPTH):
        last = l == DEPTH - 1
        mod = (s_lat @ w_ada[l] + b_ada[l]).reshape(B, N_MOD, 1, D)
        mod_c = (s_ctx @ w_ada[l] + b_ada[l]).reshape(N_MOD, 1, 1, D)

        p_l = modulate(x, norm1_g[l], mod[:, 0], mod[:, 1]) @ w_in[l]
        p_c = modulate(ctx, norm1_g[l], mod_c[0], mod_c[1]) @ w_in[l]
        pool_l, q_l, k_l, v_l, rw_l, gate_l = split_cols(p_l, IN_SPLITS)
        pool_c, q_c, k_c, v_c, rw_c, gate_c = split_cols(p_c, IN_SPLITS)

        lam_init = 0.8 - 0.6 * math.exp(-0.3 * l)
        lq = lambda_qk[l].astype(jnp.float32)
        lam = jnp.exp(jnp.sum(lq[0] * lq[1])) - jnp.exp(jnp.sum(lq[2] * lq[3])) + lam_init
        qh_l, kh_l, vh_l = diff_qkv(q_l, k_l, v_l, q_norm_g[l], k_norm_g[l])
        qh_l = axial_rope(qh_l, ang_r, ang_c)
        kh_l = axial_rope(kh_l, ang_r, ang_c)
        qh_c, kh_c, vh_c = diff_qkv(q_c, k_c, v_c, q_norm_g[l], k_norm_g[l])
        keys = jnp.concatenate([kh_c, kh_l], axis=1)
        vals = jnp.concatenate([vh_c, vh_l], axis=1)
        att_l = diff_post(diff_attn_latent(qh_l, keys, vals, lam), subln_g[l], lam_init)

        rw_par = (shift_mu[l], decay_w0[l], decay_w2[l], aaa_a0[l], aaa_a2[l], gate_w2[l], k_k[l], k_a[l])
        prep_c = rwkv_prepare(rw_c, *rw_par)
        S_c, y_c = wkv_bidir(S0, *prep_c[:6])
        prep_l = rwkv_prepare(rw_l, *rw_par)
        _, y_l = wkv_bidir(S_c, *prep_l[:6])
        rwo_l = rwkv_output(y_l, prep_l, r_k[l], gn_w[l], gn_b[l])

        mix_l = merge_branches((pool_mixer(pool_l, pool_w[l], pool_scale[l]), att_l, rwo_l), gate_l, w_br[l], w_out[l])
        x = x + mod[:, 2] * mix_l
        if not last:
            att_c = diff_post(diff_attn_block(qh_c, kh_c, vh_c, lam), subln_g[l], lam_init)
            rwo_c = rwkv_output(y_c, prep_c, r_k[l], gn_w[l], gn_b[l])
            mix_c = merge_branches((pool_mixer(pool_c, pool_w[l], pool_scale[l]), att_c, rwo_c), gate_c, w_br[l], w_out[l])
            ctx = ctx + mod_c[2] * mix_c

        moe_par = (w_router_group[l], w_router_expert[l], w_exp_gate[l], w_exp_up[l], w_exp_down[l])
        f_l = modulate(x, norm2_g[l], mod[:, 3], mod[:, 4]).reshape(B * L, D)
        if last:
            x = x + mod[:, 5] * hier_moe(f_l, *moe_par).reshape(B, L, D)
        else:
            f_c = modulate(ctx, norm2_g[l], mod_c[3], mod_c[4]).reshape(B * C, D)
            y = hier_moe(jnp.concatenate([f_c, f_l], axis=0), *moe_par)
            ctx = ctx + mod_c[5] * y[:B * C].reshape(B, C, D)
            x = x + mod[:, 5] * y[B * C:].reshape(B, L, D)
    return x


def setup_inputs(seed=0):
    out = dict(first_inputs(seed))
    for name, value in second_inputs(seed + 1).items():
        if name != "x":
            out[name + "_2"] = value
    return out


def reference(
    x, c, positions, w_ada, b_ada, norm_pre, norm_post, w_in, conv_w, conv_b, w_rg_a, b_rg_a,
    w_rg_x, b_rg_x, lru_lambda, norm_rec, norm_att, w_out, c_2, ctx_2, c_ctx_2, w_ada_2,
    b_ada_2, norm1_g_2, norm2_g_2, w_in_2, pool_w_2, pool_scale_2, q_norm_g_2, k_norm_g_2,
    lambda_qk_2, subln_g_2, shift_mu_2, decay_w0_2, decay_w2_2, aaa_a0_2, aaa_a2_2, gate_w2_2,
    k_k_2, k_a_2, r_k_2, gn_w_2, gn_b_2, w_br_2, w_out_2, w_router_group_2, w_router_expert_2,
    w_exp_gate_2, w_exp_up_2, w_exp_down_2,
):
    x = first_block(
        x, c, positions, w_ada, b_ada, norm_pre, norm_post, w_in, conv_w, conv_b, w_rg_a,
        b_rg_a, w_rg_x, b_rg_x, lru_lambda, norm_rec, norm_att, w_out,
    )
    return second_block(
        x, c_2, ctx_2, c_ctx_2, w_ada_2, b_ada_2, norm1_g_2, norm2_g_2, w_in_2, pool_w_2,
        pool_scale_2, q_norm_g_2, k_norm_g_2, lambda_qk_2, subln_g_2, shift_mu_2, decay_w0_2,
        decay_w2_2, aaa_a0_2, aaa_a2_2, gate_w2_2, k_k_2, k_a_2, r_k_2, gn_w_2, gn_b_2, w_br_2,
        w_out_2, w_router_group_2, w_router_expert_2, w_exp_gate_2, w_exp_up_2, w_exp_down_2,
    )


_drawn_inputs = setup_inputs


def setup_inputs(seed=0):
    import zlib

    import numpy as np

    out = dict(_drawn_inputs(seed))
    spreads = {}
    factors = {'conv_b': 3.531,
     'b_rg_a': 8.0,
     'b_rg_x': 8.0,
     'norm1_g_2': 4.24,
     'norm2_g_2': 3.234,
     'pool_scale_2': 3.405,
     'q_norm_g_2': 8.0,
     'k_norm_g_2': 8.0,
     'lambda_qk_2': 4.548,
     'subln_g_2': 27.596,
     'decay_w2_2': 6.55,
     'aaa_a0_2': 2.711,
     'aaa_a2_2': 3.628,
     'k_k_2': 22.417,
     'k_a_2': 3.399,
     'gn_w_2': 43.028,
     'gn_b_2': 64.0}
    for name, (base, spread) in spreads.items():
        noise = np.random.default_rng([zlib.crc32(name.encode()), seed]).standard_normal(out[name].shape)
        drawn = base * np.exp(spread * noise) if base else spread * noise
        out[name] = jnp.asarray(drawn.astype(out[name].dtype))
    for name, factor in factors.items():
        out[name] = (out[name] * factor).astype(out[name].dtype)
    return out
```

```python
import math
from contextlib import ExitStack

import numpy as np

import concourse.bass as bass
from concourse import mybir

F = mybir.dt.float32
I32 = mybir.dt.int32
U32 = mybir.dt.uint32
ALU = mybir.AluOpType
ACT = mybir.ActivationFunctionType
AX = mybir.AxisListType.X

D = 1024
S = 512
CTX = 256
NB = 39
OVF = 7
KAPPA = math.exp(-0.5)
EPS = 1e-6
GN_EPS = 64e-5
NCOL = 53100

COL_SPEC = [
    ("c", 8), ("c2", 8), ("cc", 8), ("conv_w", 16), ("conv_b", 4), ("b_a", 4), ("b_x", 4), ("lam", 4),
    ("norm_rec", 4), ("qn", 1), ("kn", 1), ("mu0", 15), ("mu1", 15), ("w0", 8), ("a0", 8), ("k_k", 4),
    ("k_a", 4), ("r_k", 4), ("pscale", 4),
]
COLS = {}
_o = 0
for _n, _w in COL_SPEC:
    COLS[_n] = (_o, _o + _w)
    _o += _w
NPARAM = _o

CONST_SPEC = [
    ("ident", 128), ("ones", 128), ("blk64", 128), ("perm1", 128), ("perm2", 128), ("tri", 128),
    ("selp", 36), ("invf", 1), ("sgn", 1), ("iota32", 32), ("grp32", 32), ("ind", 32),
]
MASK_SPEC = [("lm0", 7 * 128), ("lm1", 7 * 128), ("si0", 256), ("si1", 256), ("sb0", 128), ("sb1", 128)]
ROPE_SPEC = [("cos2", 512), ("sin2", 512), ("cnt", 2048)]


def offsets(spec):
    out, o = {}, 0
    for n, w in spec:
        out[n] = (o, o + w)
        o += w
    return out, o


CONSTS, NCONST = offsets(CONST_SPEC)
MASKS, NMASK = offsets(MASK_SPEC)
ROPES, NROPE = offsets(ROPE_SPEC)
LNC_OFF = [0, 128, 384, 768]
LNC_N = 1280


class Dma:

    def __init__(self, sem):
        self.sem, self.n = sem, 0

    def add(self):
        self.n += 16
        return (self.sem, self.n)


class Lane:

    def __init__(self, sem, chain):
        self.sem, self.n, self.items, self.chain = sem, 0, [], chain

    def put(self, fns, after):
        own = [(self.sem, self.n)] if self.chain and self.n else []
        self.items.append((fns, list(after) + own, (self.sem, 1)))
        self.n += 1
        return (self.sem, self.n)

    def last(self):
        return (self.sem, self.n)

    def dma(self, out, in_, d, *after):
        tok = d.add()
        self.items.append(([lambda e: e.dma_start(out, in_)], list(after), (d.sem, 16)))
        return tok

    def run(self, e, seen):
        for fns, after, inc in self.items:
            need = {}
            for t in after:
                if t is not None:
                    need[id(t[0])] = max(t, need.get(id(t[0]), t), key=lambda q: q[1])
            for k, (sem, v) in need.items():
                if v > seen.get(k, 0):
                    seen[k] = v
                    e.wait_ge(sem, v)
            for f in fns:
                ins = f(e)
            if inc is not None:
                ins.then_inc(*inc)

    def tt(self, out, a, b, op, *after):
        return self.put([lambda e: e.tensor_tensor(out, a, b, op)], after)

    def ts(self, out, a, s1, s2, op0, op1, *after):
        if s2 is None:
            return self.put([lambda e: e.tensor_scalar(out, a, s1, None, op0)], after)
        return self.put([lambda e: e.tensor_scalar(out, a, s1, s2, op0, op1)], after)

    def stt(self, out, a, s, b, op0, op1, *after):
        return self.put([lambda e: e.scalar_tensor_tensor(out=out, in0=a, scalar=s, in1=b, op0=op0, op1=op1)], after)

    def cp(self, out, a, *after):
        return self.put([lambda e: e.tensor_copy(out, a)], after)

    def rec(self, out, a, *after):
        return self.put([lambda e: e.reciprocal(out, a)], after)

    def zero(self, out, *after, value=0.0):
        return self.put([lambda e: e.memset(out, value)], after)

    def red(self, out, a, op, *after, negate=None):
        return self.put([lambda e: e.tensor_reduce(out, a, AX, op, negate=negate)], after)

    def pred(self, out, mask, a, *after):
        return self.put([lambda e: e.copy_predicated(out, mask, a)], after)

    def scan(self, out, d0, d1, *after):
        return self.put([lambda e: e.tensor_tensor_scan(out, d0, d1, 0.0, ALU.mult, ALU.add)], after)

    def act(self, out, a, func, *after, **kw):
        return self.put([lambda e: e.activation(out, a, func, **kw)], after)

    def mm(self, group, *after):
        return self.put([lambda e, g=g: e.matmul(g[0], g[1], g[2], start=g[3], stop=g[4]) for g in group], after)

    def tr(self, group, ident, *after):
        return self.put([lambda e, g=g: e.transpose(g[0], g[1], ident) for g in group], after)


class Slots:

    def __init__(self, bufs):
        self.bufs, self.free, self.i = bufs, [[] for _ in bufs], 0

    def take(self):
        j = self.i % len(self.bufs)
        self.i += 1
        return j, self.bufs[j], self.free[j]

    def give(self, j, *toks):
        self.free[j] = list(toks)


class Arena:
    def __init__(self, tile, n):
        self.t, self.n, self.top = tile, n, 0

    def get(self, w, dt=None, **dims):
        a = self.t[:, self.top:self.top + w]
        self.top += w
        assert self.top <= self.n, (self.top, self.n)
        if dt is not None:
            a = a.bitcast(dt)
        if dims:
            names = " ".join(dims)
            a = a.rearrange(f"p ({names}) -> p {names}", **dims)
        return a


def bc(ap, n):
    return ap.unsqueeze(2).broadcast_to([128, ap.shape[1], n])


def bm(ap, n):
    return ap.unsqueeze(1).broadcast_to([128, n, ap.shape[1]])


def build(nc, T_, dbg=None, force_ovf=False):
    dram = {}

    def internal(name, shape, dt=F):
        return nc.dram_tensor(name, shape, dt, kind="Internal").ap()

    mods1 = internal("mods1", (3072,))
    mods2 = internal("mods2", (2, 6144))
    xd = internal("xd", (128, 4096))
    htd = internal("htd", (128, 4096))
    brd = internal("brd", (2, 128, 2048))
    fd = internal("fd", (S, D))
    idxd = internal("idxd", (128 * NB, 1), I32)
    yd = internal("yd", (128 * NB, D))
    ydv = yd.rearrange("(r b) d -> r b d", b=NB)
    out_d = T_["out"].rearrange("o (t p) d -> p (o t) d", p=128)

    ctx = ExitStack()
    with ctx:
        A_ = ctx.enter_context(nc.sbuf_tensor("arena", [128, NCOL], F))
        PSUM = ctx.enter_context(nc.psum_tensor("psum", [128, 8, 512], F))

        def sem(n):
            return ctx.enter_context(nc.semaphore(n))

        T = Lane(sem("s_pe"), False)
        V = Lane(sem("s_dve"), True)
        A = Lane(sem("s_act"), True)
        G = Lane(sem("s_pool"), True)
        Y = Lane(sem("s_sp"), False)
        main = dict(T=T, V=V, A=A, G=G, Y=Y)
        nsem = [0]

        def dsem():
            nsem[0] += 1
            return Dma(sem(f"d{nsem[0]}"))

        if dbg:
            dbg.lanes = [V, A, T]
        ar = Arena(A_, NCOL)
        banks = Slots([PSUM[:, i, :] for i in range(8)])
        pairs_of = PSUM

        class Stream:
            def __init__(self):
                self.slots = Slots([])
                self.d = []

            def grow(self, bufs, *toks):
                assert self.slots.i % max(1, len(self.slots.bufs)) == 0 or not self.slots.bufs
                for b in bufs:
                    self.slots.bufs.append(b)
                    self.slots.free.append(list(toks))
                    self.d.append(dsem())

            def load(self, src, lane=Y):
                j, buf, free = self.slots.take()
                tok = lane.dma(buf, src, self.d[j], *free)
                return j, buf, tok

            def give(self, j, *toks):
                self.slots.give(j, *toks)

        W = Stream()
        W.grow([ar.get(4096) for _ in range(4)])

        def chunk(i):
            return W.load(T_["w"][i])

        cst = ar.get(NCONST)
        par = ar.get(NPARAM)
        eps = ar.get(4)
        cs = ar.get(24, k=8, v=3)
        lamc = ar.get(1)
        iov = ar.get(8, I32)
        iovn = ar.get(1, I32)
        C = {n: cst[:, a:b] for n, (a, b) in CONSTS.items()}
        P = {n: par[:, a:b] for n, (a, b) in COLS.items()}
        ident, ones = C["ident"], C["ones"]

        d_c = dsem()
        t_par = A.dma(par, T_["params"], d_c)
        t_cst = A.dma(cst, T_["consts"], d_c)
        t_cst = (d_c.sem, d_c.n)

        t_eps = V.zero(eps[:, 0:1], value=EPS)
        V.zero(eps[:, 1:2], value=GN_EPS)
        t_eps = V.zero(eps[:, 2:3], value=0.0)

        mark0 = ar.top
        X = ar.get(4096, t=4, d=1024)
        HT = ar.get(4096, k=8, s=512)
        base = ar.top

        d_x = dsem()
        t_x = A.dma(X, T_["x"].rearrange("o (t p) d -> p (o t) d", p=128), d_x)

        r0 = ar.get(4096)
        sg = r0[:, 0:24]
        t = A.act(sg, par[:, 0:24], ACT.Sigmoid, t_cst)
        t_cs = V.tt(cs.rearrange("p k v -> p v k"), sg.rearrange("p (v k) -> p v k", v=3),
                    par[:, 0:24].rearrange("p (v k) -> p v k", v=3), ALU.mult, t, t_cst)

        bias = r0[:, 64:64 + 512]
        d_b = dsem()
        t_bias = A.dma(bias[0:18, :], T_["bias"], d_b)
        mrow = Slots([r0[:, 640 + 512 * i:640 + 512 * (i + 1)] for i in range(4)])
        d_m = [dsem() for _ in range(4)]
        t_m1, t_m2 = [], []
        for j in range(18):
            ws, wb, wt = chunk(j if j < 6 else 14 + j - 6)
            w = wb.rearrange("p (k n) -> p k n", k=8)
            M = 1 if j < 6 else 2
            bi, b, bf = banks.take()
            sel = C["selp"][0:18, 2 * j:2 * j + M]
            g = [(b[0:M, :], sel, bias[0:18, :], True, False)]
            for k in range(8):
                lhs = cs[:, k, 0:1] if j < 6 else cs[:, k, 1:3]
                g.append((b[0:M, :], lhs, w[:, k, :], False, k == 7))
            t = T.mm(g, t_cs, t_bias, t_cst, wt, *bf)
            W.give(ws, t)
            ri, row, rf = mrow.take()
            t = V.cp(row[0:M, :], b[0:M, :], t, *rf)
            banks.give(bi, t)
            if j < 6:
                dst = mods1[j * 512:(j + 1) * 512].unsqueeze(0)
            else:
                dst = mods2[:, (j - 6) * 512:(j - 5) * 512]
            t = G.dma(dst, row[0:M, :], d_m[ri], t)
            mrow.give(ri, t)
            (t_m1 if j < 6 else t_m2).append(t)

        d_mod = dsem()

        def mod_load(dst, which, i, after=()):
            if which == 1:
                src, toks = mods1[i * 1024:(i + 1) * 1024], t_m1
            else:
                src, toks = mods2[which - 2, i * 1024:(i + 1) * 1024], t_m2
            return G.dma(dst, src.partition_broadcast(128), d_mod, *toks, *after)

        d_row = dsem()

        def row_load(dst, name, after=()):
            return G.dma(dst, T_[name].partition_broadcast(128), d_row, *after)

        small = ar.get(64)

        def modulated(n_tiles, xt, t_in, gs, sh, t_gs, tiles, t_tiles, dest, sq, t_dest=()):
            ss = small[:, 0:n_tiles]
            for i in range(n_tiles):
                t = A.act(sq, xt(i), ACT.Square, *t_in, *t_tiles, accum_out=ss[:, i:i + 1])
            t = A.act(small[:, 8:8 + n_tiles], ss, ACT.Sqrt, t_eps, bias=eps[:, 0:1], scale=1.0 / D)
            t = V.rec(small[:, 16:16 + n_tiles], small[:, 8:8 + n_tiles], t)
            last = [None, None]
            toks = []
            for i in range(n_tiles):
                h = tiles[i % 2]
                V.stt(h, xt(i), small[:, 16 + i:17 + i], gs, ALU.mult, ALU.mult, *t_gs, last[i % 2])
                t = V.tt(h, h, sh, ALU.add)
                last[i % 2] = dest(i, h, t)
                toks.append(last[i % 2])
            return toks

        def transposed(dst, t_dst=()):
            def f(i, h, t):
                for half in range(2):
                    bi, b, bf = banks.take()
                    tt = T.tr([(b[:, q * 128:(q + 1) * 128], h[:, (4 * half + q) * 128:(4 * half + q + 1) * 128])
                               for q in range(4)], ident, t, t_cst, *bf)
                    o = dst[:, 4 * half:4 * half + 4, i * 128:(i + 1) * 128]
                    eng = V if half else A
                    src = b.rearrange("p (q s) -> p q s", q=4)
                    if half:
                        te = V.cp(o, src, tt, *t_dst)
                    else:
                        te = A.act(o, src, ACT.Copy, tt, *t_dst)
                    banks.give(bi, te)
                    f.done.append(te)
                return tt
            f.done = []
            return f

        r0b = ar.get(1024)
        gs1, sh1 = ar.get(1024), ar.get(1024)
        ht = [r0[:, 3072:4096], r0b]
        sqb = ar.get(1024)
        t1 = mod_load(gs1, 1, 1)
        t2 = mod_load(sh1, 1, 0)
        npre = sqb
        d_np = dsem()
        t3 = G.dma(npre, T_["norm_pre"].partition_broadcast(128), d_np)
        t_gs = V.stt(gs1, gs1, 1.0, npre, ALU.add, ALU.mult, t1, t2, t3)
        f1 = transposed(HT)
        modulated(4, lambda i: X[:, i, :], [t_x], gs1, sh1, [t_gs, t2], ht, [t_gs], f1, sqb)
        t_ht = f1.done
        ar.top = base + 4096 + 64 + 1024
        XA = ar.get(2064, m=4, s=516)
        XC = ar.get(2048, m=4, s=512)
        GA = ar.get(2048, m=4, s=512)
        QT = ar.get(2048, m=4, s=512)
        KT = ar.get(2048, m=4, s=512)
        VN = ar.get(2048, t=4, s=512)
        GB = ar.get(2048, t=4, s=512)
        tm = [ar.get(512) for _ in range(6)]
        LNC = ar.get(LNC_N)
        COS, SIN = ar.get(512), ar.get(512)
        d_l = dsem()
        wait_r = [V.last(), A.last(), T.last(), *t_m1, *t_m2]
        t_lnc = G.dma(LNC, T_["lnc"], d_l, *wait_r)
        posb = tm[0].bitcast(I32)
        d_p = dsem()
        t_pos = G.dma(posb, T_["positions"][0, :].partition_broadcast(128), d_p, *wait_r)
        ang, kk_, u_ = tm[1], tm[2], tm[3]
        V.cp(ang, posb, t_pos, *wait_r)
        V.ts(ang, ang, C["invf"], None, ALU.mult, None, t_cst)
        V.ts(kk_, ang, 1.0 / (2 * math.pi), 12582912.0, ALU.mult, ALU.add)
        V.ts(kk_, kk_, -12582912.0, None, ALU.add, None)
        c1 = 6.28125
        c2 = float(np.float32(int((2 * math.pi - c1) * 2 ** 17) / 2 ** 17))
        c3 = float(np.float32(2 * math.pi - c1 - c2))
        for c in (c1, c2, c3):
            V.stt(ang, kk_, -c, ang, ALU.mult, ALU.add)
        V.ts(ang, ang, math.pi, -math.pi, ALU.min, ALU.max)
        t = V.ts(u_, ang, -1.0, None, ALU.mult, None)
        t = V.tt(u_, u_, ang, ALU.max)
        t = V.ts(u_, u_, -1.0, math.pi / 2, ALU.mult, ALU.add)
        t_cos = A.act(COS, u_, ACT.Sin, t)
        t = A.act(SIN, ang, ACT.Sin, t)
        t_rope = V.ts(SIN, SIN, C["sgn"], None, ALU.mult, None, t, t_cos)

        def proj_t(ci, n_m, rhs, t_rhs, width, sink, used=512):
            ws, wb, wt = chunk(ci)
            w = wb.rearrange("p (k n) -> p k n", k=8)
            toks = []
            for m in range(n_m):
                bi, b, bf = banks.take()
                t = T.mm([(b[:, 0:width], w[:, k, m * 128:(m + 1) * 128], rhs(k), k == 0, k == 7) for k in range(8)],
                         wt, *t_rhs, *bf)
                if m == n_m - 1:
                    W.give(ws, t)
                banks.give(bi, *sink(m, b[:, 0:width], t))

        def proj_n(ci, tiles, sink, t_in):
            ws, wb, wt = chunk(ci)
            w = wb.rearrange("p (k n) -> p k n", k=8)
            for i, lhs in enumerate(tiles):
                bi, b, bf = banks.take()
                t = T.mm([(b, lhs(k), w[:, k, :], k == 0, k == 7) for k in range(8)], wt, *t_in, *bf)
                if i == len(tiles) - 1:
                    W.give(ws, t)
                banks.give(bi, *sink(i, b, t))

        hr = lambda k: HT[:, k, :]
        t_pad = V.zero(XA[:, :, 0:4])
        toks = {}

        def sink_xa(m, b, t):
            toks["xa", m] = A.act(XA[:, m, 4:516], b, ACT.Copy, t, *wait_r)
            return [toks["xa", m]]

        proj_t(6, 4, hr, t_ht, 512, sink_xa)

        def sink_ga(m, b, t):
            t = A.act(GA[:, m, :], b, ACT.Sigmoid, t, *wait_r)
            toks["ga", m] = V.tt(GA[:, m, :], GA[:, m, :], b, ALU.mult, t)
            return [toks["ga", m]]

        proj_t(7, 4, hr, t_ht, 512, sink_ga)

        def rope(m, b, t, cosb, sinb, perm, dst, raw, tmp, t_tab):
            n = dst.shape[1]
            t = V.cp(raw[:, 0:n], b, t, T.last())
            bi, b2, bf = banks.take()
            tp = T.mm([(b2[:, 0:n], perm, raw[:, 0:n], True, True)], t, t_cst, *bf)
            V.tt(dst, raw[:, 0:n], cosb, ALU.mult, *t_tab)
            t2 = V.tt(tmp[:, 0:n], b2[:, 0:n], sinb, ALU.mult, tp)
            banks.give(bi, t2)
            return t, V.tt(dst, dst, tmp[:, 0:n], ALU.add)

        def sink_rope(name, dst):
            def f(m, b, t):
                t1, t2 = rope(m, b, t, COS, SIN, C["perm1"], dst[:, m, :], tm[m % 2], tm[2], [t_rope])
                toks[name, m] = t2
                return [t1]
            return f

        proj_t(8, 4, hr, t_ht, 512, sink_rope("q", QT))
        proj_t(9, 4, hr, t_ht, 512, sink_rope("k", KT))
        tl = [lambda k, i=i: HT[:, k, i * 128:(i + 1) * 128] for i in range(4)]

        def sink_v(i, b, t):
            toks["v", i] = A.act(VN[:, i, :], b, ACT.Copy, t, *wait_r)
            return [toks["v", i]]

        proj_n(10, tl, sink_v, t_ht)

        def sink_gb(i, b, t):
            t = A.act(GB[:, i, :], b, ACT.Sigmoid, t, *wait_r)
            toks["gb", i] = V.tt(GB[:, i, :], GB[:, i, :], b, ALU.mult, t)
            return [toks["gb", i]]

        proj_n(11, tl, sink_gb, t_ht)

        lw = [small[:, 24 + 4 * i:28 + 4 * i] for i in range(8)]
        lam = P["lam"]
        V.ts(lw[0], lam, -1.0, None, ALU.mult, None)
        t = V.tt(lw[1], lam, lw[0], ALU.min)
        t = A.act(lw[2], lw[1], ACT.Exp, t)
        V.ts(lw[3], lw[2], 2.0, None, ALU.add, None, t)
        V.rec(lw[3], lw[3])
        V.tt(lw[2], lw[2], lw[3], ALU.mult)
        V.tt(lw[4], lw[2], lw[2], ALU.mult)
        V.zero(lw[5], value=1.0 / 19)
        for n in range(8, -1, -1):
            V.tt(lw[5], lw[5], lw[4], ALU.mult)
            V.ts(lw[5], lw[5], 1.0 / (2 * n + 1), None, ALU.add, None)
        V.stt(lw[5], lw[5], 2.0, lw[2], ALU.mult, ALU.mult)
        V.stt(lw[5], lw[0], 0.0, lw[5], ALU.max, ALU.add)
        t_sp = V.ts(lw[6], lw[5], 8.0, None, ALU.mult, None)
        t_spn = V.ts(lw[7], lw[5], -8.0, None, ALU.mult, None)
        wbd = r0[:, 0:1024]
        d_w = dsem()
        t_wbd = G.dma(wbd, T_["w_rg"], d_w, *wait_r)
        ssb = {}
        cw = P["conv_w"]
        for m in range(4):
            xc = XC[:, m, :]
            V.ts(xc, XA[:, m, 1:513], cw[:, m:m + 1], P["conv_b"][:, m:m + 1], ALU.mult, ALU.add, toks["xa", m])
            for k in range(1, 4):
                t_xc = V.stt(xc, XA[:, m, 1 + k:513 + k], cw[:, 4 * k + m:4 * k + m + 1], xc, ALU.mult, ALU.add)
            gates = []
            for j, (bn, tmp) in enumerate((("b_a", tm[0]), ("b_x", tm[1]))):
                bi, b, bf = banks.take()
                t = T.mm([(b, wbd[:, (4 * j + m) * 128:(4 * j + m + 1) * 128], xc, True, True)], t_xc, t_wbd, *bf)
                t = A.act(tmp, b, ACT.Sigmoid, t, V.last(), bias=P[bn][:, m:m + 1])
                banks.give(bi, t)
            ta = A.act(tm[2], tm[0], ACT.Exp, t_spn, scale=lw[7][:, m:m + 1])
            t_th = A.act(tm[3], tm[0], ACT.Tanh, t_sp, scale=lw[6][:, m:m + 1])
            V.ts(tm[4], tm[3], 1.0, None, ALU.add, None, t_th)
            V.rec(tm[4], tm[4])
            t = V.stt(tm[3], tm[3], 2.0, tm[4], ALU.mult, ALU.mult)
            t = A.act(tm[3], tm[3], ACT.Sqrt, t)
            V.tt(tm[1], tm[1], xc, ALU.mult)
            V.tt(tm[1], tm[1], tm[3], ALU.mult, t)
            V.scan(tm[4], tm[2], tm[1], ta)
            t = V.tt(xc, tm[4], GA[:, m, :], ALU.mult, T.last())
            toks["ya", m] = t
        bi, b, bf = banks.take()
        for m in range(4):
            t = A.act(tm[m % 2], XC[:, m, :], ACT.Square, toks["ya", 3], T.last())
            t = T.mm([(b, ones, tm[m % 2], m == 0, m == 3)], t, *bf)
        t = A.act(tm[2], b, ACT.Sqrt, t, bias=eps[:, 0:1], scale=1.0 / 512)
        banks.give(bi, t)
        t = V.rec(tm[2], tm[2], t)
        t_ya = None
        for m in range(4):
            t_ya = V.stt(XC[:, m, :], XC[:, m, :], P["norm_rec"][:, m:m + 1], tm[2], ALU.mult, ALU.mult)

        sl = [r0[:, 512 * i:512 * (i + 1)] for i in range(8)]
        Sb, Pb, PTb, YB = sl[0:2], [sl[2], sl[3], tm[3]], sl[4:6], sl[6:8]
        free_r0 = [T.last(), A.last()]
        YBT = XA.rearrange("p m s -> p (m s)")[:, 0:2048].rearrange("p (m s) -> p m s", m=4)
        nbb = ar.get(512)
        d_na = dsem()
        t_na = G.dma(nbb, T_["norm_att"].partition_broadcast(128), d_na)
        st = ar.get(64)
        ab_free = [T.last(), V.last(), A.last()]
        abanks, obanks = Slots(banks.bufs[0:6]), Slots(banks.bufs[6:8])
        for j in range(6):
            abanks.give(j, *ab_free)
        for j in range(2):
            obanks.give(j, *ab_free)
        it = [(i, h) for i in range(4) for h in range(8)]
        tS, tP, tPT = {}, {}, {}
        obank = {}
        q_all = [toks["q", m] for m in range(4)] + [toks["k", m] for m in range(4)] + [toks["v", i] for i in range(4)]

        def scores(x):
            i, h = it[x]
            n = 128 * (i + 1)
            hb, m = 64 * (h % 2), h // 2
            bi, b, bf = abanks.take()
            t = T.mm([(b[:, 0:n], QT[hb:hb + 64, m, i * 128:(i + 1) * 128], KT[hb:hb + 64, m, 0:n], True, True)],
                     *q_all, *bf)
            s, p = Sb[x % 2], Pb[x % 3]
            o = LNC_OFF[i]
            t = V.stt(s[:, 0:n], b[:, 0:n], 0.125, LNC[:, o:o + n], ALU.mult, ALU.add, t, t_lnc, tP.get(x - 2), *free_r0)
            abanks.give(bi, t)
            t = V.red(st[:, x % 2:x % 2 + 1], s[:, 0:n], ALU.max, negate=True)
            tP[x] = A.act(p[:, 0:n], s[:, 0:n], ACT.Exp, t, tPT.get(x - 3), bias=st[:, x % 2:x % 2 + 1],
                          accum_out=st[:, 8 + 8 * (i % 2) + h:9 + 8 * (i % 2) + h])

        def turn(x):
            i, h = it[x]
            n = 128 * (i + 1)
            bi, b, bf = abanks.take()
            t = T.tr([(b[:, j * 128:(j + 1) * 128], Pb[x % 3][:, j * 128:(j + 1) * 128]) for j in range(i + 1)],
                     ident, tP[x], *bf)
            tPT[x] = t
            tS[x] = A.act(PTb[x % 2][:, 0:n], b[:, 0:n], ACT.Copy, t, obank.get(("pv", x - 2)))
            abanks.give(bi, tS[x])

        def pv(x):
            i, h = it[x]
            if h == 0:
                obank[i] = obanks.take()
            bi, b, bf = obank[i]
            t = T.mm([(b[:, h * 64:(h + 1) * 64], PTb[x % 2][:, j * 128:(j + 1) * 128], VN[:, j, h * 64:(h + 1) * 64],
                       j == 0, j == i) for j in range(i + 1)], tS[x], *bf)
            obank["pv", x] = t
            if h == 7:
                ri = st[:, 24 + 8 * (i % 2):32 + 8 * (i % 2)]
                V.rec(ri, st[:, 8 + 8 * (i % 2):16 + 8 * (i % 2)], tP[x])
                y = YB[i % 2]
                t = V.tt(y.rearrange("p (h d) -> p h d", h=8), b.rearrange("p (h d) -> p h d", h=8), bc(ri, 64),
                         ALU.mult, t, obank.get(("yt", i - 2)))
                obanks.give(bi, t)
                t = V.tt(y, y, GB[:, i, :], ALU.mult)
                t = A.act(tm[0], y, ACT.Square, t, V.last(), accum_out=st[:, 40 + i:41 + i])
                t = A.act(st[:, 44 + i:45 + i], st[:, 40 + i:41 + i], ACT.Sqrt, bias=eps[:, 0:1], scale=1.0 / 512)
                t = V.rec(st[:, 48 + i:49 + i], st[:, 44 + i:45 + i], t)
                t = V.stt(y, y, st[:, 48 + i:49 + i], nbb, ALU.mult, ALU.mult, t_na)
                b2i, b2, b2f = abanks.take()
                t = T.tr([(b2[:, q * 128:(q + 1) * 128], y[:, q * 128:(q + 1) * 128]) for q in range(4)], ident, t, *b2f)
                obank["yt", i] = t
                t = V.cp(YBT[:, :, i * 128:(i + 1) * 128], b2.rearrange("p (q s) -> p q s", q=4), t)
                obank["y", i] = t
                abanks.give(b2i, t)

        for x in range(len(it) + 3):
            if x < len(it):
                scores(x)
            if 0 <= x - 2 < len(it):
                turn(x - 2)
            if 0 <= x - 3 < len(it):
                pv(x - 3)

        for j in range(8):
            banks.give(j, T.last(), V.last(), A.last())

        gp1 = tm[2]
        wo = [chunk(12), chunk(13)]
        G1 = r0[:, 0:1024]
        w_r0 = [T.last(), V.last(), A.last()]
        d_g1 = dsem()
        t1 = G.dma(G1, mods1[2048:3072].partition_broadcast(128), d_g1, *t_m1, *w_r0)
        d_np2 = dsem()
        np_ = r0[:, 1024:2048]
        t2 = G.dma(np_, T_["norm_post"].partition_broadcast(128), d_np2, *w_r0)
        t_gp = V.tt(G1, G1, np_, ALU.mult, t1, t2)
        msb = [r0[:, 2048:3072], r0[:, 3072:4096]]
        y_all = [obank["y", i] for i in range(4)] + [t_ya]
        t_x1 = []
        for i in range(4):
            bb = []
            for hf in range(2):
                ws, wb, wt = wo[hf]
                w = wb.rearrange("p (k n) -> p k n", k=8)
                bi, b, bf = banks.take()
                g = []
                for k in range(8):
                    lhs = (XC if k < 4 else YBT)[:, k % 4, i * 128:(i + 1) * 128]
                    g.append((b, lhs, w[:, k, :], k == 0, k == 7))
                t = T.mm(g, wt, *y_all, *bf)
                if i == 3:
                    W.give(ws, t)
                bb.append((bi, b, t))
            mx = msb[i % 2]
            for hf in range(2):
                bi, b, t = bb[hf]
                t = V.cp(mx[:, hf * 512:(hf + 1) * 512], b, t, *w_r0)
                banks.give(bi, t)
            t = A.act(np_, mx, ACT.Square, t, t_gp, accum_out=st[:, 40 + i:41 + i])
            t = A.act(st[:, 44 + i:45 + i], st[:, 40 + i:41 + i], ACT.Sqrt, bias=eps[:, 0:1], scale=1.0 / D)
            V.rec(st[:, 48 + i:49 + i], st[:, 44 + i:45 + i], t)
            V.stt(mx, mx, st[:, 48 + i:49 + i], G1, ALU.mult, ALU.mult)
            t_x1.append(V.tt(X[:, i, :], X[:, i, :], mx, ALU.add))

        def fence():
            return [T.last(), V.last(), A.last(), G.last()]

        ar.top = base
        fb1 = fence()
        if dbg:
            dbg("x1", X, V, G, dsem)
        HCT = ar.get(2048, k=8, s=256)
        small = ar.get(64)
        mark2 = ar.top
        gs, sh, gsc, shc = [ar.get(1024) for _ in range(4)]
        ht = [ar.get(1024), ar.get(1024)]
        sqb, n1 = ar.get(1024), ar.get(1024)
        CX = ar.get(2048, t=2, d=1024)
        d_n1 = dsem()
        t_l = [mod_load(gs, 2, 1, fb1), mod_load(sh, 2, 0, fb1), mod_load(gsc, 3, 1, fb1), mod_load(shc, 3, 0, fb1),
               G.dma(n1, T_["norm1_g_2"].partition_broadcast(128), d_n1, *fb1),
               G.dma(CX, T_["ctx_2"].rearrange("o (t p) d -> p (o t) d", p=128), d_n1, *fb1)]
        V.stt(gs, gs, 1.0, n1, ALU.add, ALU.mult, *t_l, *fb1)
        t_gs = V.stt(gsc, gsc, 1.0, n1, ALU.add, ALU.mult)
        f2 = transposed(HCT, fb1)
        modulated(2, lambda i: CX[:, i, :], t_l, gsc, shc, [t_gs], ht, fb1, f2, sqb)
        f3 = transposed(HT, fb1)
        modulated(4, lambda i: X[:, i, :], t_x1, gs, sh, [t_gs], ht, fb1, f3, sqb)
        t_h2 = f2.done + f3.done
        d_sp = dsem()
        t_xd = G.dma(xd, X.rearrange("p t d -> p (t d)"), d_sp, *t_x1)
        t_hd = G.dma(htd, HT.rearrange("p k s -> p (k s)"), d_sp, *t_h2)
        t_xd = t_hd
        ar.top = mark2
        f = fence()

        TB = ar.get(NROPE)
        d_tb = dsem()
        t_tb = G.dma(TB, T_["ropes"], d_tb, *f)
        RP = {n: TB[:, a:b] for n, (a, b) in ROPES.items()}
        PW = ar.get(512, g=4, d=128)
        t_tb = G.dma(PW, T_["pool_w_2"][0].rearrange("g c d -> c g d"), d_tb, *f)
        lqb = ar.get(256)
        t_tb = G.dma(lqb, T_["lambda_qk_2"][0].rearrange("a b -> (a b)").partition_broadcast(128), d_tb, *f)
        SUB = ar.get(512)
        t_tb = G.dma(SUB, T_["subln"].partition_broadcast(128), d_tb, *f)
        V.tt(lqb[:, 0:64], lqb[:, 0:64], lqb[:, 64:128], ALU.mult, t_tb)
        V.tt(lqb[:, 128:192], lqb[:, 128:192], lqb[:, 192:256], ALU.mult)
        V.red(small[:, 40:41], lqb[:, 0:64], ALU.add)
        t = V.red(small[:, 41:42], lqb[:, 128:192], ALU.add)
        t = A.act(small[:, 42:44], small[:, 40:42], ACT.Exp, t)
        V.tt(lamc, small[:, 42:43], small[:, 43:44], ALU.subtract, t)
        V.ts(lamc, lamc, 0.8 - 0.6 * math.exp(0.0), None, ALU.add, None)

        mark3 = ar.top
        PP = ar.get(4 * 528, m=4, s=528)
        pt = [ar.get(528) for _ in range(2)]
        B0 = ar.get(2048, m=4, s=512)
        t_z = V.zero(PP, *f)
        hl = lambda k: HT[:, k, :]
        hc = lambda k: HCT[:, k, :]
        t_b0 = []

        def sink_pool(m, b, t):
            w = 2 << m
            u = PP[:, m, :]
            tA = A.act(u[:, 8:520], b, ACT.Copy, t, t_z)
            src, step = u, 1
            n = 528
            j = 0
            while step < w:
                dst = pt[j % 2]
                n2 = n - step
                V.tt(dst[:, 0:n2], src[:, 0:n2], src[:, step:step + n2], ALU.add, tA)
                src, n, step, j = dst, n2, step * 2, j + 1
            o = 8 - w // 2
            dst = pt[j % 2]
            V.tt(dst[:, 0:512], src[:, o:o + 512], RP["cnt"][:, m * 512:(m + 1) * 512], ALU.mult, t_tb)
            t = V.tt(dst[:, 0:512], dst[:, 0:512], u[:, 8:520], ALU.subtract)
            bi, b2, bf = banks.take()
            t = T.mm([(b2, PW[:, m, :], dst[:, 0:512], True, True)], t, t_tb, *bf)
            t = V.ts(B0[:, m, :], b2, P["pscale"][:, m:m + 1], None, ALU.mult, None, t)
            banks.give(bi, t)
            t_b0.append(t)
            return [tA]

        proj_t(26, 4, hl, t_h2, 512, sink_pool)
        d_br = dsem()
        t_brd = G.dma(brd[0], B0.rearrange("p m s -> p (m s)"), d_br, *t_b0)

        if dbg:
            dbg("b0", B0, V, G, dsem)

        ar.top = mark3 + 4 * 528 + 2 * 528 + 2048
        QT = ar.get(2048, m=4, s=512)
        KT = ar.get(4 * 768, m=4, s=768)
        VN = ar.get(6 * 512, t=6, s=512)
        tm = [ar.get(512) for _ in range(4)]
        toks = {}

        def qk_norm(b, t, n, g, raw, sq):
            t1 = A.act(sq[:, 0:n], b, ACT.Square, t, *f, V.last(), T.last())
            bi, b2, bf = banks.take()
            t2 = T.mm([(b2[:, 0:n], C["blk64"], sq[:, 0:n], True, True)], t1, *bf)
            t3 = A.act(sq[:, 0:n], b2[:, 0:n], ACT.Sqrt, t2, bias=eps[:, 0:1], scale=1.0 / 64)
            banks.give(bi, t3)
            V.rec(sq[:, 0:n], sq[:, 0:n], t3)
            return V.stt(raw, b, g, sq[:, 0:n], ALU.mult, ALU.mult, t, T.last(), *f)

        def sink_qk(name, dst, col, off):
            def fn(m, b, t):
                n1_, n2_ = tm[2 * (m % 2)], tm[2 * (m % 2) + 1]
                t0 = qk_norm(b, t, 512, col, n1_, n2_)
                bi, b2, bf = banks.take()
                tp = T.mm([(b2, C["perm2"], n1_, True, True)], t0, *bf)
                o = dst[:, m, off:off + 512]
                V.tt(o, n1_, RP["cos2"], ALU.mult, t_tb)
                t2 = V.tt(n2_, b2, RP["sin2"], ALU.mult, tp)
                banks.give(bi, t2)
                toks[name, m] = V.tt(o, o, n2_, ALU.add)
                return [t0]
            return fn

        proj_t(27, 4, hl, t_h2, 512, sink_qk("q", QT, P["qn"], 0))
        ws, wb, wt = chunk(28)
        w = wb.rearrange("p (k n) -> p k n", k=8)
        sk = sink_qk("k", KT, P["kn"], 256)
        for m in range(4):
            bi, b, bf = banks.take()
            t = T.mm([(b[:, 0:256], w[:, k, m * 128:(m + 1) * 128], hc(k), k == 0, k == 7) for k in range(8)], wt, *t_h2, *bf)
            t = qk_norm(b[:, 0:256], t, 256, P["kn"], KT[:, m, 0:256], tm[2 * (m % 2)])
            toks["kc", m] = t
            banks.give(bi, t)
            bi, b, bf = banks.take()
            t = T.mm([(b, w[:, k, m * 128:(m + 1) * 128], hl(k), k == 0, k == 7) for k in range(8)], *bf)
            if m == 3:
                W.give(ws, t)
            banks.give(bi, *sk(m, b, t))
        tl6 = [lambda k, i=i: HCT[:, k, i * 128:(i + 1) * 128] for i in range(2)] + \
              [lambda k, i=i: HT[:, k, i * 128:(i + 1) * 128] for i in range(4)]

        def sink_v2(i, b, t):
            toks["v", i] = A.act(VN[:, i, :], b, ACT.Copy, t, *f)
            return [toks["v", i]]

        proj_n(29, tl6, sink_v2, t_h2)
        ar2 = ar.top
        ar.top = mark3
        f4 = fence() + [t_brd] + (dbg.toks if dbg else [])
        Pm = [[ar.get(768) for _ in range(2)] for _ in range(2)]
        AT = [ar.get(768) for _ in range(2)]
        ATN = [tm[0], tm[1]]
        assert ar.top <= mark3 + 4 * 528 + 2 * 528 + 2048
        ar.top = ar2
        B1 = ar.get(2048, m=4, s=512)
        st = ar.get(64)
        it = [(i, h) for i in range(4) for h in range(4)]
        spair = Slots([PSUM[:, 0:2, :].rearrange("p a b -> p (a b)"), PSUM[:, 2:4, :].rearrange("p a b -> p (a b)")])
        tpair = Slots([PSUM[:, 4:6, :].rearrange("p a b -> p (a b)")])
        for s_ in (spair, tpair):
            for j in range(len(s_.bufs)):
                s_.give(j, *f4)
        fp = f4
        qkv = list(toks.values())
        tA, tTR, tAT, tPV = {}, {}, {}, {}

        def d_scores(x):
            i, h = it[x]
            o = 4 * (x % 2)
            for mp in range(2):
                bi, b, bf = spair.take()
                lhs = QT[64 * mp:64 * mp + 64, h, i * 128:(i + 1) * 128]
                t = T.mm([(b[:, 0:512], lhs, KT[64 * mp:64 * mp + 64, h, 0:512], True, True),
                          (b[:, 512:768], lhs, KT[64 * mp:64 * mp + 64, h, 512:768], True, True)], *qkv, *bf)
                V.red(st[:, o + mp:o + mp + 1], b[:, 0:768], ALU.max, t, A.last())
                t = V.ts(st[:, o + mp:o + mp + 1], st[:, o + mp:o + mp + 1], -0.125, None, ALU.mult, None)
                t = A.act(Pm[x % 2][mp], b[:, 0:768], ACT.Exp, t, *fp, tTR.get(x - 2), bias=st[:, o + mp:o + mp + 1],
                          scale=0.125, accum_out=st[:, 8 + o + mp:9 + o + mp])
                spair.give(bi, t)
            rc = st[:, 16 + o:18 + o]
            V.rec(rc, st[:, 8 + o:10 + o], t)
            V.tt(rc[:, 1:2], rc[:, 1:2], lamc, ALU.mult)
            V.ts(Pm[x % 2][1], Pm[x % 2][1], rc[:, 1:2], None, ALU.mult, None)
            tA[x] = V.stt(Pm[x % 2][0], Pm[x % 2][0], rc[:, 0:1], Pm[x % 2][1], ALU.mult, ALU.subtract)

        def d_turn(x):
            bi, b, bf = tpair.take()
            t = T.tr([(b[:, j * 128:(j + 1) * 128], Pm[x % 2][0][:, j * 128:(j + 1) * 128]) for j in range(6)], ident, tA[x], *bf)
            tTR[x] = t
            tAT[x] = A.act(AT[x % 2], b[:, 0:768], ACT.Copy, t, *fp, tPV.get(x - 2))
            tpair.give(bi, tAT[x])

        ob = Slots([PSUM[:, 6, :]])
        tb = Slots([PSUM[:, 7, :]])
        ob.give(0, *f4)
        tb.give(0, *f4)
        t_b1 = []
        hold = {}

        def d_pv(x):
            i, h = it[x]
            if h == 0:
                hold["o"] = ob.take()
            bi, b, bf = hold["o"]
            tPV[x] = t = T.mm([(b[:, h * 128:(h + 1) * 128], AT[x % 2][:, j * 128:(j + 1) * 128],
                                VN[:, j, h * 128:(h + 1) * 128], j == 0, j == 5) for j in range(6)], tAT[x], *bf)
            if h == 3:
                y, sq = ATN[i % 2], tm[2]
                t = V.cp(y, b, t, hold.get(i - 2))
                ob.give(0, t)
                t = V.tt(sq, y, y, ALU.mult)
                t = V.red(st[:, 32:36], sq.rearrange("p (h d) -> p h d", h=4), ALU.add)
                t = A.act(st[:, 36:40], st[:, 32:36], ACT.Sqrt, t, bias=eps[:, 0:1], scale=1.0 / 128)
                V.rec(st[:, 40:44], st[:, 36:40], t)
                V.tt(y.rearrange("p (h d) -> p h d", h=4), y.rearrange("p (h d) -> p h d", h=4), bc(st[:, 40:44], 128), ALU.mult)
                t = V.stt(y, y, 1.0 - (0.8 - 0.6 * math.exp(0.0)), SUB, ALU.mult, ALU.mult)
                b2i, b2, b2f = tb.take()
                t = T.tr([(b2[:, q * 128:(q + 1) * 128], y[:, q * 128:(q + 1) * 128]) for q in range(4)], ident, t, *b2f)
                hold[i] = t
                t = V.cp(B1[:, :, i * 128:(i + 1) * 128], b2.rearrange("p (q s) -> p q s", q=4), t)
                tb.give(0, t)
                t_b1.append(t)

        for x in range(len(it) + 2):
            if x < len(it):
                d_scores(x)
            if 0 <= x - 1 < len(it):
                d_turn(x - 1)
            if 0 <= x - 2 < len(it):
                d_pv(x - 2)
        t_brd = G.dma(brd[1], B1.rearrange("p m s -> p (m s)"), d_br, *t_b1)
        if dbg:
            dbg("b1", B1, V, G, dsem)

        f = fence() + [t_brd, t_xd]
        if dbg:
            f = f + dbg.toks
        for j in range(8):
            banks.give(j, *f)
        ar.top = mark2
        R = ar.get(2048, m=4, s=512)
        K = ar.get(3072, m=4, s=768)
        VR = ar.get(3072, t=6, s=512)
        WL, AL = ar.get(768), ar.get(768)
        SG = ar.get(512)
        KK = ar.get(3072, m=4, s=768)
        YS = ar.get(2048, t=4, s=512)
        W2, A2, G2 = ar.get(512), ar.get(512), ar.get(512)
        MK = ar.get(NMASK)
        IRK = ar.get(32, m=4, h=8)
        COEF = ar.get(32, t=4, h=8)
        MM = {n: MK[:, a:b] for n, (a, b) in MASKS.items()}
        d_rw = dsem()
        for dst, n in ((W2, "decay_w2"), (A2, "aaa_a2"), (G2, "gate_w2"), (MK, "masks")):
            t_rw = G.dma(dst, T_[n], d_rw, *f)
        V.tt(IRK, C["ind"].rearrange("p (m h) -> p m h", m=4), bc(P["r_k"], 8), ALU.mult, *f)
        mark4 = ar.top
        PR = [ar.get(772) for _ in range(2)]
        vt = [ar.get(768) for _ in range(2)]
        m01 = ar.get(16)
        t_pz = None
        for z in PR:
            t_pz = V.zero(z, *f)
        V.tt(m01[:, 0:15], P["mu0"], P["mu1"], ALU.add)
        V.ts(m01[:, 0:15], m01[:, 0:15], -1.0, 1.0, ALU.mult, ALU.add)
        shifted = {}
        rd = [None, None]
        ti = 0
        for ci, n_m, f0 in ((30, 4, 0), (31, 4, 4), (32, 4, 8), (33, 3, 12)):
            ws, wb, wt = chunk(ci)
            w = wb.rearrange("p (k n) -> p k n", k=8)
            for m in range(n_m):
                fi = f0 + m
                pr = PR[ti % 2]
                has_c = fi not in (0, 1, 2, 3, 14)
                tc = None
                if has_c:
                    bi, b, bf = banks.take()
                    t = T.mm([(b[:, 0:256], w[:, k, m * 128:(m + 1) * 128], hc(k), k == 0, k == 7) for k in range(8)], wt, *bf)
                    tc = A.act(pr[:, 1:257], b[:, 0:256], ACT.Copy, t, t_pz, rd[ti % 2])
                    banks.give(bi, tc)
                bi, b, bf = banks.take()
                t = T.mm([(b, w[:, k, m * 128:(m + 1) * 128], hl(k), k == 0, k == 7) for k in range(8)], wt, *bf)
                if m == n_m - 1:
                    W.give(ws, t)
                tl_ = A.act(pr[:, 258:770], b, ACT.Copy, t, t_pz, rd[ti % 2])
                banks.give(bi, tl_)
                if fi < 4:
                    dl, dc = R[:, fi, :], None
                elif fi < 8:
                    dl, dc = K[:, fi - 4, 256:768], K[:, fi - 4, 0:256]
                elif fi < 12:
                    v_ = vt[ti % 2]
                    dl, dc = v_[:, 256:768], v_[:, 0:256]
                elif fi < 14:
                    q_ = (WL, AL)[fi - 12]
                    dl, dc = q_[:, 256:768], q_[:, 0:256]
                else:
                    dl, dc = SG, None
                wv = shifted.get("vt%d" % (ti % 2)) if 8 <= fi < 12 else None
                for dst, o, n in ((dl, 258, 512), (dc, 1, 256)):
                    if dst is None:
                        continue
                    V.ts(dst, pr[:, o:o + n], m01[:, fi:fi + 1], None, ALU.mult, None, tl_, tc, wv)
                    V.stt(dst, pr[:, o - 1:o - 1 + n], P["mu0"][:, fi:fi + 1], dst, ALU.mult, ALU.add)
                    t = V.stt(dst, pr[:, o + 1:o + 1 + n], P["mu1"][:, fi:fi + 1], dst, ALU.mult, ALU.add)
                rd[ti % 2] = t
                if 8 <= fi < 12:
                    for hf in range(2):
                        nb_ = 4 if hf == 0 else 2
                        bi, b, bf = banks.take()
                        t2 = T.tr([(b[:, q * 128:(q + 1) * 128], v_[:, (4 * hf + q) * 128:(4 * hf + q + 1) * 128])
                                   for q in range(nb_)], ident, t, *bf)
                        t3 = A.act(VR[:, 4 * hf:4 * hf + nb_, (fi - 8) * 128:(fi - 7) * 128],
                                   b[:, 0:nb_ * 128].rearrange("p (q s) -> p q s", q=nb_), ACT.Copy, t2, *f)
                        banks.give(bi, t3)
                        shifted["vt%d" % (ti % 2)] = t2
                        shifted["vr", fi, hf] = t3
                ti += 1
        t = V.last()
        t_wl = A.act(WL, WL, ACT.Tanh, t)
        t_sg = A.act(SG, SG, ACT.Sigmoid, t)
        t_vr = [v for k_, v in shifted.items() if isinstance(k_, tuple)]
        ar.top = mark4
        f5 = fence()
        tmp = [ar.get(512, m=4, s=128) for _ in range(5)]
        fl = [x_.rearrange("p m s -> p (m s)") for x_ in tmp]
        for c in range(6):
            kc = KK[:, :, c * 128:(c + 1) * 128]
            V.tt(kc, K[:, :, c * 128:(c + 1) * 128], bc(P["k_k"], 128), ALU.mult, *f5)
            q_ = tmp[c % 2]
            t = V.tt(q_, kc, kc, ALU.mult, T.last())
            bi, b, bf = banks.take()
            t = T.mm([(b, C["blk64"], fl[c % 2], True, True)], t, *bf)
            t = A.act(fl[2 + c % 2], b, ACT.Sqrt, t, V.last(), bias=eps[:, 2:3])
            banks.give(bi, t)
            V.ts(fl[2 + c % 2], fl[2 + c % 2], 1e-12, None, ALU.max, None, t)
            V.rec(fl[2 + c % 2], fl[2 + c % 2])
            V.tt(kc, kc, tmp[2 + c % 2], ALU.mult)

        low = Arena(A_, base + 2048)
        low.top = mark0
        AR = low.get(1024, m=4, j=2, s=128)
        KB = low.get(1024, j=2, m=4, s=128)
        KNB = low.get(1024, j=2, n=512)
        GBm = low.get(2048, h=8, n=256)
        GKm = low.get(2048, h=8, n=256)
        NM = low.get(1024, h=8, n=128)
        TI = low.get(1024, h=8, n=128)
        TT = low.get(1024, h=8, n=128)
        XB = ar.get(1024, h=8, n=128)
        MS = [ar.get(512, m=4, v=128) for _ in range(2)]
        MP = ar.get(512, m=4, v=128)
        DD = ar.get(4)
        X0, SA = [XB.rearrange("p h n -> p (h n)")[:, 512 * q:512 * (q + 1)] for q in range(2)]
        f6 = fence()
        for d in range(2):
            V.zero(MS[d], *f6)
        order = [[0, 1, 2, 3, 4, 5], [1, 0, 5, 4, 3, 2]]
        hp = lambda h: (64 * (h % 2), h // 2)
        LMI = {}
        rel = {"G": None}
        t_seq = []
        for step in range(6):
            for d in range(2):
                c = order[d][step]
                lat = c >= 2
                cs_ = slice(c * 128, (c + 1) * 128)
                ls = slice((c - 2) * 128, (c - 1) * 128)
                first = step == 0
                pe_prev = T.last()
                sig, ag, L, ex, e2 = tmp
                for dst, wgt, lo, b0, tin in ((sig, W2, WL, "w0", t_wl), (ag, A2, AL, "a0", None)):
                    bi, b, bf = banks.take()
                    t = T.mm([(b[:, m * 128:(m + 1) * 128], wgt[64 * d:64 * d + 64, m * 128:(m + 1) * 128],
                               lo[64 * d:64 * d + 64, cs_], True, True) for m in range(4)], tin, t_rw, *f5, *bf)
                    for m in range(4):
                        t = A.act(dst[:, m, :], b[:, m * 128:(m + 1) * 128], ACT.Sigmoid, t, V.last(), *f5,
                                  bias=P[b0][:, 4 * d + m:4 * d + m + 1])
                    banks.give(bi, t)
                t_ag = t
                for m in range(4):
                    if d == 0:
                        V.scan(L[:, m, :], ones, sig[:, m, :], t_ag, t_rw)
                    else:
                        V.scan(L[:, m, ::-1], ones, sig[:, m, ::-1], t_ag, t_rw)
                tot = L[:, :, 127:128] if d == 0 else L[:, :, 0:1]
                t = V.cp(DD.unsqueeze(2), tot)
                t_dd = V.cp(ex[:, :, 0:1], tot)
                t_D = A.act(DD, DD, ACT.Exp, t_dd, scale=-0.5 * KAPPA)
                V.stt(L, ex[:, :, 0:1].broadcast_to([128, 4, 128]), -0.5, L, ALU.mult, ALU.add)
                t = V.tt(sig, L, sig, ALU.subtract)
                t = A.act(ex, L, ACT.Exp, t, scale=KAPPA)
                t = A.act(L, L, ACT.Exp, t, scale=-KAPPA)
                t_e = A.act(sig, sig, ACT.Exp, t, scale=-KAPPA)
                kcs, kkc = K[:, :, cs_], KK[:, :, cs_]
                V.stt(e2, ag, -1.0, bc(P["k_a"], 128), ALU.add, ALU.mult)
                V.stt(e2, e2, 1.0, kcs, ALU.add, ALU.mult)
                V.tt(ag, ag, kkc, ALU.mult)
                V.stt(AR[:, :, 0, :], kkc, -1.0, sig, ALU.mult, ALU.mult, t_e, pe_prev)
                if lat:
                    V.tt(AR[:, :, 1, :], R[:, :, ls], L, ALU.mult)
                V.tt(KB[:, 0], e2, ex, ALU.mult)
                t_kb = V.tt(KB[:, 1], ag, ex, ALU.mult)
                if lat:
                    t = V.tt(e2, e2, R[:, :, ls], ALU.mult)
                    bi, b, bf = banks.take()
                    t = T.mm([(b[:, 0:8], e2[:, m, :], IRK[:, m, :], m == 0, m == 3) for m in range(4)], t, *bf)
                    i0, i1 = order[0].index(c), order[1].index(c)
                    opens = (d == 0) if i0 == i1 else (d == (0 if i0 < i1 else 1))
                    if opens:
                        t = V.cp(COEF[:, c - 2, :], b[:, 0:8], t)
                    else:
                        t = V.tt(COEF[:, c - 2, :], COEF[:, c - 2, :], b[:, 0:8], ALU.add, t)
                    banks.give(bi, t)
                for j in range(2):
                    bi, b, bf = banks.take()
                    t = T.tr([(b[:, m * 128:(m + 1) * 128], KB[:, j, m, :]) for m in range(4)], ident, t_kb, *bf)
                    t_knb = A.act(KNB[:, j, :], b, ACT.Copy, t, pe_prev)
                    banks.give(bi, t_knb)
                w_ = 256 if lat else 128
                tG = {}
                tzm = {}
                for buf, nm in ((GBm, "b"), (GKm, "k"), (NM, "n")):
                    n_ = w_ if nm != "n" else 128
                    for g in range(2):
                        tzm[nm, g] = G.zero(buf[:, 4 * g:4 * g + 4, 0:n_], pe_prev, V.last())
                for g in range(2):
                    hs = range(4 * g, 4 * g + 4)
                    for nm, buf, j in (("b", GBm, 1), ("k", GKm, 0)):
                        for q in range(2):
                            hq = range(4 * g + q, 4 * g + 4, 2)
                            bi, b, bf = banks.take()
                            bv = b[:, 0:2 * w_].rearrange("p (h n) -> p h n", h=2)
                            grp = []
                            for n_, h in enumerate(hq):
                                hb, m = hp(h)
                                rhs = AR[hb:hb + 64, m, :, :].rearrange("p j s -> p (j s)")[:, 0:w_]
                                grp.append((bv[:, n_, :], KB[hb:hb + 64, j, m, :], rhs, True, True))
                            t = T.mm(grp, t_kb, *bf)
                            t = V.pred(buf[:, 4 * g + q:4 * g + 4:2, 0:w_], bm(MM["si%d" % d][:, 0:w_].bitcast(U32), 2), bv, t, tzm[nm, g])
                            banks.give(bi, t)
                            tG[nm, g] = t
                for q in range(2):
                    bi, b, bf = banks.take()
                    t = T.mm([(b[:, m * 128:(m + 1) * 128], AR[64 * q:64 * q + 64, m, 0, :], KB[64 * q:64 * q + 64, 1, m, :],
                               True, True) for m in range(4)], t_kb, *bf)
                    t = V.pred(NM[:, q::2, :], bm(MM["sb%d" % d].bitcast(U32), 4),
                               b.rearrange("p (h n) -> p h n", h=4), t, tzm["n", 0], tzm["n", 1])
                    banks.give(bi, t)
                tT, tTT = {}, {}
                for g in range(2):
                    hs = slice(4 * g, 4 * g + 4)
                    V.tt(TI[:, hs, :], NM[:, hs, :], bm(MM["lm%d" % d][:, 0:128], 4), ALU.mult, pe_prev)
                    tT[g] = V.tt(TI[:, hs, :], TI[:, hs, :], bm(ident, 4), ALU.add)
                    V.tt(TT[:, hs, :], GBm[:, hs, 0:128], bm(MM["lm%d" % (1 - d)][:, 0:128], 4), ALU.mult)
                    tTT[g] = V.tt(TT[:, hs, :], TT[:, hs, :], bm(ident, 4), ALU.add)
                for lv in range(1, 7):
                    tX = {}
                    for g in range(2):
                        bi, b, bf = banks.take()
                        t = T.mm([(b[:, n_ * 128:(n_ + 1) * 128], GBm[:, 4 * g + n_, 0:128], TI[:, 4 * g + n_, :], True, True)
                                  for n_ in range(4)], tT[g], *bf)
                        tX[g] = V.tt(XB[:, 4 * g:4 * g + 4, :], b.rearrange("p (h n) -> p h n", h=4),
                                     bm(MM["lm%d" % d][:, lv * 128:(lv + 1) * 128], 4), ALU.mult, t, tTT[g])
                        banks.give(bi, tX[g])
                    for g in range(2):
                        hs = slice(4 * g, 4 * g + 4)
                        bi2, b2, bf2 = banks.take()
                        t2 = T.mm([(b2[:, n_ * 128:(n_ + 1) * 128], XB[:, 4 * g + n_, :], TT[:, 4 * g + n_, :], True, True)
                                   for n_ in range(4)], tX[g], tTT[g], *bf2)
                        if lv < 6:
                            bi1, b1, bf1 = banks.take()
                            t1 = T.mm([(b1[:, n_ * 128:(n_ + 1) * 128], TT[:, 4 * g + n_, :], XB[:, 4 * g + n_, :], True, True)
                                       for n_ in range(4)], tX[g], *bf1)
                            tT[g] = V.tt(TI[:, hs, :], TI[:, hs, :], b1.rearrange("p (h n) -> p h n", h=4), ALU.add, t1)
                            banks.give(bi1, tT[g])
                            t2 = t1
                        tTT[g] = V.tt(TT[:, hs, :], TT[:, hs, :], b2.rearrange("p (h n) -> p h n", h=4), ALU.add, t2)
                        banks.give(bi2, tTT[g])
                t_mp = V.tt(MP, MS[d], bc(DD, 128), ALU.mult, t_D, pe_prev)
                bi, b, bf = banks.take()
                grp = []
                for m in range(4):
                    grp.append((b[:, m * 128:(m + 1) * 128], AR[:, m, 0, :], MP[:, m, :], True, False))
                    for h in (2 * m, 2 * m + 1):
                        grp.append((b[:, h * 64:(h + 1) * 64], GKm[:, h, 0:128], VR[:, c, h * 64:(h + 1) * 64],
                                    False, h % 2 == 1))
                t = T.mm(grp, t_mp, tG["k", 0], tG["k", 1], *t_vr, *bf)
                t = A.act(X0, b, ACT.Copy, t, pe_prev)
                banks.give(bi, t)
                bi, b, bf = banks.take()
                t = T.mm([(b[:, h * 64:(h + 1) * 64], TT[:, h, :], X0[:, h * 64:(h + 1) * 64], True, True) for h in range(8)],
                         t, tTT[0], tTT[1], *bf)
                t_sa = A.act(SA, b, ACT.Copy, t, pe_prev)
                banks.give(bi, t_sa)
                bi, b, bf = banks.take()
                grp = []
                for m in range(4):
                    o, ms = b[:, m * 128:(m + 1) * 128], slice(m * 128, (m + 1) * 128)
                    grp.append((o, KNB[:, 0, ms], VR[:, c, ms], True, False))
                    grp.append((o, KNB[:, 1, ms], SA[:, ms], False, True))
                t = T.mm(grp, t_sa, t_knb, *bf)
                V.tt(MS[d], b.rearrange("p (m v) -> p m v", m=4), bm(C["blk64"], 4), ALU.mult, t)
                banks.give(bi, V.last())
                V.tt(MS[d], MS[d], MP, ALU.add)
                V.tt(MS[d], MS[d], bc(DD, 128), ALU.mult)
                if lat:
                    bi, b, bf = banks.take()
                    grp = []
                    for m in range(4):
                        grp.append((b[:, m * 128:(m + 1) * 128], AR[:, m, 1, :], MP[:, m, :], True, False))
                        for h in (2 * m, 2 * m + 1):
                            o, hs = b[:, h * 64:(h + 1) * 64], slice(h * 64, (h + 1) * 64)
                            grp.append((o, GKm[:, h, 128:256], VR[:, c, hs], False, False))
                            grp.append((o, GBm[:, h, 128:256], SA[:, hs], False, h % 2 == 1))
                    t = T.mm(grp, t_sa, *bf)
                    if opens:
                        t = V.cp(YS[:, c - 2, :], b, t)
                    else:
                        t = V.tt(YS[:, c - 2, :], YS[:, c - 2, :], b, ALU.add, t)
                    banks.give(bi, t)

        if dbg:
            dbg("ys", YS, V, G, dsem)
        f = fence()
        if dbg:
            f = f + dbg.toks
        ar.top = mark4 + 5 * 512
        GW, GBi = ar.get(512), ar.get(512)
        B2 = ar.get(2048, m=4, s=512)
        st = ar.get(64)
        d_gn = dsem()
        d_bk = dsem()
        t_hb = G.dma(HT.rearrange("p k s -> p (k s)"), htd, d_bk, *f)
        t_xb = G.dma(X.rearrange("p t d -> p (t d)"), xd, d_bk, *f)
        t_hb = t_xb
        t_gn = G.dma(GW, T_["gn_w_2"][0, :].partition_broadcast(128), d_gn, *f)
        t_gn = G.dma(GBi, T_["gn_b_2"][0, :].partition_broadcast(128), d_gn, *f)
        t_b2 = []
        yp = [None, None]
        for i in range(4):
            y3 = YS[:, i, :].rearrange("p (h d) -> p h d", h=8)
            q_ = fl[2 + i % 2]
            q3 = q_.rearrange("p (h d) -> p h d", h=8)
            V.red(st[:, 0:8], y3, ALU.add, *f)
            V.ts(st[:, 0:8], st[:, 0:8], 1.0 / 64, None, ALU.mult, None)
            V.tt(y3, y3, bc(st[:, 0:8], 64), ALU.subtract)
            V.tt(q3, y3, y3, ALU.mult, yp[i % 2])
            t = V.red(st[:, 8:16], q3, ALU.add)
            t = A.act(st[:, 16:24], st[:, 8:16], ACT.Sqrt, t, bias=eps[:, 1:2], scale=1.0 / 64)
            V.rec(st[:, 24:32], st[:, 16:24], t)
            V.tt(y3, y3, bc(st[:, 24:32], 64), ALU.mult)
            V.tt(YS[:, i, :], YS[:, i, :], GW, ALU.mult, t_gn)
            V.tt(YS[:, i, :], YS[:, i, :], GBi, ALU.add)
            V.tt(q3, VR[:, 2 + i, :].rearrange("p (h d) -> p h d", h=8), bc(COEF[:, i, :], 64), ALU.mult)
            V.tt(YS[:, i, :], YS[:, i, :], q_, ALU.add)
            bi, b, bf = banks.take()
            t = T.mm([(b, SG[:, i * 128:(i + 1) * 128], G2, True, True)], t_sg, t_rw, *bf)
            t = V.tt(YS[:, i, :], YS[:, i, :], b, ALU.mult, t)
            banks.give(bi, t)
            bi, b, bf = banks.take()
            t = T.tr([(b[:, q * 128:(q + 1) * 128], YS[:, i, q * 128:(q + 1) * 128]) for q in range(4)], ident, t, *bf)
            t = A.act(B2[:, :, i * 128:(i + 1) * 128], b.rearrange("p (q s) -> p q s", q=4), ACT.Copy, t, *f)
            banks.give(bi, t)
            t_b2.append(t)
        if dbg:
            dbg("b2", B2, V, G, dsem)

        f = fence()
        if dbg:
            f = f + dbg.toks
        b2_top = ar.top
        ar.top = mark2
        B01 = ar.get(4096, b=2, m=4, s=512)
        MG = ar.get(4096, m=8, s=512)
        gt = [ar.get(512) for _ in range(4)]
        assert ar.top <= mark4 + 5 * 512
        d_re = dsem()
        t_re = G.dma(B01.rearrange("p b m s -> p b (m s)"), brd.rearrange("b p n -> p b n"), d_re, *f, t_brd)
        br = [B01[:, 0], B01[:, 1], B2]
        t_bin = [t_re] + t_b2
        gj = 0
        grd = [None, None, None, None]
        t_mg = {}
        for n in range(3):
            g0 = chunk(34 + 2 * n)
            wbr = chunk(40 + n)
            g1 = chunk(35 + 2 * n)
            wb3 = wbr[1].rearrange("p (k n) -> p k n", k=4)
            for m in range(8):
                gs_ = g0 if m < 4 else g1
                wg = gs_[1].rearrange("p (k n) -> p k n", k=8)
                mc = slice((m % 4) * 128, (m % 4 + 1) * 128)
                bi, b, bf = banks.take()
                t = T.mm([(b, wg[:, k, mc], HT[:, k, :], k == 0, k == 7) for k in range(8)], gs_[2], t_hb, *bf)
                if m % 4 == 3:
                    W.give(gs_[0], t)
                gg = gt[gj % 4]
                tg = A.act(gg, b, ACT.Sigmoid, t, *f, grd[gj % 4])
                banks.give(bi, tg)
                bi, b, bf = banks.take()
                t = T.mm([(b, wb3[:, k, m * 128:(m + 1) * 128], br[n][:, k, :], k == 0, k == 3) for k in range(4)],
                         wbr[2], *t_bin, *bf)
                if m == 7:
                    W.give(wbr[0], t)
                if n == 0:
                    t = V.tt(MG[:, m, :], gg, b, ALU.mult, tg, t, *f)
                    banks.give(bi, t)
                else:
                    t = V.tt(gg, gg, b, ALU.mult, tg, t)
                    banks.give(bi, t)
                    t = V.tt(MG[:, m, :], MG[:, m, :], gg, ALU.add)
                grd[gj % 4] = t
                t_mg[m] = t
                gj += 1
        f = fence()
        ar.top = mark2 + 8192 + 2048
        rowA, rowB = ar.get(1024), ar.get(1024)
        d_r = dsem()
        t_m = mod_load(rowA, 2, 2, f)
        tt_ = [ar.get(512) for _ in range(2)]
        t_x2 = []
        for hf in range(2):
            ws, wb, wt = chunk(43 + hf)
            w = wb.rearrange("p (k n) -> p k n", k=8)
            for i in range(4):
                bi, b, bf = banks.take()
                t = T.mm([(b, MG[:, k, i * 128:(i + 1) * 128], w[:, k, :], k == 0, k == 7) for k in range(8)],
                         wt, *t_mg.values(), *bf)
                if i == 3:
                    W.give(ws, t)
                tq = tt_[i % 2]
                t = V.tt(tq, b, rowA[:, hf * 512:(hf + 1) * 512], ALU.mult, t, t_m, *f)
                banks.give(bi, t)
                xs = X[:, i, hf * 512:(hf + 1) * 512]
                t_x2.append(V.tt(xs, xs, tq, ALU.add, t_xb))
        if dbg:
            dbg("x2", X, V, G, dsem)

        f = fence()
        if dbg:
            f = f + dbg.toks
        ar.top = base + 2048 + 64
        extra = ar.top
        small2 = small
        gs, sh = ar.get(1024), ar.get(1024)
        ht = [ar.get(1024) for _ in range(4)]
        sqb = ar.get(1024)
        n2 = ar.get(1024)
        WRT = ar.get(288, k=8, e=36)
        RT = ar.get(4 * 36, t=4, e=36)
        d_q = dsem()
        t_l = [mod_load(gs, 2, 4, f), mod_load(sh, 2, 3, f), G.dma(n2, T_["norm2_g_2"].partition_broadcast(128), d_q, *f),
               G.dma(WRT, T_["w_router"].rearrange("(k p) e -> p k e", p=128), d_q, *f)]
        t_l[2] = t_l[3]
        t_gs = V.stt(gs, gs, 1.0, n2, ALU.add, ALU.mult, *t_l, *f)
        d_fd = dsem()
        fdv = fd.rearrange("(t p) d -> p t d", p=128)
        f5_ = transposed(HT, f)
        t_fd = []

        def dest(i, h, t):
            t_fd.append(G.dma(fdv[:, i, :], h, d_fd, t))
            f5_(i, h, t)
            return None

        ss = small[:, 0:4]
        for i in range(4):
            t = A.act(sqb, X[:, i, :], ACT.Square, *t_x2, *f, accum_out=ss[:, i:i + 1])
        t = A.act(small[:, 8:12], ss, ACT.Sqrt, bias=eps[:, 0:1], scale=1.0 / D)
        V.rec(small[:, 16:20], small[:, 8:12], t)
        for i in range(4):
            V.stt(ht[i], X[:, i, :], small[:, 16 + i:17 + i], gs, ALU.mult, ALU.mult, *t_l, *f)
            t = V.tt(ht[i], ht[i], sh, ALU.add)
            dest(i, ht[i], t)
        bi, b, bf = banks.take()
        g_ = []
        for i in range(4):
            g_ += [(b[:, i * 36:(i + 1) * 36], HT[:, k, i * 128:(i + 1) * 128], WRT[:, k, :], k == 0, k == 7) for k in range(8)]
        t = T.mm(g_, *f5_.done, *t_l, *bf)
        t = V.cp(RT, b[:, 0:144].rearrange("p (t e) -> p t e", t=4), t)
        banks.give(bi, t)

        def s4(n, **dims):
            return ar.get(n, **dims)

        GP = s4(32, t=4, e=8)
        GM = s4(32, t=4, e=8)
        GI = ar.get(32, U32, t=4, e=8)
        grp = s4(4)
        EQ = s4(128, t=4, e=32)
        LE = s4(128, t=4, e=32)
        TV = s4(32, t=4, e=8)
        TIx = ar.get(32, U32, t=4, e=8)
        EF = s4(8, t=4, e=2)
        E1, E2, IN, RK, Q_, QP, DM = [s4(128, t=4, e=32) for _ in range(7)]
        sm_, pg, dif, exd, g1_, g2_ = [s4(4) for _ in range(6)]
        gex = s4(16, t=4, e=4)
        OVi, OVx, cnt, ov, o1 = [s4(32) for _ in range(5)]
        EID = s4(8)
        DF = s4(8, t=4, e=2)
        DI = ar.get(8, I32, t=4, e=2)
        TOK = ar.get(4, I32)
        IDX = ar.get(NB, I32)
        ZI = ar.get(NB, I32)
        onesr = s4(32)
        zrow = sqb
        Gg = ar.get(8, t=4, e=2)
        t_z = V.zero(zrow, *f)
        V.zero(ZI.bitcast(F))
        V.zero(onesr, value=1.0)
        V.zero(GP, value=-3.0e38)
        t = V.zero(LE, value=-3.0e38)
        d_i = dsem()
        t_i0 = G.dma(idxd.rearrange("(r b) o -> r (b o)", b=NB), ZI, d_i, t)
        t_tok = G.dma(TOK, T_["tok"], d_i, *f)
        d_y0 = dsem()
        t_y0 = None
        for j in range(OVF):
            t_y0 = G.dma(ydv[:, 32 + j, :], zrow, d_y0, t)
        V.cp(GP[:, :, 0:4], RT[:, :, 0:4])
        for i in range(4):
            V.put([lambda e, i=i: e.max(GM[:, i, :], GP[:, i, :])], [])
            V.put([lambda e, i=i: e.max_index(GI[:, i, :], GM[:, i, :], GP[:, i, :])], [])
        V.cp(grp.unsqueeze(2), GI[:, :, 0:1])
        V.ts(pg.unsqueeze(2), GM[:, :, 0:1], -1.0, None, ALU.mult, None)
        t = V.tt(gex, RT[:, :, 0:4], bc(pg, 4), ALU.add)
        t = A.act(gex, gex, ACT.Exp, t)
        V.red(sm_, gex, ALU.add, t)
        V.rec(pg, sm_)
        V.tt(EQ, bm(C["grp32"], 4), bc(grp, 32), ALU.is_equal)
        V.pred(LE, EQ.bitcast(U32), RT[:, :, 4:36])
        for i in range(4):
            V.put([lambda e, i=i: e.max(TV[:, i, :], LE[:, i, :])], [])
            V.put([lambda e, i=i: e.max_index(TIx[:, i, :], TV[:, i, :], LE[:, i, :])], [])
        V.cp(EF, TIx[:, :, 0:2])
        t = V.tt(dif.unsqueeze(2), TV[:, :, 1:2], TV[:, :, 0:1], ALU.subtract)
        t = A.act(exd, dif, ACT.Exp, t)
        V.ts(g1_, exd, 1.0, None, ALU.add, None, t)
        V.rec(g1_, g1_)
        V.tt(g1_, g1_, pg, ALU.mult)
        V.tt(g2_, g1_, exd, ALU.mult)
        V.cp(Gg[:, :, 0], g1_)
        t_gate = V.cp(Gg[:, :, 1], g2_)
        V.tt(E1, bm(C["iota32"], 4), EF[:, :, 0:1].broadcast_to([128, 4, 32]), ALU.is_equal)
        V.tt(E2, bm(C["iota32"], 4), EF[:, :, 1:2].broadcast_to([128, 4, 32]), ALU.is_equal)
        t = V.tt(IN, E1, E2, ALU.add)
        bi, b, bf = banks.take()
        g_ = []
        for i in range(4):
            o = b[:, i * 32:(i + 1) * 32]
            for q in range(i):
                g_.append((o, ones, IN[:, q, :], q == 0, False))
            g_.append((o, C["tri"], IN[:, i, :], i == 0, True))
        for q in range(4):
            g_.append((b[:, 128:160], ones, IN[:, q, :], q == 0, q == 3))
        t = T.mm(g_, t, *bf)
        V.cp(RK, b[:, 0:128].rearrange("p (t e) -> p t e", t=4), t)
        t = V.cp(cnt, b[:, 128:160])
        banks.give(bi, t)
        V.ts(ov, cnt, 128.5, None, ALU.is_ge, None)
        for th in (256.5, 384.5):
            V.ts(o1, cnt, th, None, ALU.is_ge, None)
            V.tt(ov, ov, o1, ALU.add)
        V.scan(OVi, onesr, ov)
        V.tt(OVx, OVi, ov, ALU.subtract)
        t_iov = V.cp(iovn, OVi[:, 31:32])
        for j in range(OVF):
            V.ts(o1, OVi, j + 0.5, None, ALU.is_le, None)
            V.red(EID[:, j:j + 1], o1, ALU.add)
        V.ts(EID[:, 0:OVF], EID[:, 0:OVF], 31.0, None, ALU.min, None)
        t_iov = V.cp(iov[:, 0:OVF], EID[:, 0:OVF])
        V.ts(Q_, RK, 127.5, None, ALU.is_ge, None)
        V.cp(QP, Q_)
        for th in (255.5, 383.5):
            V.ts(DM, RK, th, None, ALU.is_ge, None)
            V.tt(Q_, Q_, DM, ALU.add)
        V.stt(RK, Q_, -128.0, RK, ALU.mult, ALU.add)
        V.tt(DM, Q_, bm(OVx, 4), ALU.add)
        V.ts(DM, DM, 31.0, None, ALU.add, None)
        V.tt(DM, DM, bm(C["iota32"], 4), ALU.subtract)
        V.tt(DM, DM, QP, ALU.mult)
        V.tt(DM, DM, bm(C["iota32"], 4), ALU.add)
        V.stt(DM, RK, float(NB), DM, ALU.mult, ALU.add)
        for j, E_ in enumerate((E1, E2)):
            V.tt(E_, E_, DM, ALU.mult)
            V.red(DF[:, :, j:j + 1], E_, ALU.add)
        t_di = V.cp(DI, DF)
        d_s = dsem()
        for i in range(4):
            for j in range(2):
                tok = d_s.add()
                G.items.append(([lambda e, i=i, j=j: e.indirect_dma_start(
                    idxd, bass.IndirectOffsetOnAxis(ap=DI[:, i, j:j + 1], axis=0), TOK[:, i:i + 1], None)],
                    [t_di, t_i0, t_tok], (d_s.sem, 16)))
        d_ix = dsem()
        t_idx = G.dma(IDX, idxd.rearrange("(r b) o -> r (b o)", b=NB), d_ix, tok)

        f = fence() + [t_fd[-1], t_y0, t_i0, t_idx]
        YO = [ar.get(1024) for _ in range(2)]
        n_extra = (NCOL - ar.top) // 4096
        more = [ar.get(4096) for _ in range(n_extra)] + [HT.rearrange("p k s -> p (k s)")]
        ar.top = extra
        XG = [ar.get(1024) for _ in range(2)]
        XT = [ar.get(1024, k=8, s=128) for _ in range(2)]
        SGm = [ar.get(512) for _ in range(2)]
        AC = [ar.get(512) for _ in range(2)]
        ACT_T = [ar.get(512, k=4, s=128) for _ in range(2)]
        rowC = ar.get(1024)
        assert ar.top <= extra + 8192
        pad = (-W.slots.i) % len(W.slots.bufs)
        W.slots.i += pad
        W.grow(more, *f)
        W.slots.i = 0
        t_rc = mod_load(rowC, 2, 5, f)
        d_xg = [dsem() for _ in range(2)]
        d_yo = [dsem() for _ in range(2)]

        class Experts:
            def __init__(self, L, W_, f, dx, dy):
                self.L, self.W, self.f = L, W_, f
                self.s = {}
                self.dx, self.dy = dx, dy
                self.done = []

            def front(self, e, blk, src, idx_ap):
                T, V, A, G, Y = [self.L[x] for x in "TVAGY"]
                s, p = self.s, e % 2
                tok = self.dx[p].add()
                G.items.append(([lambda eng: eng.indirect_dma_start(
                    XG[p], None, fd, bass.IndirectOffsetOnAxis(ap=idx_ap, axis=0))],
                    [t_idx, *t_fd, *self.f, s.get(("tr", e - 2))], (self.dx[p].sem, 16)))
                w = [self.W.load(src(j), Y) for j in range(3)]
                s["w", e] = w
                for half in range(2):
                    bi, b, bf = banks.take()
                    t = T.tr([(b[:, q * 128:(q + 1) * 128], XG[p][:, (4 * half + q) * 128:(4 * half + q + 1) * 128])
                              for q in range(4)], ident, tok, *bf)
                    o = XT[p][:, 4 * half:4 * half + 4, :]
                    sv = b.rearrange("p (q s) -> p q s", q=4)
                    te = V.cp(o, sv, t, s.get(("gu", e - 2)), *self.f)
                    banks.give(bi, te)
                    s["xt", e, half] = te
                s["tr", e] = t
                bb = []
                for j in range(2):
                    ws, wb, wt = w[j]
                    wv = wb.rearrange("p (k n) -> p k n", k=8)
                    bi, b, bf = banks.take()
                    t = T.mm([(b, XT[p][:, k, :], wv[:, k, :], k == 0, k == 7) for k in range(8)],
                             wt, s["xt", e, 0], s["xt", e, 1], *bf)
                    self.W.give(ws, t)
                    bb.append((bi, b, t))
                s["gu", e] = t
                (gi, gb, tg), (ui, ub, tu) = bb
                t = A.act(SGm[p], gb, ACT.Sigmoid, tg, s.get(("ac", e - 2)), *self.f)
                t = V.tt(SGm[p], SGm[p], gb, ALU.mult, t)
                banks.give(gi, t)
                s["ac", e] = t = V.tt(AC[p], SGm[p], ub, ALU.mult, tu, s.get(("at", e - 2)))
                banks.give(ui, t)

            def back(self, e, blk):
                T, V, A, G, Y = [self.L[x] for x in "TVAGY"]
                s, p = self.s, e % 2
                bi, b, bf = banks.take()
                s["at", e] = t = T.tr([(b[:, q * 128:(q + 1) * 128], AC[p][:, q * 128:(q + 1) * 128]) for q in range(4)],
                                      ident, s["ac", e], *bf)
                t = A.act(ACT_T[p], b.rearrange("p (q s) -> p q s", q=4), ACT.Copy, t, s.get(("dn", e - 2)), *self.f)
                banks.give(bi, t)
                ws, wb, wt = s["w", e][2]
                wv = wb.rearrange("p (k n) -> p k n", k=4)
                for hf in range(2):
                    bi, b, bf = banks.take()
                    td = T.mm([(b, ACT_T[p][:, k, :], wv[:, k, hf * 512:(hf + 1) * 512], k == 0, k == 3) for k in range(4)],
                              wt, t, *bf)
                    o = YO[p][:, hf * 512:(hf + 1) * 512]
                    ty = A.act(o, b, ACT.Copy, td, s.get(("yo", e - 2)), *self.f)
                    banks.give(bi, ty)
                s["dn", e] = td
                self.W.give(ws, td)
                s["yo", e] = A.dma(ydv[:, blk, :], YO[p], self.dy[p], ty, t_y0)
                self.done.append(s["yo", e])

        ex = Experts(main, W, f, d_xg, d_yo)
        for e in range(33):
            if e < 32:
                ex.front(e, e, lambda j, e=e: T_["w"][45 + 3 * e + j], IDX[:, e:e + 1])
            if e >= 1:
                ex.back(e - 1, e - 1)
        t_yd = ex.done[-2:]

        f = fence() + t_yd
        ovl = {n: Lane(sem(f"o_{n}"), n in "VAG") for n in "TVAGY"}
        saved = (banks.free, banks.i)
        banks.free = [[] for _ in banks.bufs]

        class OvfStream(Stream):
            pass

        WO = OvfStream()
        WO.grow(W.slots.bufs[0:6])
        ev = {}
        oex = Experts(ovl, WO, [], [dsem(), dsem()], [dsem(), dsem()])
        for n in "TVAGY":
            ovl[n].items.append(([], f, None))
        regs = {}
        for j in range(OVF):
            def src(q, j=j):
                return ("dyn", j, q)
            oex_load = WO.load

            def load(s_, lane, j=j):
                k, buf, free = WO.slots.take()
                d = WO.d[k]
                tok = d.add()

                def go(e, s_=s_, buf=buf):
                    if s_[2] == 0:
                        regs[s_[1]] = e.value_load(iov[0:1, s_[1]:s_[1] + 1], min_val=0, max_val=31)
                    r = regs[s_[1]]
                    return e.dma_start(buf, T_["w"][bass.ds(r * 3 + (45 + s_[2]), 1)][0])
                lane.items.append(([go], free, (d.sem, 16)))
                return k, buf, tok
            WO.load = load
            oex.front(j, 32 + j, src, IDX[:, 32 + j:33 + j])
            oex.back(j, 32 + j)
        ovl["A"].items.append(([], oex.done[-2:], None))
        ovl["G"].items.append(([], oex.done[-2:] + [ovl["T"].last(), ovl["V"].last(), ovl["A"].last()], None))
        banks.free, banks.i = saved

        tail = {n: Lane(sem(f"t_{n}"), n in "VAG") for n in "TVAGY"}
        V2, G2_, A2_ = tail["V"], tail["G"], tail["A"]
        y12 = [[XG[0], XG[1]], [YO[0], YO[1]]]
        d_y = [dsem() for _ in range(2)]
        d_o = dsem()
        done = [None, None]
        t_all = [*t_yd, t_y0, T.last(), V.last(), A.last()]
        for i in range(4):
            bufs = y12[i % 2]
            for j in range(2):
                ty = d_y[i % 2].add()
                G2_.items.append(([lambda e, i=i, j=j, bufs=bufs: e.indirect_dma_start(
                    bufs[j], None, yd, bass.IndirectOffsetOnAxis(ap=DI[:, i, j:j + 1], axis=0))],
                    [*t_all, done[i % 2]], (d_y[i % 2].sem, 16)))
            V2.ts(bufs[0], bufs[0], Gg[:, i, 0:1], None, ALU.mult, None, ty, t_gate, t_rc)
            V2.stt(bufs[0], bufs[1], Gg[:, i, 1:2], bufs[0], ALU.mult, ALU.add)
            V2.tt(bufs[0], bufs[0], rowC, ALU.mult)
            t = done[i % 2] = V2.tt(X[:, i, :], X[:, i, :], bufs[0], ALU.add)
            t_out = A2_.dma(out_d[:, i, :], X[:, i, :], d_o, t)
        A2_.items.append(([], [t_out], None))
        ends = [t_out]
        if dbg:
            A2_.items.append(([], dbg.toks, None))

        block = ctx.enter_context(nc.Block())

        def program(eng, n):
            seen = {}
            main[n].run(eng, seen)
            eng.wait_ge(V.sem, t_iov[1])
            r = eng.value_load(iovn[0:1, 0:1], min_val=0, max_val=OVF)
            with eng.If(r > (-1 if force_ovf else 0)):
                ovl[n].run(eng, dict(seen))
            tail[n].run(eng, dict(seen))

        @block.sync
        def _(e):
            program(e, "Y")

        @block.gpsimd
        def _(e):
            program(e, "G")

        @block.scalar
        def _(e):
            program(e, "A")

        @block.vector
        def _(e):
            program(e, "V")

        @block.tensor
        def _(e):
            program(e, "T")


def chunks(i):
    def cut(w, k, n):
        r, c = w.shape
        return [w[:, j * n:(j + 1) * n].reshape(k, 128, n).transpose(1, 0, 2).reshape(128, k * n) for j in range(c // n)]

    w2 = i["w_in_2"][0]
    mid = np.zeros((1024, 512), np.float32)
    mid[:, 0:384] = w2[:, 3584:3968]
    out = np.empty((141, 128, 4096), np.float32)
    at = 0
    parts = [(i["w_ada"][0], 8, 512), (i["w_in"][0], 8, 512), (i["w_out"][0], 8, 512), (i["w_ada_2"][0], 8, 512),
             (w2[:, 0:3584], 8, 512), (mid, 8, 512), (w2[:, 3968:7040], 8, 512)]
    parts += [(i["w_br_2"][0, n], 4, 1024) for n in range(3)] + [(i["w_out_2"][0], 8, 512)]
    for e in range(32):
        parts += [(i["w_exp_gate_2"][0, e], 8, 512), (i["w_exp_up_2"][0, e], 8, 512), (i["w_exp_down_2"][0, e], 4, 1024)]
    for w, k, n in parts:
        for c in cut(w, k, n):
            out[at] = c
            at += 1
    assert at == 141
    return out


def params(i):
    def col(v):
        return np.ascontiguousarray(v, np.float32).reshape(-1, 128).T

    p = {
        "c": col(i["c"]), "c2": col(i["c_2"]), "cc": col(i["c_ctx_2"]), "conv_w": col(i["conv_w"][0]),
        "conv_b": col(i["conv_b"]), "b_a": col(i["b_rg_a"]), "b_x": col(i["b_rg_x"]), "lam": col(i["lru_lambda"]),
        "norm_rec": col(i["norm_rec"]), "qn": col(np.tile(i["q_norm_g_2"][0], 2)), "kn": col(np.tile(i["k_norm_g_2"][0], 2)),
        "mu0": col(i["shift_mu_2"][0, 0]), "mu1": col(i["shift_mu_2"][0, 1]), "w0": col(i["decay_w0_2"][0]),
        "a0": col(i["aaa_a0_2"][0]), "k_k": col(i["k_k_2"]), "k_a": col(i["k_a_2"]), "r_k": col(i["r_k_2"]),
        "pscale": col(i["pool_scale_2"]),
    }
    return np.concatenate([p[n] for n, _ in COL_SPEC], 1)


def lru_weights(i):
    out = np.zeros((128, 8, 128), np.float32)
    for j, n in enumerate(("w_rg_a", "w_rg_x")):
        for h in range(8):
            o = 64 * (h % 2)
            out[o:o + 64, 4 * j + h // 2, o:o + 64] = i[n][0, h]
    return out.reshape(128, 1024)


def constants():
    p = np.arange(128)
    c = {n: np.zeros((128, w), np.float32) for n, w in CONST_SPEC}
    c["ident"][:] = np.eye(128)
    c["ones"][:] = 1
    c["blk64"][:] = (p[:, None] // 64 == p[None] // 64)
    s1 = (p // 64) * 64 + (p % 64 + 32) % 64
    c["perm1"][s1, p] = 1
    s2 = (p // 32) * 32 + (p % 32 + 16) % 32
    c["perm2"][s2, p] = 1
    c["tri"][:] = p[:, None] < p[None]
    for j in range(18):
        c["selp"][j, 2 * j:2 * j + 2] = 1
    f = (10000.0 ** (-np.arange(32) / 32.0)).astype(np.float32)
    c["invf"][:, 0] = f[p % 32]
    c["sgn"][:, 0] = np.where(p % 64 < 32, -1, 1)
    c["iota32"][:] = np.arange(32)
    c["grp32"][:] = np.arange(32) // 8
    for m in range(4):
        c["ind"][p, 8 * m + 2 * m + p // 64] = 1
    return np.concatenate([c[n] for n, _ in CONST_SPEC], 1)


def mask_constants():
    p = np.arange(128)
    t, s = p[:, None], p[None]
    c = {}
    for d in range(2):
        lv = []
        for b in range(7):
            m = 1 << b
            same = t // (2 * m) == s // (2 * m)
            tb, sb_ = (t // m) % 2, (s // m) % 2
            lv.append(same & ((tb == 1) & (sb_ == 0) if d == 0 else (tb == 0) & (sb_ == 1)))
        c["lm%d" % d] = np.concatenate(lv, 1)
        before = (t < s) if d == 0 else (t > s)
        c["si%d" % d] = np.concatenate([before, before | (t == s)], 1)
        c["sb%d" % d] = (s < t) if d == 0 else (s > t)
    return np.concatenate([c[n] for n, _ in MASK_SPEC], 1).astype(np.float32)


def rope_constants():
    tok = np.arange(S)
    f = (10000.0 ** (-np.arange(16) / 16.0)).astype(np.float32)
    rows, cols = (tok // 64).astype(np.float32), (tok % 64).astype(np.float32)
    p = np.arange(128)
    pos = np.where(((p % 64) < 32)[:, None], rows[None], cols[None])
    ang = (pos * f[p % 16][:, None]).astype(np.float32).astype(np.float64)
    sgn = np.where(p % 32 < 16, -1.0, 1.0)[:, None]
    cnt = []
    for w in (2, 4, 8, 16):
        lo = np.clip(tok - w // 2, 0, S - 1)
        hi = np.clip(tok + w // 2 - 1, 0, S - 1)
        cnt.append(np.broadcast_to(1.0 / (hi - lo + 1), (128, S)))
    return np.concatenate([np.cos(ang), np.sin(ang) * sgn] + cnt, 1).astype(np.float32)


def multiplicities():
    out = []
    for i in range(4):
        q = np.arange(128)[:, None] + 128 * i
        k = np.arange(128 * (i + 1))[None]
        dist = q - k
        n = ((dist >= 0) & (dist <= 128)).astype(int) + ((dist >= 0) & (dist % 4 == 0)) + ((dist >= 0) & (dist % 16 == 0))
        out.append(np.where(n > 0, np.log(np.maximum(n, 1)), -1e30))
    return np.concatenate(out, 1).astype(np.float32)


def arrays_of(i):
    i = {k: np.asarray(v) for k, v in i.items()}
    a = {
        "w": chunks(i), "params": params(i), "consts": constants(), "masks": mask_constants(), "ropes": rope_constants(),
        "lnc": multiplicities(), "w_rg": lru_weights(i),
        "bias": np.concatenate([i["b_ada"][0].reshape(6, 512), i["b_ada_2"][0].reshape(12, 512)], 0),
        "x": i["x"], "positions": i["positions"].astype(np.int32) if i["positions"].dtype != np.int32 else i["positions"],
        "norm_pre": i["norm_pre"][0], "norm_post": i["norm_post"][0], "norm_att": i["norm_att"][0],
        "ctx_2": i["ctx_2"], "norm1_g_2": i["norm1_g_2"][0], "norm2_g_2": i["norm2_g_2"][0],
        "pool_w_2": i["pool_w_2"], "lambda_qk_2": i["lambda_qk_2"], "subln": np.tile(i["subln_g_2"][0], 4),
        "decay_w2": i["decay_w2_2"][0].reshape(128, 512), "aaa_a2": i["aaa_a2_2"][0].reshape(128, 512),
        "gate_w2": i["gate_w2_2"][0], "gn_w_2": i["gn_w_2"], "gn_b_2": i["gn_b_2"],
        "w_router": np.concatenate([i["w_router_group_2"][0], i["w_router_expert_2"][0]], 1),
        "tok": (np.arange(4)[None] * 128 + np.arange(128)[:, None]).astype(np.int32),
    }
    return {k: np.ascontiguousarray(v) for k, v in a.items()}


def kernel(**inputs):
    import concourse.bacc as bacc
    from concourse.bass_utils import run_bass_kernel_spmd

    nc = bacc.Bacc("TRN2", target_bir_lowering=False, num_devices=1)
    a = arrays_of(inputs)
    t = {n: nc.dram_tensor(f"in_{n}", v.shape, mybir.dt.from_np(v.dtype), kind="ExternalInput").ap() for n, v in a.items()}
    t["out"] = nc.dram_tensor("out", (1, S, D), F, kind="ExternalOutput").ap()
    build(nc, t)
    r = run_bass_kernel_spmd(nc, [{f"in_{n}": v for n, v in a.items()}], core_ids=[0])
    return r.results[0]["out"]
```

```python
import math
from contextlib import ExitStack

import numpy as np

import concourse.bass as bass
from concourse import mybir

F = mybir.dt.float32
I32 = mybir.dt.int32
U32 = mybir.dt.uint32
ALU = mybir.AluOpType
ACT = mybir.ActivationFunctionType
AX = mybir.AxisListType.X

D = 1024
S = 512
CTX = 256
NB = 39
OVF = 7
KAPPA = math.exp(-0.5)
EPS = 1e-6
GN_EPS = 64e-5
NCOL = 53100
LAG = 12

COL_SPEC = [
    ("c", 8), ("c2", 8), ("cc", 8), ("conv_w", 16), ("conv_b", 4), ("b_a", 4), ("b_x", 4), ("lam", 4),
    ("norm_rec", 4), ("qn", 1), ("kn", 1), ("mu0", 15), ("mu1", 15), ("w0", 8), ("a0", 8), ("k_k", 4),
    ("k_a", 4), ("r_k", 4), ("pscale", 4),
]
COLS = {}
_o = 0
for _n, _w in COL_SPEC:
    COLS[_n] = (_o, _o + _w)
    _o += _w
NPARAM = _o

CONST_SPEC = [
    ("ident", 128), ("ones", 128), ("blk64", 128), ("perm1", 128), ("perm2", 128), ("tri", 128),
    ("selp", 36), ("invf", 1), ("sgn", 1), ("iota32", 32), ("grp32", 32), ("ind", 32),
]
MASK_SPEC = [("lm0", 7 * 128), ("lm1", 7 * 128), ("si0", 256), ("si1", 256), ("sb0", 128), ("sb1", 128)]
ROPE_SPEC = [("cos2", 512), ("sin2", 512), ("cnt", 2048)]


def offsets(spec):
    out, o = {}, 0
    for n, w in spec:
        out[n] = (o, o + w)
        o += w
    return out, o


CONSTS, NCONST = offsets(CONST_SPEC)
MASKS, NMASK = offsets(MASK_SPEC)
ROPES, NROPE = offsets(ROPE_SPEC)
LNC_OFF = [0, 128, 384, 768]
LNC_N = 1280


class Dma:

    def __init__(self, sem):
        self.sem, self.n = sem, 0

    def add(self):
        self.n += 16
        return (self.sem, self.n)


class Lane:

    def __init__(self, sem, chain):
        self.sem, self.n, self.items, self.chain = sem, 0, [], chain

    def put(self, fns, after):
        own = [(self.sem, self.n)] if self.chain and self.n else []
        self.items.append((fns, list(after) + own, (self.sem, 1)))
        self.n += 1
        return (self.sem, self.n)

    def last(self):
        return (self.sem, self.n)

    def dma(self, out, in_, d, *after):
        tok = d.add()
        self.items.append(([lambda e: e.dma_start(out, in_)], list(after), (d.sem, 16)))
        return tok

    def run(self, e, seen):
        for fns, after, inc in self.items:
            need = {}
            for t in after:
                if t is not None:
                    need[id(t[0])] = max(t, need.get(id(t[0]), t), key=lambda q: q[1])
            for k, (sem, v) in need.items():
                if v > seen.get(k, 0):
                    seen[k] = v
                    e.wait_ge(sem, v)
            for f in fns:
                ins = f(e)
            if inc is not None:
                ins.then_inc(*inc)

    def tt(self, out, a, b, op, *after):
        return self.put([lambda e: e.tensor_tensor(out, a, b, op)], after)

    def ts(self, out, a, s1, s2, op0, op1, *after):
        if s2 is None:
            return self.put([lambda e: e.tensor_scalar(out, a, s1, None, op0)], after)
        return self.put([lambda e: e.tensor_scalar(out, a, s1, s2, op0, op1)], after)

    def stt(self, out, a, s, b, op0, op1, *after):
        return self.put([lambda e: e.scalar_tensor_tensor(out=out, in0=a, scalar=s, in1=b, op0=op0, op1=op1)], after)

    def cp(self, out, a, *after):
        return self.put([lambda e: e.tensor_copy(out, a)], after)

    def rec(self, out, a, *after):
        return self.put([lambda e: e.reciprocal(out, a)], after)

    def zero(self, out, *after, value=0.0):
        return self.put([lambda e: e.memset(out, value)], after)

    def red(self, out, a, op, *after, negate=None):
        return self.put([lambda e: e.tensor_reduce(out, a, AX, op, negate=negate)], after)

    def pred(self, out, mask, a, *after):
        return self.put([lambda e: e.copy_predicated(out, mask, a)], after)

    def scan(self, out, d0, d1, *after):
        return self.put([lambda e: e.tensor_tensor_scan(out, d0, d1, 0.0, ALU.mult, ALU.add)], after)

    def act(self, out, a, func, *after, **kw):
        return self.put([lambda e: e.activation(out, a, func, **kw)], after)

    def mm(self, group, *after):
        return self.put([lambda e, g=g: e.matmul(g[0], g[1], g[2], start=g[3], stop=g[4]) for g in group], after)

    def tr(self, group, ident, *after):
        return self.put([lambda e, g=g: e.transpose(g[0], g[1], ident) for g in group], after)


class Slots:

    def __init__(self, bufs):
        self.bufs, self.free, self.i = bufs, [[] for _ in bufs], 0

    def take(self):
        j = self.i % len(self.bufs)
        self.i += 1
        return j, self.bufs[j], self.free[j]

    def give(self, j, *toks):
        self.free[j] = list(toks)


class Arena:
    def __init__(self, tile, n):
        self.t, self.n, self.top = tile, n, 0

    def get(self, w, dt=None, **dims):
        a = self.t[:, self.top:self.top + w]
        self.top += w
        assert self.top <= self.n, (self.top, self.n)
        if dt is not None:
            a = a.bitcast(dt)
        if dims:
            names = " ".join(dims)
            a = a.rearrange(f"p ({names}) -> p {names}", **dims)
        return a


def bc(ap, n):
    return ap.unsqueeze(2).broadcast_to([128, ap.shape[1], n])


def bm(ap, n):
    return ap.unsqueeze(1).broadcast_to([128, n, ap.shape[1]])


def build(nc, T_, dbg=None, force_ovf=False):
    dram = {}

    def internal(name, shape, dt=F):
        return nc.dram_tensor(name, shape, dt, kind="Internal").ap()

    mods1 = internal("mods1", (3072,))
    mods2 = internal("mods2", (2, 6144))
    xd = internal("xd", (128, 4096))
    htd = internal("htd", (128, 4096))
    brd = internal("brd", (2, 128, 2048))
    fd = internal("fd", (S, D))
    idxd = internal("idxd", (128 * NB, 1), I32)
    yd = internal("yd", (128 * NB, D))
    ydv = yd.rearrange("(r b) d -> r b d", b=NB)
    out_d = T_["out"].rearrange("o (t p) d -> p (o t) d", p=128)

    ctx = ExitStack()
    with ctx:
        A_ = ctx.enter_context(nc.sbuf_tensor("arena", [128, NCOL], F))
        PSUM = ctx.enter_context(nc.psum_tensor("psum", [128, 8, 512], F))

        def sem(n):
            return ctx.enter_context(nc.semaphore(n))

        T = Lane(sem("s_pe"), False)
        V = Lane(sem("s_dve"), True)
        A = Lane(sem("s_act"), True)
        G = Lane(sem("s_pool"), True)
        Y = Lane(sem("s_sp"), False)
        main = dict(T=T, V=V, A=A, G=G, Y=Y)
        nsem = [0]

        def dsem():
            nsem[0] += 1
            return Dma(sem(f"d{nsem[0]}"))

        if dbg:
            dbg.lanes = [V, A, T]
        ar = Arena(A_, NCOL)
        banks = Slots([PSUM[:, i, :] for i in range(8)])
        pairs_of = PSUM

        class Stream:
            def __init__(self):
                self.slots = Slots([])
                self.d = []

            def grow(self, bufs, *toks):
                assert self.slots.i % max(1, len(self.slots.bufs)) == 0 or not self.slots.bufs
                for b in bufs:
                    self.slots.bufs.append(b)
                    self.slots.free.append(list(toks))
                    self.d.append(dsem())

            def load(self, src, lane=Y):
                j, buf, free = self.slots.take()
                tok = lane.dma(buf, src, self.d[j], *free)
                return j, buf, tok

            def give(self, j, *toks):
                self.slots.give(j, *toks)

        W = Stream()
        W.grow([ar.get(4096) for _ in range(3)])

        def chunk(i):
            return W.load(T_["w"][i])

        cst = ar.get(NCONST)
        par = ar.get(NPARAM)
        eps = ar.get(4)
        cs = ar.get(24, k=8, v=3)
        lamc = ar.get(1)
        iov = ar.get(8, I32)
        iovn = ar.get(1, I32)
        C = {n: cst[:, a:b] for n, (a, b) in CONSTS.items()}
        P = {n: par[:, a:b] for n, (a, b) in COLS.items()}
        ident, ones = C["ident"], C["ones"]

        d_c = dsem()
        t_par = A.dma(par, T_["params"], d_c)
        t_cst = A.dma(cst, T_["consts"], d_c)
        t_cst = (d_c.sem, d_c.n)

        t_eps = V.zero(eps[:, 0:1], value=EPS)
        V.zero(eps[:, 1:2], value=GN_EPS)
        t_eps = V.zero(eps[:, 2:3], value=0.0)

        mark0 = ar.top
        X = ar.get(4096, t=4, d=1024)
        HT = ar.get(4096, k=8, s=512)
        base = ar.top

        d_x = dsem()
        t_x = A.dma(X, T_["x"].rearrange("o (t p) d -> p (o t) d", p=128), d_x)

        r0 = ar.get(4096)
        sg = r0[:, 0:24]
        t = A.act(sg, par[:, 0:24], ACT.Sigmoid, t_cst)
        t_cs = V.tt(cs.rearrange("p k v -> p v k"), sg.rearrange("p (v k) -> p v k", v=3),
                    par[:, 0:24].rearrange("p (v k) -> p v k", v=3), ALU.mult, t, t_cst)

        bias = ar.get(512)
        d_b = dsem()
        t_bias = A.dma(bias[0:18, :], T_["bias"], d_b)
        mrow = Slots([ar.get(512) for _ in range(3)])
        d_m = [dsem() for _ in range(3)]
        t_m1, t_m2 = [], []

        def modulation(j, bank_ring):
            ws, wb, wt = chunk(j if j < 6 else 14 + j - 6)
            w = wb.rearrange("p (k n) -> p k n", k=8)
            M = 1 if j < 6 else 2
            bi, b, bf = bank_ring.take()
            sel = C["selp"][0:18, 2 * j:2 * j + M]
            g = [(b[0:M, :], sel, bias[0:18, :], True, False)]
            for k in range(8):
                lhs = cs[:, k, 0:1] if j < 6 else cs[:, k, 1:3]
                g.append((b[0:M, :], lhs, w[:, k, :], False, k == 7))
            for q in range(3):
                t = T.mm(g[3 * q:3 * q + 3], t_cs, t_bias, t_cst, wt, *bf)
                if q < 2:
                    yield
            W.give(ws, t)
            ri, row, rf = mrow.take()
            t = A.act(row[0:M, :], b[0:M, :], ACT.Copy, t, *rf)
            bank_ring.give(bi, t)
            if j < 6:
                dst = mods1[j * 512:(j + 1) * 512].unsqueeze(0)
            else:
                dst = mods2[:, (j - 6) * 512:(j - 5) * 512]
            t = G.dma(dst, row[0:M, :], d_m[ri], t)
            mrow.give(ri, t)
            (t_m1 if j < 6 else t_m2).append(t)
            yield

        for j in range(6):
            for _ in modulation(j, banks):
                pass

        d_mod = dsem()

        def mod_load(dst, which, i, after=()):
            if which == 1:
                src, toks = mods1[i * 1024:(i + 1) * 1024], t_m1
            else:
                src, toks = mods2[which - 2, i * 1024:(i + 1) * 1024], t_m2
            return G.dma(dst, src.partition_broadcast(128), d_mod, *toks, *after)

        d_row = dsem()

        def row_load(dst, name, after=()):
            return G.dma(dst, T_[name].partition_broadcast(128), d_row, *after)

        small = ar.get(64)

        def modulated(n_tiles, xt, t_in, gs, sh, t_gs, tiles, t_tiles, dest, sq, o=0):
            last = {}
            for i in range(n_tiles):
                c = [small[:, 12 * i + o + q:12 * i + o + q + 1] for q in range(3)]
                tx = t_in[i] if len(t_in) > 1 else t_in[0]
                t = A.act(sq, xt(i), ACT.Square, tx, *t_tiles, accum_out=c[0])
                t = A.act(c[1], c[0], ACT.Sqrt, t_eps, bias=eps[:, 0:1], scale=1.0 / D)
                V.rec(c[2], c[1], t)
                h = tiles[i % len(tiles)]
                V.stt(h, xt(i), c[2], gs, ALU.mult, ALU.mult, *t_gs, last.get(i - len(tiles)), tx)
                t = V.tt(h, h, sh, ALU.add)
                last[i] = dest(i, h, t)

        def transposed(dst, t_dst=()):
            def f(i, h, t):
                for half in range(2):
                    bi, b, bf = banks.take()
                    tt = T.tr([(b[:, q * 128:(q + 1) * 128], h[:, (4 * half + q) * 128:(4 * half + q + 1) * 128])
                               for q in range(4)], ident, t, t_cst, *bf)
                    o = dst[:, 4 * half:4 * half + 4, i * 128:(i + 1) * 128]
                    eng = V if half else A
                    src = b.rearrange("p (q s) -> p q s", q=4)
                    if half:
                        te = V.cp(o, src, tt, *t_dst)
                    else:
                        te = A.act(o, src, ACT.Copy, tt, *t_dst)
                    banks.give(bi, te)
                    f.done.append(te)
                return tt
            f.done = []
            return f

        r0b = ar.get(1024)
        gs1, sh1 = ar.get(1024), ar.get(1024)
        ht = [r0[:, 3072:4096], r0b]
        sqb = ar.get(1024)
        t1 = mod_load(gs1, 1, 1)
        t2 = mod_load(sh1, 1, 0)
        npre = sqb
        d_np = dsem()
        t3 = G.dma(npre, T_["norm_pre"].partition_broadcast(128), d_np)
        t_gs = V.stt(gs1, gs1, 1.0, npre, ALU.add, ALU.mult, t1, t2, t3)
        f1 = transposed(HT)
        modulated(4, lambda i: X[:, i, :], [t_x], gs1, sh1, [t_gs, t2], ht, [t_gs], f1, sqb)
        t_ht = f1.done
        ar.top = base + 4096 + 512 + 3 * 512 + 64 + 1024
        XA = ar.get(2064, m=4, s=516)
        XC = ar.get(2048, m=4, s=512)
        GA = ar.get(2048, m=4, s=512)
        QT = ar.get(2048, m=4, s=512)
        KT = ar.get(2048, m=4, s=512)
        VN = ar.get(2048, t=4, s=512)
        GB = ar.get(2048, t=4, s=512)
        tm = [ar.get(512) for _ in range(6)]
        LNC = ar.get(LNC_N)
        COS, SIN = ar.get(512), ar.get(512)
        d_l = dsem()
        wait_r = [V.last(), A.last(), T.last(), *t_m1]
        t_lnc = G.dma(LNC, T_["lnc"], d_l, *wait_r)
        posb = tm[0].bitcast(I32)
        d_p = dsem()
        t_pos = G.dma(posb, T_["positions"][0, :].partition_broadcast(128), d_p, *wait_r)
        ang, kk_, u_ = tm[1], tm[2], tm[3]
        V.cp(ang, posb, t_pos, *wait_r)
        V.ts(ang, ang, C["invf"], None, ALU.mult, None, t_cst)
        V.ts(kk_, ang, 1.0 / (2 * math.pi), 12582912.0, ALU.mult, ALU.add)
        V.ts(kk_, kk_, -12582912.0, None, ALU.add, None)
        c1 = 6.28125
        c2 = float(np.float32(int((2 * math.pi - c1) * 2 ** 17) / 2 ** 17))
        c3 = float(np.float32(2 * math.pi - c1 - c2))
        for c in (c1, c2, c3):
            V.stt(ang, kk_, -c, ang, ALU.mult, ALU.add)
        V.ts(ang, ang, math.pi, -math.pi, ALU.min, ALU.max)
        t = V.ts(u_, ang, -1.0, None, ALU.mult, None)
        t = V.tt(u_, u_, ang, ALU.max)
        t = V.ts(u_, u_, -1.0, math.pi / 2, ALU.mult, ALU.add)
        t_cos = A.act(COS, u_, ACT.Sin, t)
        t = A.act(SIN, ang, ACT.Sin, t)
        t_rope = V.ts(SIN, SIN, C["sgn"], None, ALU.mult, None, t, t_cos)

        def proj_t(ci, n_m, rhs, t_rhs, width, sink, used=512):
            ws, wb, wt = chunk(ci)
            w = wb.rearrange("p (k n) -> p k n", k=8)
            toks = []
            for m in range(n_m):
                bi, b, bf = banks.take()
                t = T.mm([(b[:, 0:width], w[:, k, m * 128:(m + 1) * 128], rhs(k), k == 0, k == 7) for k in range(8)],
                         wt, *t_rhs, *bf)
                if m == n_m - 1:
                    W.give(ws, t)
                banks.give(bi, *sink(m, b[:, 0:width], t))

        def proj_n(ci, tiles, sink, t_in):
            ws, wb, wt = chunk(ci)
            w = wb.rearrange("p (k n) -> p k n", k=8)
            for i, lhs in enumerate(tiles):
                bi, b, bf = banks.take()
                t = T.mm([(b, lhs(k), w[:, k, :], k == 0, k == 7) for k in range(8)], wt, *t_in, *bf)
                if i == len(tiles) - 1:
                    W.give(ws, t)
                banks.give(bi, *sink(i, b, t))

        hr = lambda k: HT[:, k, :]
        t_pad = V.zero(XA[:, :, 0:4])
        toks = {}

        def sink_xa(m, b, t):
            toks["xa", m] = A.act(XA[:, m, 4:516], b, ACT.Copy, t, *wait_r)
            return [toks["xa", m]]

        proj_t(6, 4, hr, t_ht, 512, sink_xa)

        def sink_ga(m, b, t):
            t = A.act(GA[:, m, :], b, ACT.Sigmoid, t, *wait_r)
            toks["ga", m] = V.tt(GA[:, m, :], GA[:, m, :], b, ALU.mult, t)
            return [toks["ga", m]]

        proj_t(7, 4, hr, t_ht, 512, sink_ga)

        def rope(m, b, t, cosb, sinb, perm, dst, raw, tmp, t_tab):
            n = dst.shape[1]
            t = V.cp(raw[:, 0:n], b, t, T.last())
            bi, b2, bf = banks.take()
            tp = T.mm([(b2[:, 0:n], perm, raw[:, 0:n], True, True)], t, t_cst, *bf)
            V.tt(dst, raw[:, 0:n], cosb, ALU.mult, *t_tab)
            t2 = V.tt(tmp[:, 0:n], b2[:, 0:n], sinb, ALU.mult, tp)
            banks.give(bi, t2)
            return t, V.tt(dst, dst, tmp[:, 0:n], ALU.add)

        def sink_rope(name, dst):
            def f(m, b, t):
                t1, t2 = rope(m, b, t, COS, SIN, C["perm1"], dst[:, m, :], tm[m % 2], tm[2], [t_rope])
                toks[name, m] = t2
                return [t1]
            return f

        proj_t(8, 4, hr, t_ht, 512, sink_rope("q", QT))
        proj_t(9, 4, hr, t_ht, 512, sink_rope("k", KT))
        tl = [lambda k, i=i: HT[:, k, i * 128:(i + 1) * 128] for i in range(4)]

        def sink_v(i, b, t):
            toks["v", i] = A.act(VN[:, i, :], b, ACT.Copy, t, *wait_r)
            return [toks["v", i]]

        proj_n(10, tl, sink_v, t_ht)

        def sink_gb(i, b, t):
            t = A.act(GB[:, i, :], b, ACT.Sigmoid, t, *wait_r)
            toks["gb", i] = V.tt(GB[:, i, :], GB[:, i, :], b, ALU.mult, t)
            return [toks["gb", i]]

        proj_n(11, tl, sink_gb, t_ht)

        lws = ar.get(32)
        lw = [lws[:, 4 * i:4 * i + 4] for i in range(8)]
        lam = P["lam"]
        V.ts(lw[0], lam, -1.0, None, ALU.mult, None)
        t = V.tt(lw[1], lam, lw[0], ALU.min)
        t = A.act(lw[2], lw[1], ACT.Exp, t)
        V.ts(lw[3], lw[2], 2.0, None, ALU.add, None, t)
        V.rec(lw[3], lw[3])
        V.tt(lw[2], lw[2], lw[3], ALU.mult)
        V.tt(lw[4], lw[2], lw[2], ALU.mult)
        V.zero(lw[5], value=1.0 / 19)
        for n in range(8, -1, -1):
            V.tt(lw[5], lw[5], lw[4], ALU.mult)
            V.ts(lw[5], lw[5], 1.0 / (2 * n + 1), None, ALU.add, None)
        V.stt(lw[5], lw[5], 2.0, lw[2], ALU.mult, ALU.mult)
        V.stt(lw[5], lw[0], 0.0, lw[5], ALU.max, ALU.add)
        t_sp = V.ts(lw[6], lw[5], 8.0, None, ALU.mult, None)
        t_spn = V.ts(lw[7], lw[5], -8.0, None, ALU.mult, None)
        wbd = r0[:, 0:1024]
        d_w = dsem()
        t_wbd = G.dma(wbd, T_["w_rg"], d_w, *wait_r)
        ada2 = (y for j in range(6, 18) for y in modulation(j, mbank))
        mbank = Slots([banks.bufs[7]])
        mbank.give(0, T.last(), V.last(), A.last())
        lbanks = Slots(banks.bufs[0:7])
        for j in range(7):
            lbanks.give(j, T.last(), V.last(), A.last())
        cw = P["conv_w"]
        for m in range(4):
            xc = XC[:, m, :]
            V.ts(xc, XA[:, m, 1:513], cw[:, m:m + 1], P["conv_b"][:, m:m + 1], ALU.mult, ALU.add, toks["xa", m])
            for k in range(1, 4):
                t_xc = V.stt(xc, XA[:, m, 1 + k:513 + k], cw[:, 4 * k + m:4 * k + m + 1], xc, ALU.mult, ALU.add)
            gates = []
            for j, (bn, tmp) in enumerate((("b_a", tm[0]), ("b_x", tm[1]))):
                bi, b, bf = lbanks.take()
                t = T.mm([(b, wbd[:, (4 * j + m) * 128:(4 * j + m + 1) * 128], xc, True, True)], t_xc, t_wbd, *bf)
                t = A.act(tmp, b, ACT.Sigmoid, t, V.last(), bias=P[bn][:, m:m + 1])
                lbanks.give(bi, t)
            ta = A.act(tm[2], tm[0], ACT.Exp, t_spn, scale=lw[7][:, m:m + 1])
            t_th = A.act(tm[3], tm[0], ACT.Tanh, t_sp, scale=lw[6][:, m:m + 1])
            V.ts(tm[4], tm[3], 1.0, None, ALU.add, None, t_th)
            V.rec(tm[4], tm[4])
            t = V.stt(tm[3], tm[3], 2.0, tm[4], ALU.mult, ALU.mult)
            t = A.act(tm[3], tm[3], ACT.Sqrt, t)
            V.tt(tm[1], tm[1], xc, ALU.mult)
            V.tt(tm[1], tm[1], tm[3], ALU.mult, t)
            V.scan(tm[4], tm[2], tm[1], ta)
            t = V.tt(xc, tm[4], GA[:, m, :], ALU.mult, T.last())
            toks["ya", m] = t
            for _ in range(3):
                next(ada2, None)
        bi, b, bf = lbanks.take()
        for m in range(4):
            t = A.act(tm[m % 2], XC[:, m, :], ACT.Square, toks["ya", 3], T.last())
            t = T.mm([(b, ones, tm[m % 2], m == 0, m == 3)], t, *bf)
        t = A.act(tm[2], b, ACT.Sqrt, t, bias=eps[:, 0:1], scale=1.0 / 512)
        lbanks.give(bi, t)
        t = V.rec(tm[2], tm[2], t)
        t_ya = None
        for m in range(4):
            t_ya = V.stt(XC[:, m, :], XC[:, m, :], P["norm_rec"][:, m:m + 1], tm[2], ALU.mult, ALU.mult)

        sl = [r0[:, 512 * i:512 * (i + 1)] for i in range(8)]
        Sb, Pb, PTb, YB = sl[0:2], [sl[2], sl[3], tm[3]], sl[4:6], sl[6:8]
        free_r0 = [T.last(), A.last()]
        YBT = XA.rearrange("p m s -> p (m s)")[:, 0:2048].rearrange("p (m s) -> p m s", m=4)
        nbb = ar.get(512)
        d_na = dsem()
        t_na = G.dma(nbb, T_["norm_att"].partition_broadcast(128), d_na)
        st = ar.get(64)
        ab_free = [T.last(), V.last(), A.last()]
        abanks, obanks = Slots(banks.bufs[0:5]), Slots(banks.bufs[5:7])
        for j in range(5):
            abanks.give(j, *ab_free)
        for j in range(2):
            obanks.give(j, *ab_free)
        it = [(i, h) for i in range(4) for h in range(8)]
        tS, tP, tPT = {}, {}, {}
        obank = {}
        q_all = [toks["q", m] for m in range(4)] + [toks["k", m] for m in range(4)] + [toks["v", i] for i in range(4)]

        def scores(x):
            i, h = it[x]
            n = 128 * (i + 1)
            hb, m = 64 * (h % 2), h // 2
            bi, b, bf = abanks.take()
            t = T.mm([(b[:, 0:n], QT[hb:hb + 64, m, i * 128:(i + 1) * 128], KT[hb:hb + 64, m, 0:n], True, True)],
                     *q_all, *bf)
            s, p = Sb[x % 2], Pb[x % 3]
            o = LNC_OFF[i]
            t = V.stt(s[:, 0:n], b[:, 0:n], 0.125, LNC[:, o:o + n], ALU.mult, ALU.add, t, t_lnc, tP.get(x - 2), *free_r0)
            abanks.give(bi, t)
            t = V.red(st[:, x % 2:x % 2 + 1], s[:, 0:n], ALU.max, negate=True)
            tP[x] = A.act(p[:, 0:n], s[:, 0:n], ACT.Exp, t, tPT.get(x - 3), bias=st[:, x % 2:x % 2 + 1],
                          accum_out=st[:, 8 + 8 * (i % 2) + h:9 + 8 * (i % 2) + h])

        def turn(x):
            i, h = it[x]
            n = 128 * (i + 1)
            bi, b, bf = abanks.take()
            t = T.tr([(b[:, j * 128:(j + 1) * 128], Pb[x % 3][:, j * 128:(j + 1) * 128]) for j in range(i + 1)],
                     ident, tP[x], *bf)
            tPT[x] = t
            tS[x] = A.act(PTb[x % 2][:, 0:n], b[:, 0:n], ACT.Copy, t, obank.get(("pv", x - 2)))
            abanks.give(bi, tS[x])

        def pv(x):
            i, h = it[x]
            if h == 0:
                obank[i] = obanks.take()
            bi, b, bf = obank[i]
            t = T.mm([(b[:, h * 64:(h + 1) * 64], PTb[x % 2][:, j * 128:(j + 1) * 128], VN[:, j, h * 64:(h + 1) * 64],
                       j == 0, j == i) for j in range(i + 1)], tS[x], *bf)
            obank["pv", x] = t
            if h == 7:
                ri = st[:, 24 + 8 * (i % 2):32 + 8 * (i % 2)]
                V.rec(ri, st[:, 8 + 8 * (i % 2):16 + 8 * (i % 2)], tP[x])
                y = YB[i % 2]
                t = V.tt(y.rearrange("p (h d) -> p h d", h=8), b.rearrange("p (h d) -> p h d", h=8), bc(ri, 64),
                         ALU.mult, t, obank.get(("yt", i - 2)))
                obanks.give(bi, t)
                t = V.tt(y, y, GB[:, i, :], ALU.mult)
                t = A.act(tm[0], y, ACT.Square, t, V.last(), accum_out=st[:, 40 + i:41 + i])
                t = A.act(st[:, 44 + i:45 + i], st[:, 40 + i:41 + i], ACT.Sqrt, bias=eps[:, 0:1], scale=1.0 / 512)
                t = V.rec(st[:, 48 + i:49 + i], st[:, 44 + i:45 + i], t)
                t = V.stt(y, y, st[:, 48 + i:49 + i], nbb, ALU.mult, ALU.mult, t_na)
                b2i, b2, b2f = abanks.take()
                t = T.tr([(b2[:, q * 128:(q + 1) * 128], y[:, q * 128:(q + 1) * 128]) for q in range(4)], ident, t, *b2f)
                obank["yt", i] = t
                t = V.cp(YBT[:, :, i * 128:(i + 1) * 128], b2.rearrange("p (q s) -> p q s", q=4), t)
                obank["y", i] = t
                abanks.give(b2i, t)

        for x in range(len(it) + 3):
            if x < len(it):
                scores(x)
            if 0 <= x - 2 < len(it):
                turn(x - 2)
            next(ada2, None)
            if 0 <= x - 3 < len(it):
                pv(x - 3)
        for _ in ada2:
            pass

        for j in range(8):
            banks.give(j, T.last(), V.last(), A.last())

        gp1 = tm[2]
        wo = [chunk(12), chunk(13)]
        G1 = r0[:, 0:1024]
        w_r0 = [T.last(), V.last(), A.last()]
        d_g1 = dsem()
        t1 = G.dma(G1, mods1[2048:3072].partition_broadcast(128), d_g1, *t_m1, *w_r0)
        d_np2 = dsem()
        np_ = r0[:, 1024:2048]
        t2 = G.dma(np_, T_["norm_post"].partition_broadcast(128), d_np2, *w_r0)
        t_gp = V.tt(G1, G1, np_, ALU.mult, t1, t2)
        msb = [r0[:, 2048:3072], r0[:, 3072:4096]]
        y_all = [obank["y", i] for i in range(4)] + [t_ya]
        t_x1 = []
        for i in range(4):
            bb = []
            for hf in range(2):
                ws, wb, wt = wo[hf]
                w = wb.rearrange("p (k n) -> p k n", k=8)
                bi, b, bf = banks.take()
                g = []
                for k in range(8):
                    lhs = (XC if k < 4 else YBT)[:, k % 4, i * 128:(i + 1) * 128]
                    g.append((b, lhs, w[:, k, :], k == 0, k == 7))
                t = T.mm(g, wt, *y_all, *bf)
                if i == 3:
                    W.give(ws, t)
                bb.append((bi, b, t))
            mx = msb[i % 2]
            for hf in range(2):
                bi, b, t = bb[hf]
                t = V.cp(mx[:, hf * 512:(hf + 1) * 512], b, t, *w_r0)
                banks.give(bi, t)
            t = A.act(np_, mx, ACT.Square, t, t_gp, accum_out=st[:, 40 + i:41 + i])
            t = A.act(st[:, 44 + i:45 + i], st[:, 40 + i:41 + i], ACT.Sqrt, bias=eps[:, 0:1], scale=1.0 / D)
            V.rec(st[:, 48 + i:49 + i], st[:, 44 + i:45 + i], t)
            V.stt(mx, mx, st[:, 48 + i:49 + i], G1, ALU.mult, ALU.mult)
            t_x1.append(V.tt(X[:, i, :], X[:, i, :], mx, ALU.add))

        def fence():
            return [T.last(), V.last(), A.last(), G.last()]

        ar.top = base
        fb1 = fence() + t_m2
        if dbg:
            dbg("x1", X, V, G, dsem)
        HCT = ar.get(2048, k=8, s=256)
        small = ar.get(64)
        mark2 = ar.top
        gs, sh, gsc, shc = [ar.get(1024) for _ in range(4)]
        ht = [ar.get(1024), ar.get(1024)]
        sqb, n1 = ar.get(1024), ar.get(1024)
        CX = ar.get(2048, t=2, d=1024)
        d_n1 = dsem()
        t_l = [mod_load(gs, 2, 1, fb1), mod_load(sh, 2, 0, fb1), mod_load(gsc, 3, 1, fb1), mod_load(shc, 3, 0, fb1),
               G.dma(n1, T_["norm1_g_2"].partition_broadcast(128), d_n1, *fb1),
               G.dma(CX, T_["ctx_2"].rearrange("o (t p) d -> p (o t) d", p=128), d_n1, *fb1)]
        V.stt(gs, gs, 1.0, n1, ALU.add, ALU.mult, *t_l, *fb1)
        t_gs = V.stt(gsc, gsc, 1.0, n1, ALU.add, ALU.mult)
        f2 = transposed(HCT, fb1)
        modulated(2, lambda i: CX[:, i, :], [t_l[5]], gsc, shc, [t_gs], ht, fb1, f2, sqb)
        f3 = transposed(HT, fb1)
        modulated(4, lambda i: X[:, i, :], t_x1, gs, sh, [t_gs], ht, fb1, f3, sqb)
        t_h2 = f2.done + f3.done
        d_sp = dsem()
        G.dma(xd, X.rearrange("p t d -> p (t d)"), d_sp, *t_x1)
        t_xd = G.dma(htd, HT.rearrange("p k s -> p (k s)"), d_sp, *t_h2)
        ar.top = mark2
        f = fence()

        TB = ar.get(NROPE)
        d_tb = dsem()
        t_tb = G.dma(TB, T_["ropes"], d_tb, *f)
        RP = {n: TB[:, a:b] for n, (a, b) in ROPES.items()}
        PW = ar.get(512, g=4, d=128)
        t_tb = G.dma(PW, T_["pool_w_2"][0].rearrange("g c d -> c g d"), d_tb, *f)
        lqb = ar.get(256)
        t_tb = G.dma(lqb, T_["lambda_qk_2"][0].rearrange("a b -> (a b)").partition_broadcast(128), d_tb, *f)
        SUB = ar.get(512)
        t_tb = G.dma(SUB, T_["subln"].partition_broadcast(128), d_tb, *f)
        V.tt(lqb[:, 0:64], lqb[:, 0:64], lqb[:, 64:128], ALU.mult, t_tb)
        V.tt(lqb[:, 128:192], lqb[:, 128:192], lqb[:, 192:256], ALU.mult)
        V.red(small[:, 40:41], lqb[:, 0:64], ALU.add)
        t = V.red(small[:, 41:42], lqb[:, 128:192], ALU.add)
        t = A.act(small[:, 42:44], small[:, 40:42], ACT.Exp, t)
        V.tt(lamc, small[:, 42:43], small[:, 43:44], ALU.subtract, t)
        V.ts(lamc, lamc, 0.8 - 0.6 * math.exp(0.0), None, ALU.add, None)

        mark3 = ar.top
        PP = ar.get(4 * 528, m=4, s=528)
        pt = [ar.get(528) for _ in range(2)]
        B0 = ar.get(2048, m=4, s=512)
        t_z = V.zero(PP, *f)
        hl = lambda k: HT[:, k, :]
        hc = lambda k: HCT[:, k, :]
        t_b0 = []

        def sink_pool(m, b, t):
            w = 2 << m
            u = PP[:, m, :]
            tA = A.act(u[:, 8:520], b, ACT.Copy, t, t_z)
            src, step = u, 1
            n = 528
            j = 0
            while step < w:
                dst = pt[j % 2]
                n2 = n - step
                V.tt(dst[:, 0:n2], src[:, 0:n2], src[:, step:step + n2], ALU.add, tA)
                src, n, step, j = dst, n2, step * 2, j + 1
            o = 8 - w // 2
            dst = pt[j % 2]
            V.tt(dst[:, 0:512], src[:, o:o + 512], RP["cnt"][:, m * 512:(m + 1) * 512], ALU.mult, t_tb)
            t = V.tt(dst[:, 0:512], dst[:, 0:512], u[:, 8:520], ALU.subtract)
            bi, b2, bf = banks.take()
            t = T.mm([(b2, PW[:, m, :], dst[:, 0:512], True, True)], t, t_tb, *bf)
            t = V.ts(B0[:, m, :], b2, P["pscale"][:, m:m + 1], None, ALU.mult, None, t)
            banks.give(bi, t)
            t_b0.append(t)
            return [tA]

        proj_t(26, 4, hl, t_h2, 512, sink_pool)
        d_br = dsem()
        t_brd = G.dma(brd[0], B0.rearrange("p m s -> p (m s)"), d_br, *t_b0)

        if dbg:
            dbg("b0", B0, V, G, dsem)

        ar.top = mark3 + 4 * 528 + 2 * 528 + 2048
        QT = ar.get(2048, m=4, s=512)
        KT = ar.get(4 * 768, m=4, s=768)
        VN = ar.get(6 * 512, t=6, s=512)
        tm = [ar.get(512) for _ in range(4)]
        toks = {}

        def qk_norm(b, t, n, g, raw, sq):
            t1 = A.act(sq[:, 0:n], b, ACT.Square, t, *f, V.last(), T.last())
            bi, b2, bf = banks.take()
            t2 = T.mm([(b2[:, 0:n], C["blk64"], sq[:, 0:n], True, True)], t1, *bf)
            t3 = A.act(sq[:, 0:n], b2[:, 0:n], ACT.Sqrt, t2, bias=eps[:, 0:1], scale=1.0 / 64)
            banks.give(bi, t3)
            V.rec(sq[:, 0:n], sq[:, 0:n], t3)
            return V.stt(raw, b, g, sq[:, 0:n], ALU.mult, ALU.mult, t, T.last(), *f)

        def sink_qk(name, dst, col, off):
            def fn(m, b, t):
                n1_, n2_ = tm[2 * (m % 2)], tm[2 * (m % 2) + 1]
                t0 = qk_norm(b, t, 512, col, n1_, n2_)
                bi, b2, bf = banks.take()
                tp = T.mm([(b2, C["perm2"], n1_, True, True)], t0, *bf)
                o = dst[:, m, off:off + 512]
                V.tt(o, n1_, RP["cos2"], ALU.mult, t_tb)
                t2 = V.tt(n2_, b2, RP["sin2"], ALU.mult, tp)
                banks.give(bi, t2)
                toks[name, m] = V.tt(o, o, n2_, ALU.add)
                return [t0]
            return fn

        proj_t(27, 4, hl, t_h2, 512, sink_qk("q", QT, P["qn"], 0))
        ws, wb, wt = chunk(28)
        w = wb.rearrange("p (k n) -> p k n", k=8)
        sk = sink_qk("k", KT, P["kn"], 256)
        for m in range(4):
            bi, b, bf = banks.take()
            t = T.mm([(b[:, 0:256], w[:, k, m * 128:(m + 1) * 128], hc(k), k == 0, k == 7) for k in range(8)], wt, *t_h2, *bf)
            t = qk_norm(b[:, 0:256], t, 256, P["kn"], KT[:, m, 0:256], tm[2 * (m % 2)])
            toks["kc", m] = t
            banks.give(bi, t)
            bi, b, bf = banks.take()
            t = T.mm([(b, w[:, k, m * 128:(m + 1) * 128], hl(k), k == 0, k == 7) for k in range(8)], *bf)
            if m == 3:
                W.give(ws, t)
            banks.give(bi, *sk(m, b, t))
        tl6 = [lambda k, i=i: HCT[:, k, i * 128:(i + 1) * 128] for i in range(2)] + \
              [lambda k, i=i: HT[:, k, i * 128:(i + 1) * 128] for i in range(4)]

        def sink_v2(i, b, t):
            toks["v", i] = A.act(VN[:, i, :], b, ACT.Copy, t, *f)
            return [toks["v", i]]

        proj_n(29, tl6, sink_v2, t_h2)
        ar2 = ar.top
        ar.top = mark3
        f4 = fence() + [t_brd] + (dbg.toks if dbg else [])
        Pm = [[ar.get(768) for _ in range(2)] for _ in range(2)]
        AT = [ar.get(768) for _ in range(2)]
        ATN = [tm[0], tm[1]]
        assert ar.top <= mark3 + 4 * 528 + 2 * 528 + 2048
        ar.top = ar2
        B1 = ar.get(2048, m=4, s=512)
        st = ar.get(64)
        it = [(i, h) for i in range(4) for h in range(4)]
        spair = Slots([PSUM[:, 0:2, :].rearrange("p a b -> p (a b)"), PSUM[:, 2:4, :].rearrange("p a b -> p (a b)")])
        tpair = Slots([PSUM[:, 4:6, :].rearrange("p a b -> p (a b)")])
        for s_ in (spair, tpair):
            for j in range(len(s_.bufs)):
                s_.give(j, *f4)
        fp = f4
        qkv = list(toks.values())
        tA, tTR, tAT, tPV = {}, {}, {}, {}

        def d_scores(x):
            i, h = it[x]
            o = 4 * (x % 2)
            for mp in range(2):
                bi, b, bf = spair.take()
                lhs = QT[64 * mp:64 * mp + 64, h, i * 128:(i + 1) * 128]
                t = T.mm([(b[:, 0:512], lhs, KT[64 * mp:64 * mp + 64, h, 0:512], True, True),
                          (b[:, 512:768], lhs, KT[64 * mp:64 * mp + 64, h, 512:768], True, True)], *qkv, *bf)
                V.red(st[:, o + mp:o + mp + 1], b[:, 0:768], ALU.max, t, A.last())
                t = V.ts(st[:, o + mp:o + mp + 1], st[:, o + mp:o + mp + 1], -0.125, None, ALU.mult, None)
                t = A.act(Pm[x % 2][mp], b[:, 0:768], ACT.Exp, t, *fp, tTR.get(x - 2), bias=st[:, o + mp:o + mp + 1],
                          scale=0.125, accum_out=st[:, 8 + o + mp:9 + o + mp])
                spair.give(bi, t)
            rc = st[:, 16 + o:18 + o]
            V.rec(rc, st[:, 8 + o:10 + o], t)
            V.tt(rc[:, 1:2], rc[:, 1:2], lamc, ALU.mult)
            V.ts(Pm[x % 2][1], Pm[x % 2][1], rc[:, 1:2], None, ALU.mult, None)
            tA[x] = V.stt(Pm[x % 2][0], Pm[x % 2][0], rc[:, 0:1], Pm[x % 2][1], ALU.mult, ALU.subtract)

        def d_turn(x):
            bi, b, bf = tpair.take()
            t = T.tr([(b[:, j * 128:(j + 1) * 128], Pm[x % 2][0][:, j * 128:(j + 1) * 128]) for j in range(6)], ident, tA[x], *bf)
            tTR[x] = t
            tAT[x] = A.act(AT[x % 2], b[:, 0:768], ACT.Copy, t, *fp, tPV.get(x - 2))
            tpair.give(bi, tAT[x])

        ob = Slots([PSUM[:, 6, :]])
        tb = Slots([PSUM[:, 7, :]])
        ob.give(0, *f4)
        tb.give(0, *f4)
        t_b1 = []
        hold = {}

        def d_pv(x):
            i, h = it[x]
            if h == 0:
                hold["o"] = ob.take()
            bi, b, bf = hold["o"]
            tPV[x] = t = T.mm([(b[:, h * 128:(h + 1) * 128], AT[x % 2][:, j * 128:(j + 1) * 128],
                                VN[:, j, h * 128:(h + 1) * 128], j == 0, j == 5) for j in range(6)], tAT[x], *bf)
            if h == 3:
                y, sq = ATN[i % 2], tm[2]
                t = V.cp(y, b, t, hold.get(i - 2))
                ob.give(0, t)
                t = V.tt(sq, y, y, ALU.mult)
                t = V.red(st[:, 32:36], sq.rearrange("p (h d) -> p h d", h=4), ALU.add)
                t = A.act(st[:, 36:40], st[:, 32:36], ACT.Sqrt, t, bias=eps[:, 0:1], scale=1.0 / 128)
                V.rec(st[:, 40:44], st[:, 36:40], t)
                V.tt(y.rearrange("p (h d) -> p h d", h=4), y.rearrange("p (h d) -> p h d", h=4), bc(st[:, 40:44], 128), ALU.mult)
                t = V.stt(y, y, 1.0 - (0.8 - 0.6 * math.exp(0.0)), SUB, ALU.mult, ALU.mult)
                b2i, b2, b2f = tb.take()
                t = T.tr([(b2[:, q * 128:(q + 1) * 128], y[:, q * 128:(q + 1) * 128]) for q in range(4)], ident, t, *b2f)
                hold[i] = t
                t = V.cp(B1[:, :, i * 128:(i + 1) * 128], b2.rearrange("p (q s) -> p q s", q=4), t)
                tb.give(0, t)
                t_b1.append(t)

        for x in range(len(it) + 2):
            if x < len(it):
                d_scores(x)
            if 0 <= x - 1 < len(it):
                d_turn(x - 1)
            if 0 <= x - 2 < len(it):
                d_pv(x - 2)
        t_brd = G.dma(brd[1], B1.rearrange("p m s -> p (m s)"), d_br, *t_b1)
        if dbg:
            dbg("b1", B1, V, G, dsem)

        f = fence() + [t_brd, t_xd]
        if dbg:
            f = f + dbg.toks
        for j in range(8):
            banks.give(j, *f)
        ar.top = mark2
        R = ar.get(2048, m=4, s=512)
        K = ar.get(3072, m=4, s=768)
        VR = ar.get(3072, t=6, s=512)
        WL, AL = ar.get(768), ar.get(768)
        SG = ar.get(512)
        KK = ar.get(3072, m=4, s=768)
        YS = ar.get(2048, t=4, s=512)
        W2, A2, G2 = ar.get(512), ar.get(512), ar.get(512)
        MK = ar.get(NMASK)
        IRK = ar.get(32, m=4, h=8)
        COEF = ar.get(32, t=4, h=8)
        MM = {n: MK[:, a:b] for n, (a, b) in MASKS.items()}
        d_rw = dsem()
        for dst, n in ((W2, "decay_w2"), (A2, "aaa_a2"), (G2, "gate_w2"), (MK, "masks")):
            t_rw = G.dma(dst, T_[n], d_rw, *f)
        V.tt(IRK, C["ind"].rearrange("p (m h) -> p m h", m=4), bc(P["r_k"], 8), ALU.mult, *f)
        mark4 = ar.top
        PR = [ar.get(772) for _ in range(2)]
        vt = [ar.get(768) for _ in range(2)]
        m01 = ar.get(16)
        t_pz = None
        for z in PR:
            t_pz = V.zero(z, *f)
        V.tt(m01[:, 0:15], P["mu0"], P["mu1"], ALU.add)
        V.ts(m01[:, 0:15], m01[:, 0:15], -1.0, 1.0, ALU.mult, ALU.add)
        shifted = {}
        rd = [None, None]
        ti = 0
        for ci, n_m, f0 in ((30, 4, 0), (31, 4, 4), (32, 4, 8), (33, 3, 12)):
            ws, wb, wt = chunk(ci)
            w = wb.rearrange("p (k n) -> p k n", k=8)
            for m in range(n_m):
                fi = f0 + m
                pr = PR[ti % 2]
                has_c = fi not in (0, 1, 2, 3, 14)
                tc = None
                if has_c:
                    bi, b, bf = banks.take()
                    t = T.mm([(b[:, 0:256], w[:, k, m * 128:(m + 1) * 128], hc(k), k == 0, k == 7) for k in range(8)], wt, *bf)
                    tc = A.act(pr[:, 1:257], b[:, 0:256], ACT.Copy, t, t_pz, rd[ti % 2])
                    banks.give(bi, tc)
                bi, b, bf = banks.take()
                t = T.mm([(b, w[:, k, m * 128:(m + 1) * 128], hl(k), k == 0, k == 7) for k in range(8)], wt, *bf)
                if m == n_m - 1:
                    W.give(ws, t)
                tl_ = A.act(pr[:, 258:770], b, ACT.Copy, t, t_pz, rd[ti % 2])
                banks.give(bi, tl_)
                if fi < 4:
                    dl, dc = R[:, fi, :], None
                elif fi < 8:
                    dl, dc = K[:, fi - 4, 256:768], K[:, fi - 4, 0:256]
                elif fi < 12:
                    v_ = vt[ti % 2]
                    dl, dc = v_[:, 256:768], v_[:, 0:256]
                elif fi < 14:
                    q_ = (WL, AL)[fi - 12]
                    dl, dc = q_[:, 256:768], q_[:, 0:256]
                else:
                    dl, dc = SG, None
                wv = shifted.get("vt%d" % (ti % 2)) if 8 <= fi < 12 else None
                for dst, o, n in ((dl, 258, 512), (dc, 1, 256)):
                    if dst is None:
                        continue
                    V.ts(dst, pr[:, o:o + n], m01[:, fi:fi + 1], None, ALU.mult, None, tl_, tc, wv)
                    V.stt(dst, pr[:, o - 1:o - 1 + n], P["mu0"][:, fi:fi + 1], dst, ALU.mult, ALU.add)
                    t = V.stt(dst, pr[:, o + 1:o + 1 + n], P["mu1"][:, fi:fi + 1], dst, ALU.mult, ALU.add)
                rd[ti % 2] = t
                if 8 <= fi < 12:
                    for hf in range(2):
                        nb_ = 4 if hf == 0 else 2
                        bi, b, bf = banks.take()
                        t2 = T.tr([(b[:, q * 128:(q + 1) * 128], v_[:, (4 * hf + q) * 128:(4 * hf + q + 1) * 128])
                                   for q in range(nb_)], ident, t, *bf)
                        t3 = A.act(VR[:, 4 * hf:4 * hf + nb_, (fi - 8) * 128:(fi - 7) * 128],
                                   b[:, 0:nb_ * 128].rearrange("p (q s) -> p q s", q=nb_), ACT.Copy, t2, *f)
                        banks.give(bi, t3)
                        shifted["vt%d" % (ti % 2)] = t2
                        shifted["vr", fi, hf] = t3
                ti += 1
        t = V.last()
        t_wl = A.act(WL, WL, ACT.Tanh, t)
        t_sg = A.act(SG, SG, ACT.Sigmoid, t)
        t_vr = [v for k_, v in shifted.items() if isinstance(k_, tuple)]
        ar.top = mark4
        f5 = fence()
        tmp = [ar.get(512, m=4, s=128) for _ in range(5)]
        fl = [x_.rearrange("p m s -> p (m s)") for x_ in tmp]
        for c in range(6):
            kc = KK[:, :, c * 128:(c + 1) * 128]
            V.tt(kc, K[:, :, c * 128:(c + 1) * 128], bc(P["k_k"], 128), ALU.mult, *f5)
            q_ = tmp[c % 2]
            t = V.tt(q_, kc, kc, ALU.mult, T.last())
            bi, b, bf = banks.take()
            t = T.mm([(b, C["blk64"], fl[c % 2], True, True)], t, *bf)
            t = A.act(fl[2 + c % 2], b, ACT.Sqrt, t, V.last(), bias=eps[:, 2:3])
            banks.give(bi, t)
            V.ts(fl[2 + c % 2], fl[2 + c % 2], 1e-12, None, ALU.max, None, t)
            V.rec(fl[2 + c % 2], fl[2 + c % 2])
            V.tt(kc, kc, tmp[2 + c % 2], ALU.mult)

        low, ring_mem = Arena(A_, base + 2048), Arena(A_, len(W.slots.bufs) * 4096)
        low.top = mark0

        def place(first, w, **dims):
            for r in (first, ar):
                if r.top + w <= r.n:
                    return r.get(w, **dims)
            raise AssertionError("no room")

        f6 = fence() + t_vr + [t_wl, t_sg, t_rw]
        opened = set()
        ends_of = {}

        def accumulate(key, dst, b, t):
            if key in opened:
                return V.tt(dst, dst, b, ALU.add, t)
            opened.add(key)
            return V.cp(dst, b, t)

        def recurrence(d, region, ring):
            g_ = lambda w, **dims: place(region, w, **dims)
            GBm, GKm = g_(2048, h=8, n=256), g_(2048, h=8, n=256)
            AR = g_(1024, m=4, j=2, s=128)
            KB = g_(1024, j=2, m=4, s=128)
            KNB = g_(1024, j=2, n=512)
            TI, TT, NL, XB = [g_(1024, h=8, n=128) for _ in range(4)]
            tmp = [g_(512, m=4, s=128) for _ in range(5)]
            MS, MP = [g_(512, m=4, v=128) for _ in range(2)]
            X0, SA = g_(512), g_(512)
            DD = ar.get(4)
            sig, ag, L, ex, e2 = tmp
            t_z = [G.zero(GBm, *f6), G.zero(GKm), V.zero(MS, *f6)]
            tri_i = MM["si%d" % d].bitcast(U32)
            lmT = lambda lv: bm(MM["lm%d" % (1 - d)][:, lv * 128:(lv + 1) * 128], 4)
            order = ([0, 1, 2, 3, 4, 5], [1, 0, 5, 4, 3, 2])[d]
            pe_prev, v_prep, t_co = None, None, None
            for c in order:
                lat = c >= 2
                cs_ = slice(c * 128, (c + 1) * 128)
                ls = slice((c - 2) * 128, (c - 1) * 128)
                for dst, wgt, lo, b0 in ((sig, W2, WL, "w0"), (ag, A2, AL, "a0")):
                    bi, b, bf = ring.take()
                    t = T.mm([(b[:, m * 128:(m + 1) * 128], wgt[64 * d:64 * d + 64, m * 128:(m + 1) * 128],
                               lo[64 * d:64 * d + 64, cs_], True, True) for m in range(4)], *f6, *bf)
                    for m in range(4):
                        t = A.act(dst[:, m, :], b[:, m * 128:(m + 1) * 128], ACT.Sigmoid, t, v_prep, *f6,
                                  bias=P[b0][:, 4 * d + m:4 * d + m + 1])
                    ring.give(bi, t)
                yield
                for m in range(4):
                    if d == 0:
                        V.scan(L[:, m, :], ones, sig[:, m, :], t)
                    else:
                        V.scan(L[:, m, ::-1], ones, sig[:, m, ::-1], t)
                tot = L[:, :, 127:128] if d == 0 else L[:, :, 0:1]
                V.cp(DD.unsqueeze(2), tot)
                t_dd = V.cp(ex[:, :, 0:1], tot)
                t_D = A.act(DD, DD, ACT.Exp, t_dd, scale=-0.5 * KAPPA)
                V.stt(L, ex[:, :, 0:1].broadcast_to([128, 4, 128]), -0.5, L, ALU.mult, ALU.add)
                t = V.tt(sig, L, sig, ALU.subtract)
                t = A.act(ex, L, ACT.Exp, t, scale=KAPPA)
                t = A.act(L, L, ACT.Exp, t, scale=-KAPPA)
                t_e = A.act(sig, sig, ACT.Exp, t, scale=-KAPPA)
                kcs, kkc = K[:, :, cs_], KK[:, :, cs_]
                V.stt(e2, ag, -1.0, bc(P["k_a"], 128), ALU.add, ALU.mult, t_co)
                V.stt(e2, e2, 1.0, kcs, ALU.add, ALU.mult)
                V.tt(ag, ag, kkc, ALU.mult)
                yield
                V.tt(KB[:, 0], e2, ex, ALU.mult, t_e, pe_prev)
                t_kb = V.tt(KB[:, 1], ag, ex, ALU.mult)
                t_ar = V.stt(AR[:, :, 0, :], kkc, -1.0, sig, ALU.mult, ALU.mult)
                if lat:
                    t_ar = V.tt(AR[:, :, 1, :], R[:, :, ls], L, ALU.mult)
                    t = V.tt(e2, e2, R[:, :, ls], ALU.mult)
                    bi, b, bf = ring.take()
                    t_co = T.mm([(b[:, 0:8], e2[:, m, :], IRK[:, m, :], m == 0, m == 3) for m in range(4)], t, *bf)
                    ring.give(bi, accumulate(("coef", c), COEF[:, c - 2, :], b[:, 0:8], t_co))
                t_mp = V.tt(MP, MS, bc(DD, 128), ALU.mult, t_D)
                v_prep = t_mp
                for j in range(2):
                    bi, b, bf = ring.take()
                    t = T.tr([(b[:, m * 128:(m + 1) * 128], KB[:, j, m, :]) for m in range(4)], ident, t_kb, *bf)
                    t_knb = A.act(KNB[:, j, :], b, ACT.Copy, t, pe_prev)
                    ring.give(bi, t_knb)
                yield
                w_ = 256 if lat else 128
                tG = {}
                for nm, buf, j in (("b", GBm, 1), ("k", GKm, 0)):
                    for g in range(2):
                        for q in range(2):
                            bi, b, bf = ring.take()
                            bv = b[:, 0:2 * w_].rearrange("p (h n) -> p h n", h=2)
                            grp = []
                            for n_ in range(2):
                                m = 2 * g + n_
                                rhs = AR[64 * q:64 * q + 64, m, :, :].rearrange("p j s -> p (j s)")[:, 0:w_]
                                grp.append((bv[:, n_, :], KB[64 * q:64 * q + 64, j, m, :], rhs, True, True))
                            t = T.mm(grp, t_ar, *bf)
                            t = V.pred(buf[:, 4 * g + q:4 * g + 4:2, 0:w_], bm(tri_i[:, 0:w_], 2), bv, t, pe_prev, *t_z)
                            ring.give(bi, t)
                            tG[nm, g] = t
                        yield
                tT, tTT, tN = {}, {}, {}
                for g in range(2):
                    hs = slice(4 * g, 4 * g + 4)
                    V.tt(TT[:, hs, :], GBm[:, hs, 0:128], lmT(0), ALU.mult, pe_prev)
                    tTT[g] = V.tt(TT[:, hs, :], TT[:, hs, :], bm(ident, 4), ALU.add)
                    tN[g] = G.tt(NL[:, hs, :], GBm[:, hs, 0:128], lmT(1), ALU.mult, tG["b", g], pe_prev)
                    bi, b, bf = ring.take()
                    t = T.tr([(b[:, n_ * 128:(n_ + 1) * 128], TT[:, 4 * g + n_, :]) for n_ in range(4)], ident, tTT[g], *bf)
                    tT[g] = A.act(TI[:, hs, :], b.rearrange("p (h n) -> p h n", h=4), ACT.Copy, t, pe_prev)
                    ring.give(bi, tT[g])
                yield
                bi, b, bf = ring.take()
                grp = []
                for m in range(4):
                    grp.append((b[:, m * 128:(m + 1) * 128], AR[:, m, 0, :], MP[:, m, :], True, False))
                    for h in (2 * m, 2 * m + 1):
                        grp.append((b[:, h * 64:(h + 1) * 64], GKm[:, h, 0:128], VR[:, c, h * 64:(h + 1) * 64],
                                    False, h % 2 == 1))
                t = T.mm(grp, t_mp, tG["k", 0], tG["k", 1], *bf)
                t_x0 = A.act(X0, b, ACT.Copy, t, pe_prev)
                ring.give(bi, t_x0)
                tU = {}
                for lv in range(1, 7):
                    half = lambda a: a.rearrange("p h (b two m) -> p h b two m", two=2, m=1 << lv)
                    tX = {}
                    for g in range(2):
                        hs = slice(4 * g, 4 * g + 4)
                        bi, b, bf = ring.take()
                        t = T.mm([(b[:, n_ * 128:(n_ + 1) * 128], NL[:, 4 * g + n_, :], TI[:, 4 * g + n_, :], True, True)
                                  for n_ in range(4)], tT[g], tN[g], *bf)
                        if lv < 6:
                            tN[g] = G.tt(NL[:, hs, :], GBm[:, hs, 0:128], lmT(lv + 1), ALU.mult, t)
                        tX[g] = A.act(XB[:, hs, :], b.rearrange("p (h n) -> p h n", h=4), ACT.Copy, t, tU.get(g), pe_prev)
                        ring.give(bi, tX[g])
                    yield
                    for g in range(2):
                        hs = slice(4 * g, 4 * g + 4)
                        bi, b, bf = ring.take()
                        grp = []
                        for n_ in range(4):
                            h = slice(4 * g + n_, 4 * g + n_ + 1)
                            grp.append((b[:, 256 + n_ * 64:320 + n_ * 64], XB[:, 4 * g + n_, :],
                                        half(TT[:, h, :])[:, 0, :, 1 - d, :], True, True))
                        if lv < 6:
                            for n_ in range(4):
                                h = slice(4 * g + n_, 4 * g + n_ + 1)
                                grp.append((b[:, n_ * 64:(n_ + 1) * 64], TT[:, 4 * g + n_, :],
                                            half(XB[:, h, :])[:, 0, :, d, :], True, True))
                        tU[g] = t = T.mm(grp, tX[g], tTT[g], *bf)
                        if lv < 6:
                            o = half(TI[:, hs, :])[:, :, :, d, :]
                            tT[g] = V.tt(o, o, b[:, 0:256].rearrange("p (h b m) -> p h b m", h=4, m=1 << lv), ALU.add, t)
                        o = half(TT[:, hs, :])[:, :, :, 1 - d, :]
                        tTT[g] = V.tt(o, o, b[:, 256:512].rearrange("p (h b m) -> p h b m", h=4, m=1 << lv), ALU.add, t)
                        ring.give(bi, tTT[g])
                    yield
                bi, b, bf = ring.take()
                t = T.mm([(b[:, h * 64:(h + 1) * 64], TT[:, h, :], X0[:, h * 64:(h + 1) * 64], True, True) for h in range(8)],
                         t_x0, tTT[0], tTT[1], *bf)
                t_sa = A.act(SA, b, ACT.Copy, t, pe_prev)
                ring.give(bi, t_sa)
                yield
                bi, b, bf = ring.take()
                grp = []
                for m in range(4):
                    o, ms = b[:, m * 128:(m + 1) * 128], slice(m * 128, (m + 1) * 128)
                    grp.append((o, KNB[:, 0, ms], VR[:, c, ms], True, False))
                    grp.append((o, KNB[:, 1, ms], SA[:, ms], False, True))
                pe_prev = t = T.mm(grp, t_sa, t_knb, *bf)
                V.tt(MS, b.rearrange("p (m v) -> p m v", m=4), bm(C["blk64"], 4), ALU.mult, t)
                ring.give(bi, V.last())
                V.tt(MS, MS, MP, ALU.add)
                V.tt(MS, MS, bc(DD, 128), ALU.mult)
                if lat:
                    bi, b, bf = ring.take()
                    grp = []
                    for m in range(4):
                        grp.append((b[:, m * 128:(m + 1) * 128], AR[:, m, 1, :], MP[:, m, :], True, False))
                        for h in (2 * m, 2 * m + 1):
                            o, hs = b[:, h * 64:(h + 1) * 64], slice(h * 64, (h + 1) * 64)
                            grp.append((o, GKm[:, h, 128:256], VR[:, c, hs], False, False))
                            grp.append((o, GBm[:, h, 128:256], SA[:, hs], False, h % 2 == 1))
                    pe_prev = t = T.mm(grp, t_sa, *bf)
                    ring.give(bi, accumulate(("y", c), YS[:, c - 2, :], b, t))
                yield
            ends_of[d] = [T.last(), V.last(), A.last(), G.last()]

        ar.top = mark4
        rings = [Slots(banks.bufs[4 * d:4 * d + 4]) for d in range(2)]
        for r_ in rings:
            for j in range(4):
                r_.give(j, *f6)
        woven = [recurrence(0, low, rings[0]), recurrence(1, ring_mem, rings[1])]
        for _ in range(LAG):
            next(woven[0])
        while woven:
            for s_ in list(woven):
                if next(s_, 0) == 0:
                    woven.remove(s_)

        if dbg:
            dbg("ys", YS, V, G, dsem)
        f = fence()
        for j in range(8):
            banks.give(j, *f)
        for j in range(len(W.slots.bufs)):
            W.give(j, *ends_of[1])
        if dbg:
            f = f + dbg.toks
        ar.top = mark4
        fl = [ar.get(512) for _ in range(5)]
        GW, GBi = ar.get(512), ar.get(512)
        B2 = ar.get(2048, m=4, s=512)
        st = ar.get(64)
        d_gn = dsem()
        d_bk = dsem()
        t_hb = G.dma(HT.rearrange("p k s -> p (k s)"), htd, d_bk, *ends_of[0])
        t_xb = G.dma(X.rearrange("p t d -> p (t d)"), xd, d_bk, *ends_of[0])
        t_hb = t_xb
        t_gn = G.dma(GW, T_["gn_w_2"][0, :].partition_broadcast(128), d_gn, *f)
        t_gn = G.dma(GBi, T_["gn_b_2"][0, :].partition_broadcast(128), d_gn, *f)
        t_b2 = []
        yp = [None, None]
        for i in range(4):
            y3 = YS[:, i, :].rearrange("p (h d) -> p h d", h=8)
            q_ = fl[2 + i % 2]
            q3 = q_.rearrange("p (h d) -> p h d", h=8)
            V.red(st[:, 0:8], y3, ALU.add, *f)
            V.ts(st[:, 0:8], st[:, 0:8], 1.0 / 64, None, ALU.mult, None)
            V.tt(y3, y3, bc(st[:, 0:8], 64), ALU.subtract)
            V.tt(q3, y3, y3, ALU.mult, yp[i % 2])
            t = V.red(st[:, 8:16], q3, ALU.add)
            t = A.act(st[:, 16:24], st[:, 8:16], ACT.Sqrt, t, bias=eps[:, 1:2], scale=1.0 / 64)
            V.rec(st[:, 24:32], st[:, 16:24], t)
            V.tt(y3, y3, bc(st[:, 24:32], 64), ALU.mult)
            V.tt(YS[:, i, :], YS[:, i, :], GW, ALU.mult, t_gn)
            V.tt(YS[:, i, :], YS[:, i, :], GBi, ALU.add)
            V.tt(q3, VR[:, 2 + i, :].rearrange("p (h d) -> p h d", h=8), bc(COEF[:, i, :], 64), ALU.mult)
            V.tt(YS[:, i, :], YS[:, i, :], q_, ALU.add)
            bi, b, bf = banks.take()
            t = T.mm([(b, SG[:, i * 128:(i + 1) * 128], G2, True, True)], t_sg, t_rw, *bf)
            t = V.tt(YS[:, i, :], YS[:, i, :], b, ALU.mult, t)
            banks.give(bi, t)
            bi, b, bf = banks.take()
            t = T.tr([(b[:, q * 128:(q + 1) * 128], YS[:, i, q * 128:(q + 1) * 128]) for q in range(4)], ident, t, *bf)
            t = A.act(B2[:, :, i * 128:(i + 1) * 128], b.rearrange("p (q s) -> p q s", q=4), ACT.Copy, t, *f)
            banks.give(bi, t)
            t_b2.append(t)
        if dbg:
            dbg("b2", B2, V, G, dsem)

        f = fence()
        if dbg:
            f = f + dbg.toks
        b2_top = ar.top
        ar.top = mark2
        B01 = ar.get(4096, b=2, m=4, s=512)
        MG = ar.get(4096, m=8, s=512)
        gt = [ar.get(512) for _ in range(4)]
        assert ar.top <= mark4 + 5 * 512
        d_re = dsem()
        t_re = G.dma(B01.rearrange("p b m s -> p b (m s)"), brd.rearrange("b p n -> p b n"), d_re, *f, t_brd)
        br = [B01[:, 0], B01[:, 1], B2]
        t_bin = [t_re] + t_b2
        gj = 0
        grd = [None, None, None, None]
        t_mg = {}
        for n in range(3):
            g0 = chunk(34 + 2 * n)
            wbr = chunk(40 + n)
            g1 = chunk(35 + 2 * n)
            wb3 = wbr[1].rearrange("p (k n) -> p k n", k=4)
            for m in range(8):
                gs_ = g0 if m < 4 else g1
                wg = gs_[1].rearrange("p (k n) -> p k n", k=8)
                mc = slice((m % 4) * 128, (m % 4 + 1) * 128)
                bi, b, bf = banks.take()
                t = T.mm([(b, wg[:, k, mc], HT[:, k, :], k == 0, k == 7) for k in range(8)], gs_[2], t_hb, *bf)
                if m % 4 == 3:
                    W.give(gs_[0], t)
                gg = gt[gj % 4]
                tg = A.act(gg, b, ACT.Sigmoid, t, *f, grd[gj % 4])
                banks.give(bi, tg)
                bi, b, bf = banks.take()
                t = T.mm([(b, wb3[:, k, m * 128:(m + 1) * 128], br[n][:, k, :], k == 0, k == 3) for k in range(4)],
                         wbr[2], *t_bin, *bf)
                if m == 7:
                    W.give(wbr[0], t)
                if n == 0:
                    t = V.tt(MG[:, m, :], gg, b, ALU.mult, tg, t, *f)
                    banks.give(bi, t)
                else:
                    t = V.tt(gg, gg, b, ALU.mult, tg, t)
                    banks.give(bi, t)
                    t = V.tt(MG[:, m, :], MG[:, m, :], gg, ALU.add)
                grd[gj % 4] = t
                t_mg[m] = t
                gj += 1
        f = fence()
        ar.top = mark2 + 8192 + 2048
        rowA, rowB = ar.get(1024), ar.get(1024)
        d_r = dsem()
        t_m = mod_load(rowA, 2, 2, f)
        tt_ = [ar.get(512) for _ in range(2)]
        t_x2 = []
        for hf in range(2):
            ws, wb, wt = chunk(43 + hf)
            w = wb.rearrange("p (k n) -> p k n", k=8)
            for i in range(4):
                bi, b, bf = banks.take()
                t = T.mm([(b, MG[:, k, i * 128:(i + 1) * 128], w[:, k, :], k == 0, k == 7) for k in range(8)],
                         wt, *t_mg.values(), *bf)
                if i == 3:
                    W.give(ws, t)
                tq = tt_[i % 2]
                t = V.tt(tq, b, rowA[:, hf * 512:(hf + 1) * 512], ALU.mult, t, t_m, *f)
                banks.give(bi, t)
                xs = X[:, i, hf * 512:(hf + 1) * 512]
                t_x2.append(V.tt(xs, xs, tq, ALU.add, t_xb))
        if dbg:
            dbg("x2", X, V, G, dsem)

        f = fence()
        if dbg:
            f = f + dbg.toks
        ar.top = base + 2048 + 64
        extra = ar.top
        small2 = small
        gs, sh = ar.get(1024), ar.get(1024)
        ht = [ar.get(1024) for _ in range(4)]
        sqb = ar.get(1024)
        n2 = ar.get(1024)
        WRT = ar.get(288, k=8, e=36)
        RT = ar.get(4 * 36, t=4, e=36)
        d_q = dsem()
        t_l = [mod_load(gs, 2, 4, f), mod_load(sh, 2, 3, f), G.dma(n2, T_["norm2_g_2"].partition_broadcast(128), d_q, *f),
               G.dma(WRT, T_["w_router"].rearrange("(k p) e -> p k e", p=128), d_q, *f)]
        t_l[2] = t_l[3]
        t_gs = V.stt(gs, gs, 1.0, n2, ALU.add, ALU.mult, *t_l, *f)
        d_fd = dsem()
        fdv = fd.rearrange("(t p) d -> p t d", p=128)
        f5_ = transposed(HT, f)
        t_fd = []

        def dest(i, h, t):
            t_fd.append(G.dma(fdv[:, i, :], h, d_fd, t))
            f5_(i, h, t)
            return None

        ss = small[:, 0:4]
        for i in range(4):
            t = A.act(sqb, X[:, i, :], ACT.Square, *t_x2, *f, accum_out=ss[:, i:i + 1])
        t = A.act(small[:, 8:12], ss, ACT.Sqrt, bias=eps[:, 0:1], scale=1.0 / D)
        V.rec(small[:, 16:20], small[:, 8:12], t)
        for i in range(4):
            V.stt(ht[i], X[:, i, :], small[:, 16 + i:17 + i], gs, ALU.mult, ALU.mult, *t_l, *f)
            t = V.tt(ht[i], ht[i], sh, ALU.add)
            dest(i, ht[i], t)
        bi, b, bf = banks.take()
        g_ = []
        for i in range(4):
            g_ += [(b[:, i * 36:(i + 1) * 36], HT[:, k, i * 128:(i + 1) * 128], WRT[:, k, :], k == 0, k == 7) for k in range(8)]
        t = T.mm(g_, *f5_.done, *t_l, *bf)
        t = V.cp(RT, b[:, 0:144].rearrange("p (t e) -> p t e", t=4), t)
        banks.give(bi, t)

        def s4(n, **dims):
            return ar.get(n, **dims)

        GP = s4(32, t=4, e=8)
        GM = s4(32, t=4, e=8)
        GI = ar.get(32, U32, t=4, e=8)
        grp = s4(4)
        EQ = s4(128, t=4, e=32)
        LE = s4(128, t=4, e=32)
        TV = s4(32, t=4, e=8)
        TIx = ar.get(32, U32, t=4, e=8)
        EF = s4(8, t=4, e=2)
        E1, E2, IN, RK, Q_, QP, DM = [s4(128, t=4, e=32) for _ in range(7)]
        sm_, pg, dif, exd, g1_, g2_ = [s4(4) for _ in range(6)]
        gex = s4(16, t=4, e=4)
        OVi, OVx, cnt, ov, o1 = [s4(32) for _ in range(5)]
        EID = s4(8)
        DF = s4(8, t=4, e=2)
        DI = ar.get(8, I32, t=4, e=2)
        TOK = ar.get(4, I32)
        IDX = ar.get(NB, I32)
        ZI = ar.get(NB, I32)
        onesr = s4(32)
        zrow = sqb
        Gg = ar.get(8, t=4, e=2)
        t_z = V.zero(zrow, *f)
        V.zero(ZI.bitcast(F))
        V.zero(onesr, value=1.0)
        V.zero(GP, value=-3.0e38)
        t = V.zero(LE, value=-3.0e38)
        d_i = dsem()
        t_i0 = G.dma(idxd.rearrange("(r b) o -> r (b o)", b=NB), ZI, d_i, t)
        t_tok = G.dma(TOK, T_["tok"], d_i, *f)
        d_y0 = dsem()
        t_y0 = None
        for j in range(OVF):
            t_y0 = G.dma(ydv[:, 32 + j, :], zrow, d_y0, t)
        V.cp(GP[:, :, 0:4], RT[:, :, 0:4])
        for i in range(4):
            V.put([lambda e, i=i: e.max(GM[:, i, :], GP[:, i, :])], [])
            V.put([lambda e, i=i: e.max_index(GI[:, i, :], GM[:, i, :], GP[:, i, :])], [])
        V.cp(grp.unsqueeze(2), GI[:, :, 0:1])
        V.ts(pg.unsqueeze(2), GM[:, :, 0:1], -1.0, None, ALU.mult, None)
        t = V.tt(gex, RT[:, :, 0:4], bc(pg, 4), ALU.add)
        t = A.act(gex, gex, ACT.Exp, t)
        V.red(sm_, gex, ALU.add, t)
        V.rec(pg, sm_)
        V.tt(EQ, bm(C["grp32"], 4), bc(grp, 32), ALU.is_equal)
        V.pred(LE, EQ.bitcast(U32), RT[:, :, 4:36])
        for i in range(4):
            V.put([lambda e, i=i: e.max(TV[:, i, :], LE[:, i, :])], [])
            V.put([lambda e, i=i: e.max_index(TIx[:, i, :], TV[:, i, :], LE[:, i, :])], [])
        V.cp(EF, TIx[:, :, 0:2])
        t = V.tt(dif.unsqueeze(2), TV[:, :, 1:2], TV[:, :, 0:1], ALU.subtract)
        t = A.act(exd, dif, ACT.Exp, t)
        V.ts(g1_, exd, 1.0, None, ALU.add, None, t)
        V.rec(g1_, g1_)
        V.tt(g1_, g1_, pg, ALU.mult)
        V.tt(g2_, g1_, exd, ALU.mult)
        V.cp(Gg[:, :, 0], g1_)
        t_gate = V.cp(Gg[:, :, 1], g2_)
        V.tt(E1, bm(C["iota32"], 4), EF[:, :, 0:1].broadcast_to([128, 4, 32]), ALU.is_equal)
        V.tt(E2, bm(C["iota32"], 4), EF[:, :, 1:2].broadcast_to([128, 4, 32]), ALU.is_equal)
        t = V.tt(IN, E1, E2, ALU.add)
        bi, b, bf = banks.take()
        g_ = []
        for i in range(4):
            o = b[:, i * 32:(i + 1) * 32]
            for q in range(i):
                g_.append((o, ones, IN[:, q, :], q == 0, False))
            g_.append((o, C["tri"], IN[:, i, :], i == 0, True))
        for q in range(4):
            g_.append((b[:, 128:160], ones, IN[:, q, :], q == 0, q == 3))
        t = T.mm(g_, t, *bf)
        V.cp(RK, b[:, 0:128].rearrange("p (t e) -> p t e", t=4), t)
        t = V.cp(cnt, b[:, 128:160])
        banks.give(bi, t)
        V.ts(ov, cnt, 128.5, None, ALU.is_ge, None)
        for th in (256.5, 384.5):
            V.ts(o1, cnt, th, None, ALU.is_ge, None)
            V.tt(ov, ov, o1, ALU.add)
        V.scan(OVi, onesr, ov)
        V.tt(OVx, OVi, ov, ALU.subtract)
        t_iov = V.cp(iovn, OVi[:, 31:32])
        for j in range(OVF):
            V.ts(o1, OVi, j + 0.5, None, ALU.is_le, None)
            V.red(EID[:, j:j + 1], o1, ALU.add)
        V.ts(EID[:, 0:OVF], EID[:, 0:OVF], 31.0, None, ALU.min, None)
        t_iov = V.cp(iov[:, 0:OVF], EID[:, 0:OVF])
        V.ts(Q_, RK, 127.5, None, ALU.is_ge, None)
        V.cp(QP, Q_)
        for th in (255.5, 383.5):
            V.ts(DM, RK, th, None, ALU.is_ge, None)
            V.tt(Q_, Q_, DM, ALU.add)
        V.stt(RK, Q_, -128.0, RK, ALU.mult, ALU.add)
        V.tt(DM, Q_, bm(OVx, 4), ALU.add)
        V.ts(DM, DM, 31.0, None, ALU.add, None)
        V.tt(DM, DM, bm(C["iota32"], 4), ALU.subtract)
        V.tt(DM, DM, QP, ALU.mult)
        V.tt(DM, DM, bm(C["iota32"], 4), ALU.add)
        V.stt(DM, RK, float(NB), DM, ALU.mult, ALU.add)
        for j, E_ in enumerate((E1, E2)):
            V.tt(E_, E_, DM, ALU.mult)
            V.red(DF[:, :, j:j + 1], E_, ALU.add)
        t_di = V.cp(DI, DF)
        d_s = dsem()
        for i in range(4):
            for j in range(2):
                tok = d_s.add()
                G.items.append(([lambda e, i=i, j=j: e.indirect_dma_start(
                    idxd, bass.IndirectOffsetOnAxis(ap=DI[:, i, j:j + 1], axis=0), TOK[:, i:i + 1], None)],
                    [t_di, t_i0, t_tok], (d_s.sem, 16)))
        d_ix = dsem()
        t_idx = G.dma(IDX, idxd.rearrange("(r b) o -> r (b o)", b=NB), d_ix, tok)

        f = fence() + [t_fd[-1], t_y0, t_i0, t_idx]
        YO = [ar.get(1024) for _ in range(2)]
        n_extra = (NCOL - ar.top) // 4096
        more = [ar.get(4096) for _ in range(n_extra)] + [HT.rearrange("p k s -> p (k s)")]
        ar.top = extra
        XG = [ar.get(1024) for _ in range(2)]
        XT = [ar.get(1024, k=8, s=128) for _ in range(2)]
        SGm = [ar.get(512) for _ in range(2)]
        AC = [ar.get(512) for _ in range(2)]
        ACT_T = [ar.get(512, k=4, s=128) for _ in range(2)]
        rowC = ar.get(1024)
        assert ar.top <= extra + 8192
        pad = (-W.slots.i) % len(W.slots.bufs)
        W.slots.i += pad
        W.grow(more, *f)
        W.slots.i = 0
        t_rc = mod_load(rowC, 2, 5, f)
        d_xg = [dsem() for _ in range(2)]
        d_yo = [dsem() for _ in range(2)]

        class Experts:
            def __init__(self, L, W_, f, dx, dy):
                self.L, self.W, self.f = L, W_, f
                self.s = {}
                self.dx, self.dy = dx, dy
                self.done = []

            def front(self, e, blk, src, idx_ap):
                T, V, A, G, Y = [self.L[x] for x in "TVAGY"]
                s, p = self.s, e % 2
                tok = self.dx[p].add()
                G.items.append(([lambda eng: eng.indirect_dma_start(
                    XG[p], None, fd, bass.IndirectOffsetOnAxis(ap=idx_ap, axis=0))],
                    [t_idx, *t_fd, *self.f, s.get(("tr", e - 2))], (self.dx[p].sem, 16)))
                w = [self.W.load(src(j), Y) for j in range(3)]
                s["w", e] = w
                for half in range(2):
                    bi, b, bf = banks.take()
                    t = T.tr([(b[:, q * 128:(q + 1) * 128], XG[p][:, (4 * half + q) * 128:(4 * half + q + 1) * 128])
                              for q in range(4)], ident, tok, *bf)
                    o = XT[p][:, 4 * half:4 * half + 4, :]
                    sv = b.rearrange("p (q s) -> p q s", q=4)
                    te = V.cp(o, sv, t, s.get(("gu", e - 2)), *self.f)
                    banks.give(bi, te)
                    s["xt", e, half] = te
                s["tr", e] = t
                bb = []
                for j in range(2):
                    ws, wb, wt = w[j]
                    wv = wb.rearrange("p (k n) -> p k n", k=8)
                    bi, b, bf = banks.take()
                    t = T.mm([(b, XT[p][:, k, :], wv[:, k, :], k == 0, k == 7) for k in range(8)],
                             wt, s["xt", e, 0], s["xt", e, 1], *bf)
                    self.W.give(ws, t)
                    bb.append((bi, b, t))
                s["gu", e] = t
                (gi, gb, tg), (ui, ub, tu) = bb
                t = A.act(SGm[p], gb, ACT.Sigmoid, tg, s.get(("ac", e - 2)), *self.f)
                t = V.tt(SGm[p], SGm[p], gb, ALU.mult, t)
                banks.give(gi, t)
                s["ac", e] = t = V.tt(AC[p], SGm[p], ub, ALU.mult, tu, s.get(("at", e - 2)))
                banks.give(ui, t)

            def back(self, e, blk):
                T, V, A, G, Y = [self.L[x] for x in "TVAGY"]
                s, p = self.s, e % 2
                bi, b, bf = banks.take()
                s["at", e] = t = T.tr([(b[:, q * 128:(q + 1) * 128], AC[p][:, q * 128:(q + 1) * 128]) for q in range(4)],
                                      ident, s["ac", e], *bf)
                t = A.act(ACT_T[p], b.rearrange("p (q s) -> p q s", q=4), ACT.Copy, t, s.get(("dn", e - 2)), *self.f)
                banks.give(bi, t)
                ws, wb, wt = s["w", e][2]
                wv = wb.rearrange("p (k n) -> p k n", k=4)
                for hf in range(2):
                    bi, b, bf = banks.take()
                    td = T.mm([(b, ACT_T[p][:, k, :], wv[:, k, hf * 512:(hf + 1) * 512], k == 0, k == 3) for k in range(4)],
                              wt, t, *bf)
                    o = YO[p][:, hf * 512:(hf + 1) * 512]
                    ty = A.act(o, b, ACT.Copy, td, s.get(("yo", e - 2)), *self.f)
                    banks.give(bi, ty)
                s["dn", e] = td
                self.W.give(ws, td)
                s["yo", e] = A.dma(ydv[:, blk, :], YO[p], self.dy[p], ty, t_y0)
                self.done.append(s["yo", e])

        ex = Experts(main, W, f, d_xg, d_yo)
        for e in range(33):
            if e < 32:
                ex.front(e, e, lambda j, e=e: T_["w"][45 + 3 * e + j], IDX[:, e:e + 1])
            if e >= 1:
                ex.back(e - 1, e - 1)
        t_yd = ex.done[-2:]

        f = fence() + t_yd
        ovl = {n: Lane(sem(f"o_{n}"), n in "VAG") for n in "TVAGY"}
        saved = (banks.free, banks.i)
        banks.free = [[] for _ in banks.bufs]

        class OvfStream(Stream):
            pass

        WO = OvfStream()
        WO.grow(W.slots.bufs[0:6])
        ev = {}
        oex = Experts(ovl, WO, [], [dsem(), dsem()], [dsem(), dsem()])
        for n in "TVAGY":
            ovl[n].items.append(([], f, None))
        regs = {}
        for j in range(OVF):
            def src(q, j=j):
                return ("dyn", j, q)
            oex_load = WO.load

            def load(s_, lane, j=j):
                k, buf, free = WO.slots.take()
                d = WO.d[k]
                tok = d.add()

                def go(e, s_=s_, buf=buf):
                    if s_[2] == 0:
                        regs[s_[1]] = e.value_load(iov[0:1, s_[1]:s_[1] + 1], min_val=0, max_val=31)
                    r = regs[s_[1]]
                    return e.dma_start(buf, T_["w"][bass.ds(r * 3 + (45 + s_[2]), 1)][0])
                lane.items.append(([go], free, (d.sem, 16)))
                return k, buf, tok
            WO.load = load
            oex.front(j, 32 + j, src, IDX[:, 32 + j:33 + j])
            oex.back(j, 32 + j)
        ovl["A"].items.append(([], oex.done[-2:], None))
        ovl["G"].items.append(([], oex.done[-2:] + [ovl["T"].last(), ovl["V"].last(), ovl["A"].last()], None))
        banks.free, banks.i = saved

        tail = {n: Lane(sem(f"t_{n}"), n in "VAG") for n in "TVAGY"}
        V2, G2_, A2_ = tail["V"], tail["G"], tail["A"]
        y12 = [[XG[0], XG[1]], [YO[0], YO[1]]]
        d_y = [dsem() for _ in range(2)]
        d_o = dsem()
        done = [None, None]
        t_all = [*t_yd, t_y0, T.last(), V.last(), A.last()]
        for i in range(4):
            bufs = y12[i % 2]
            for j in range(2):
                ty = d_y[i % 2].add()
                G2_.items.append(([lambda e, i=i, j=j, bufs=bufs: e.indirect_dma_start(
                    bufs[j], None, yd, bass.IndirectOffsetOnAxis(ap=DI[:, i, j:j + 1], axis=0))],
                    [*t_all, done[i % 2]], (d_y[i % 2].sem, 16)))
            V2.ts(bufs[0], bufs[0], Gg[:, i, 0:1], None, ALU.mult, None, ty, t_gate, t_rc)
            V2.stt(bufs[0], bufs[1], Gg[:, i, 1:2], bufs[0], ALU.mult, ALU.add)
            V2.tt(bufs[0], bufs[0], rowC, ALU.mult)
            t = done[i % 2] = V2.tt(X[:, i, :], X[:, i, :], bufs[0], ALU.add)
            t_out = A2_.dma(out_d[:, i, :], X[:, i, :], d_o, t)
        A2_.items.append(([], [t_out], None))
        ends = [t_out]
        if dbg:
            A2_.items.append(([], dbg.toks, None))

        block = ctx.enter_context(nc.Block())

        def program(eng, n):
            seen = {}
            main[n].run(eng, seen)
            eng.wait_ge(V.sem, t_iov[1])
            r = eng.value_load(iovn[0:1, 0:1], min_val=0, max_val=OVF)
            with eng.If(r > (-1 if force_ovf else 0)):
                ovl[n].run(eng, dict(seen))
            tail[n].run(eng, dict(seen))

        @block.sync
        def _(e):
            program(e, "Y")

        @block.gpsimd
        def _(e):
            program(e, "G")

        @block.scalar
        def _(e):
            program(e, "A")

        @block.vector
        def _(e):
            program(e, "V")

        @block.tensor
        def _(e):
            program(e, "T")


def chunks(i):
    def cut(w, k, n):
        r, c = w.shape
        return [w[:, j * n:(j + 1) * n].reshape(k, 128, n).transpose(1, 0, 2).reshape(128, k * n) for j in range(c // n)]

    w2 = i["w_in_2"][0]
    mid = np.zeros((1024, 512), np.float32)
    mid[:, 0:384] = w2[:, 3584:3968]
    out = np.empty((141, 128, 4096), np.float32)
    at = 0
    parts = [(i["w_ada"][0], 8, 512), (i["w_in"][0], 8, 512), (i["w_out"][0], 8, 512), (i["w_ada_2"][0], 8, 512),
             (w2[:, 0:3584], 8, 512), (mid, 8, 512), (w2[:, 3968:7040], 8, 512)]
    parts += [(i["w_br_2"][0, n], 4, 1024) for n in range(3)] + [(i["w_out_2"][0], 8, 512)]
    for e in range(32):
        parts += [(i["w_exp_gate_2"][0, e], 8, 512), (i["w_exp_up_2"][0, e], 8, 512), (i["w_exp_down_2"][0, e], 4, 1024)]
    for w, k, n in parts:
        for c in cut(w, k, n):
            out[at] = c
            at += 1
    assert at == 141
    return out


def params(i):
    def col(v):
        return np.ascontiguousarray(v, np.float32).reshape(-1, 128).T

    p = {
        "c": col(i["c"]), "c2": col(i["c_2"]), "cc": col(i["c_ctx_2"]), "conv_w": col(i["conv_w"][0]),
        "conv_b": col(i["conv_b"]), "b_a": col(i["b_rg_a"]), "b_x": col(i["b_rg_x"]), "lam": col(i["lru_lambda"]),
        "norm_rec": col(i["norm_rec"]), "qn": col(np.tile(i["q_norm_g_2"][0], 2)), "kn": col(np.tile(i["k_norm_g_2"][0], 2)),
        "mu0": col(i["shift_mu_2"][0, 0]), "mu1": col(i["shift_mu_2"][0, 1]), "w0": col(i["decay_w0_2"][0]),
        "a0": col(i["aaa_a0_2"][0]), "k_k": col(i["k_k_2"]), "k_a": col(i["k_a_2"]), "r_k": col(i["r_k_2"]),
        "pscale": col(i["pool_scale_2"]),
    }
    return np.concatenate([p[n] for n, _ in COL_SPEC], 1)


def lru_weights(i):
    out = np.zeros((128, 8, 128), np.float32)
    for j, n in enumerate(("w_rg_a", "w_rg_x")):
        for h in range(8):
            o = 64 * (h % 2)
            out[o:o + 64, 4 * j + h // 2, o:o + 64] = i[n][0, h]
    return out.reshape(128, 1024)


def constants():
    p = np.arange(128)
    c = {n: np.zeros((128, w), np.float32) for n, w in CONST_SPEC}
    c["ident"][:] = np.eye(128)
    c["ones"][:] = 1
    c["blk64"][:] = (p[:, None] // 64 == p[None] // 64)
    s1 = (p // 64) * 64 + (p % 64 + 32) % 64
    c["perm1"][s1, p] = 1
    s2 = (p // 32) * 32 + (p % 32 + 16) % 32
    c["perm2"][s2, p] = 1
    c["tri"][:] = p[:, None] < p[None]
    for j in range(18):
        c["selp"][j, 2 * j:2 * j + 2] = 1
    f = (10000.0 ** (-np.arange(32) / 32.0)).astype(np.float32)
    c["invf"][:, 0] = f[p % 32]
    c["sgn"][:, 0] = np.where(p % 64 < 32, -1, 1)
    c["iota32"][:] = np.arange(32)
    c["grp32"][:] = np.arange(32) // 8
    for m in range(4):
        c["ind"][p, 8 * m + 2 * m + p // 64] = 1
    return np.concatenate([c[n] for n, _ in CONST_SPEC], 1)


def mask_constants():
    p = np.arange(128)
    t, s = p[:, None], p[None]
    c = {}
    for d in range(2):
        lv = []
        for b in range(7):
            m = 1 << b
            same = t // (2 * m) == s // (2 * m)
            tb, sb_ = (t // m) % 2, (s // m) % 2
            lv.append(same & ((tb == 1) & (sb_ == 0) if d == 0 else (tb == 0) & (sb_ == 1)))
        c["lm%d" % d] = np.concatenate(lv, 1)
        before = (t < s) if d == 0 else (t > s)
        c["si%d" % d] = np.concatenate([before, before | (t == s)], 1)
        c["sb%d" % d] = (s < t) if d == 0 else (s > t)
    return np.concatenate([c[n] for n, _ in MASK_SPEC], 1).astype(np.float32)


def rope_constants():
    tok = np.arange(S)
    f = (10000.0 ** (-np.arange(16) / 16.0)).astype(np.float32)
    rows, cols = (tok // 64).astype(np.float32), (tok % 64).astype(np.float32)
    p = np.arange(128)
    pos = np.where(((p % 64) < 32)[:, None], rows[None], cols[None])
    ang = (pos * f[p % 16][:, None]).astype(np.float32).astype(np.float64)
    sgn = np.where(p % 32 < 16, -1.0, 1.0)[:, None]
    cnt = []
    for w in (2, 4, 8, 16):
        lo = np.clip(tok - w // 2, 0, S - 1)
        hi = np.clip(tok + w // 2 - 1, 0, S - 1)
        cnt.append(np.broadcast_to(1.0 / (hi - lo + 1), (128, S)))
    return np.concatenate([np.cos(ang), np.sin(ang) * sgn] + cnt, 1).astype(np.float32)


def multiplicities():
    out = []
    for i in range(4):
        q = np.arange(128)[:, None] + 128 * i
        k = np.arange(128 * (i + 1))[None]
        dist = q - k
        n = ((dist >= 0) & (dist <= 128)).astype(int) + ((dist >= 0) & (dist % 4 == 0)) + ((dist >= 0) & (dist % 16 == 0))
        out.append(np.where(n > 0, np.log(np.maximum(n, 1)), -1e30))
    return np.concatenate(out, 1).astype(np.float32)


def arrays_of(i):
    i = {k: np.asarray(v) for k, v in i.items()}
    a = {
        "w": chunks(i), "params": params(i), "consts": constants(), "masks": mask_constants(), "ropes": rope_constants(),
        "lnc": multiplicities(), "w_rg": lru_weights(i),
        "bias": np.concatenate([i["b_ada"][0].reshape(6, 512), i["b_ada_2"][0].reshape(12, 512)], 0),
        "x": i["x"], "positions": i["positions"].astype(np.int32) if i["positions"].dtype != np.int32 else i["positions"],
        "norm_pre": i["norm_pre"][0], "norm_post": i["norm_post"][0], "norm_att": i["norm_att"][0],
        "ctx_2": i["ctx_2"], "norm1_g_2": i["norm1_g_2"][0], "norm2_g_2": i["norm2_g_2"][0],
        "pool_w_2": i["pool_w_2"], "lambda_qk_2": i["lambda_qk_2"], "subln": np.tile(i["subln_g_2"][0], 4),
        "decay_w2": i["decay_w2_2"][0].reshape(128, 512), "aaa_a2": i["aaa_a2_2"][0].reshape(128, 512),
        "gate_w2": i["gate_w2_2"][0], "gn_w_2": i["gn_w_2"], "gn_b_2": i["gn_b_2"],
        "w_router": np.concatenate([i["w_router_group_2"][0], i["w_router_expert_2"][0]], 1),
        "tok": (np.arange(4)[None] * 128 + np.arange(128)[:, None]).astype(np.int32),
    }
    return {k: np.ascontiguousarray(v) for k, v in a.items()}


def kernel(**inputs):
    import concourse.bacc as bacc
    from concourse.bass_utils import run_bass_kernel_spmd

    nc = bacc.Bacc("TRN2", target_bir_lowering=False, num_devices=1)
    a = arrays_of(inputs)
    t = {n: nc.dram_tensor(f"in_{n}", v.shape, mybir.dt.from_np(v.dtype), kind="ExternalInput").ap() for n, v in a.items()}
    t["out"] = nc.dram_tensor("out", (1, S, D), F, kind="ExternalOutput").ap()
    build(nc, t)
    r = run_bass_kernel_spmd(nc, [{f"in_{n}": v for n, v in a.items()}], core_ids=[0])
    return r.results[0]["out"]
```

```python
import math
from contextlib import ExitStack

import numpy as np

import concourse.bass as bass
from concourse import mybir

F = mybir.dt.float32
I32 = mybir.dt.int32
U32 = mybir.dt.uint32
ALU = mybir.AluOpType
ACT = mybir.ActivationFunctionType
AX = mybir.AxisListType.X

D = 1024
S = 512
CTX = 256
NB = 39
OVF = 7
KAPPA = math.exp(-0.5)
EPS = 1e-6
GN_EPS = 64e-5
NCOL = 53100
LAG = 26
SMALL = 1935

COL_SPEC = [
    ("c", 8), ("c2", 8), ("cc", 8), ("conv_w", 16), ("conv_b", 4), ("b_a", 4), ("b_x", 4), ("lam", 4),
    ("norm_rec", 4), ("qn", 1), ("kn", 1), ("mu0", 15), ("mu1", 15), ("w0", 8), ("a0", 8), ("k_k", 4),
    ("k_a", 4), ("r_k", 4), ("pscale", 4), ("b_mod", 16), ("npre", 8),
]
COLS = {}
_o = 0
for _n, _w in COL_SPEC:
    COLS[_n] = (_o, _o + _w)
    _o += _w
NPARAM = _o

CONST_SPEC = [
    ("ident", 128), ("ones", 128), ("blk64", 128), ("perm1", 128), ("perm2", 128), ("tri", 128),
    ("selp", 36), ("invf", 1), ("sgn", 1), ("iota32", 32), ("grp32", 32), ("ind", 32),
]
MASK_SPEC = [("lm0", 7 * 128), ("lm1", 7 * 128), ("si0", 256), ("si1", 256), ("sb0", 128), ("sb1", 128)]
ROPE_SPEC = [("cos2", 512), ("sin2", 512), ("cnt", 2048)]


def offsets(spec):
    out, o = {}, 0
    for n, w in spec:
        out[n] = (o, o + w)
        o += w
    return out, o


CONSTS, NCONST = offsets(CONST_SPEC)
MASKS, NMASK = offsets(MASK_SPEC)
ROPES, NROPE = offsets(ROPE_SPEC)
LNC_OFF = [0, 128, 384, 768]
LNC_N = 1280


class Dma:

    def __init__(self, sem):
        self.sem, self.n = sem, 0

    def add(self):
        self.n += 16
        return (self.sem, self.n)


class Lane:

    def __init__(self, sem, chain):
        self.sem, self.n, self.items, self.chain = sem, 0, [], chain

    def put(self, fns, after):
        own = [(self.sem, self.n)] if self.chain and self.n else []
        self.items.append((fns, list(after) + own, (self.sem, 1)))
        self.n += 1
        return (self.sem, self.n)

    def last(self):
        return (self.sem, self.n)

    def dma(self, out, in_, d, *after):
        tok = d.add()
        self.items.append(([lambda e: e.dma_start(out, in_)], list(after), (d.sem, 16)))
        return tok

    def run(self, e, seen):
        for fns, after, inc in self.items:
            need = {}
            for t in after:
                if t is not None:
                    need[id(t[0])] = max(t, need.get(id(t[0]), t), key=lambda q: q[1])
            for k, (sem, v) in need.items():
                if v > seen.get(k, 0):
                    seen[k] = v
                    e.wait_ge(sem, v)
            for f in fns:
                ins = f(e)
            if inc is not None:
                ins.then_inc(*inc)

    def tt(self, out, a, b, op, *after):
        return self.put([lambda e: e.tensor_tensor(out, a, b, op)], after)

    def ts(self, out, a, s1, s2, op0, op1, *after):
        if s2 is None:
            return self.put([lambda e: e.tensor_scalar(out, a, s1, None, op0)], after)
        return self.put([lambda e: e.tensor_scalar(out, a, s1, s2, op0, op1)], after)

    def stt(self, out, a, s, b, op0, op1, *after):
        return self.put([lambda e: e.scalar_tensor_tensor(out=out, in0=a, scalar=s, in1=b, op0=op0, op1=op1)], after)

    def cp(self, out, a, *after):
        return self.put([lambda e: e.tensor_copy(out, a)], after)

    def rec(self, out, a, *after):
        return self.put([lambda e: e.reciprocal(out, a)], after)

    def zero(self, out, *after, value=0.0):
        return self.put([lambda e: e.memset(out, value)], after)

    def red(self, out, a, op, *after, negate=None):
        return self.put([lambda e: e.tensor_reduce(out, a, AX, op, negate=negate)], after)

    def pred(self, out, mask, a, *after):
        return self.put([lambda e: e.copy_predicated(out, mask, a)], after)

    def scan(self, out, d0, d1, *after):
        return self.put([lambda e: e.tensor_tensor_scan(out, d0, d1, 0.0, ALU.mult, ALU.add)], after)

    def act(self, out, a, func, *after, **kw):
        return self.put([lambda e: e.activation(out, a, func, **kw)], after)

    def mm(self, group, *after):
        return self.put([lambda e, g=g: e.matmul(g[0], g[1], g[2], start=g[3], stop=g[4]) for g in group], after)

    def tr(self, group, ident, *after):
        return self.put([lambda e, g=g: e.transpose(g[0], g[1], ident) for g in group], after)


class Slots:

    def __init__(self, bufs):
        self.bufs, self.free, self.i = bufs, [[] for _ in bufs], 0

    def take(self):
        j = self.i % len(self.bufs)
        self.i += 1
        return j, self.bufs[j], self.free[j]

    def give(self, j, *toks):
        self.free[j] = list(toks)


class Arena:
    def __init__(self, tile, n):
        self.t, self.n, self.top = tile, n, 0

    def get(self, w, dt=None, **dims):
        a = self.t[:, self.top:self.top + w]
        self.top += w
        assert self.top <= self.n, (self.top, self.n)
        if dt is not None:
            a = a.bitcast(dt)
        if dims:
            names = " ".join(dims)
            a = a.rearrange(f"p ({names}) -> p {names}", **dims)
        return a


def bc(ap, n):
    return ap.unsqueeze(2).broadcast_to([128, ap.shape[1], n])


def bm(ap, n):
    return ap.unsqueeze(1).broadcast_to([128, n, ap.shape[1]])


def build(nc, T_):
    dram = {}

    def internal(name, shape, dt=F):
        return nc.dram_tensor(name, shape, dt, kind="Internal").ap()

    mods1 = internal("mods1", (3072,))
    mods2 = internal("mods2", (2, 6144))
    xd = internal("xd", (128, 4096))
    htd = internal("htd", (128, 4096))
    brd = internal("brd", (2, 128, 2048))
    fd = internal("fd", (S, D))
    idxd = internal("idxd", (128 * NB, 1), I32)
    yd = internal("yd", (128 * NB, D))
    ydv = yd.rearrange("(r b) d -> r b d", b=NB)
    out_d = T_["out"].rearrange("o (t p) d -> p (o t) d", p=128)

    ctx = ExitStack()
    with ctx:
        A_ = ctx.enter_context(nc.sbuf_tensor("arena", [128, NCOL], F))
        PSUM = ctx.enter_context(nc.psum_tensor("psum", [128, 8, 512], F))

        def sem(n):
            return ctx.enter_context(nc.semaphore(n))

        T = Lane(sem("s_pe"), False)
        V = Lane(sem("s_dve"), True)
        A = Lane(sem("s_act"), True)
        G = Lane(sem("s_pool"), True)
        Y = Lane(sem("s_sp"), False)
        main = dict(T=T, V=V, A=A, G=G, Y=Y)
        nsem = [0]

        def dsem():
            nsem[0] += 1
            return Dma(sem(f"d{nsem[0]}"))

        ar = Arena(A_, NCOL)
        banks = Slots([PSUM[:, i, :] for i in range(8)])

        class Stream:
            def __init__(self):
                self.slots = Slots([])
                self.d = []

            def grow(self, bufs, *toks):
                assert self.slots.i % max(1, len(self.slots.bufs)) == 0 or not self.slots.bufs
                for b in bufs:
                    self.slots.bufs.append(b)
                    self.slots.free.append(list(toks))
                    self.d.append(dsem())

            def load(self, src, lane=Y):
                j, buf, free = self.slots.take()
                tok = lane.dma(buf, src, self.d[j], *free)
                return j, buf, tok

            def give(self, j, *toks):
                self.slots.give(j, *toks)

        W = Stream()
        W.grow([ar.get(4096) for _ in range(3)])

        def chunk(i):
            return W.load(T_["w"][i])

        cst = ar.get(NCONST)
        par = ar.get(NPARAM)
        eps = ar.get(4)
        cs = ar.get(24, k=8, v=3)
        lamc = ar.get(1)
        iov = ar.get(8, I32)
        iovn = ar.get(1, I32)
        C = {n: cst[:, a:b] for n, (a, b) in CONSTS.items()}
        P = {n: par[:, a:b] for n, (a, b) in COLS.items()}
        ident, ones = C["ident"], C["ones"]

        d_c = dsem()
        t_par = Y.dma(par, T_["params"], d_c)
        t_cst = Y.dma(cst, T_["consts"], d_c)
        t_cst = (d_c.sem, d_c.n)

        t_eps = V.zero(eps[:, 0:1], value=EPS)
        V.zero(eps[:, 1:2], value=GN_EPS)
        t_eps = V.zero(eps[:, 2:3], value=0.0)

        mark0 = ar.top
        X = ar.get(4096, t=4, d=1024)
        HT = ar.get(4096, k=8, s=512)
        base = ar.top

        r0 = ar.get(4096)
        sg = r0[:, 0:24]
        t = A.act(sg, par[:, 0:24], ACT.Sigmoid, t_cst)
        t_cs = V.tt(cs.rearrange("p k v -> p v k"), sg.rearrange("p (v k) -> p v k", v=3),
                    par[:, 0:24].rearrange("p (v k) -> p v k", v=3), ALU.mult, t, t_cst)

        bias = ar.get(512)
        d_b = dsem()
        t_bias = Y.dma(bias[0:18, :], T_["bias"], d_b)
        mrow = Slots([ar.get(512) for _ in range(3)])
        d_m = [dsem() for _ in range(3)]
        t_m1, t_m2 = [], []

        def modulation(j, bank_ring):
            ws, wb, wt = chunk(j if j < 6 else 14 + j - 6)
            w = wb.rearrange("p (k n) -> p k n", k=8)
            M = 1 if j < 6 else 2
            bi, b, bf = bank_ring.take()
            sel = C["selp"][0:18, 2 * j:2 * j + M]
            g = [(b[0:M, :], sel, bias[0:18, :], True, False)]
            for k in range(8):
                lhs = cs[:, k, 0:1] if j < 6 else cs[:, k, 1:3]
                g.append((b[0:M, :], lhs, w[:, k, :], False, k == 7))
            for q in range(3):
                t = T.mm(g[3 * q:3 * q + 3], t_cs, t_bias, t_cst, wt, *bf)
                if q < 2:
                    yield
            W.give(ws, t)
            ri, row, rf = mrow.take()
            t = A.act(row[0:M, :], b[0:M, :], ACT.Copy, t, *rf)
            bank_ring.give(bi, t)
            if j < 6:
                dst = mods1[j * 512:(j + 1) * 512].unsqueeze(0)
            else:
                dst = mods2[:, (j - 6) * 512:(j - 5) * 512]
            t = G.dma(dst, row[0:M, :], d_m[ri], t)
            mrow.give(ri, t)
            (t_m1 if j < 6 else t_m2).append(t)
            yield

        d_mod = dsem()

        def mod_load(dst, which, i, after=()):
            if which == 1:
                src, toks = mods1[i * 1024:(i + 1) * 1024], t_m1
            else:
                src, toks = mods2[which - 2, i * 1024:(i + 1) * 1024], t_m2
            return G.dma(dst, src.partition_broadcast(128), d_mod, *toks, *after)

        small = ar.get(64)

        def transposed(dst, t_dst=()):
            def f(i, h, t):
                for half in range(2):
                    bi, b, bf = banks.take()
                    tt = T.tr([(b[:, q * 128:(q + 1) * 128], h[:, (4 * half + q) * 128:(4 * half + q + 1) * 128])
                               for q in range(4)], ident, t, t_cst, *bf)
                    o = dst[:, 4 * half:4 * half + 4, i * 128:(i + 1) * 128]
                    eng = V if half else A
                    src = b.rearrange("p (q s) -> p q s", q=4)
                    if half:
                        te = V.cp(o, src, tt, *t_dst)
                    else:
                        te = A.act(o, src, ACT.Copy, tt, *t_dst)
                    banks.give(bi, te)
                    f.done.append(te)
                return tt
            f.done = []
            return f

        ht = [r0[:, 1024 * i:1024 * (i + 1)] for i in range(4)]
        sqb = ar.get(1024)
        mods = small[:, 40:56]
        d_x = dsem()
        f1 = transposed(HT)
        t_ht = []

        rows = {}

        def modulation_row(j):
            ws, wb, wt = chunk(j)
            w = wb.rearrange("p (k n) -> p k n", k=8)
            bi, b, bf = banks.take()
            t = T.mm([(b[0:1, :], cs[:, k, 0:1], w[:, k, :], k == 0, k == 7) for k in range(8)], t_cs, wt, *bf)
            W.give(ws, t)
            ri, row, rf = mrow.take()
            rows[j] = (ri, row, A.act(row[0:1, :], b[0:1, :], ACT.Copy, t, *rf))
            banks.give(bi, rows[j][2])

        def modulation_columns(j):
            ri, row, t = rows[j]
            bi, b, bf = banks.take()
            t = T.mm([(b[:, m:m + 1], row[0:1, m * 128:(m + 1) * 128], ones[0:1, 0:1], True, True) for m in range(4)],
                     t, t_cst, *bf)
            mrow.give(ri, t)
            o = mods[:, 4 * j:4 * j + 4]
            t = V.tt(o, b[:, 0:4], P["b_mod"][:, 4 * j:4 * j + 4], ALU.add, t)
            banks.give(bi, t)
            if j < 2:
                return
            t = V.stt(o, o, 1.0, P["npre"][:, 4 * j - 8:4 * j - 4], ALU.add, ALU.mult)
            for k in range(4 * j - 8, 4 * j - 4):
                g, b = mods[:, 8 + k:9 + k], mods[:, k:k + 1]
                if k % 2:
                    t_ht.append(A.act(HT[:, k, :], HT[:, k, :], ACT.Identity, t, *f1.done, scale=g, bias=b))
                else:
                    t_ht.append(V.ts(HT[:, k, :], HT[:, k, :], g, b, ALU.mult, ALU.add, *f1.done))

        modulation_row(0)
        modulation_row(1)
        t_x = Y.dma(X, T_["x"].rearrange("o (t p) d -> p (o t) d", p=128), d_x)
        for i in range(4):
            A.act(sqb, X[:, i, :], ACT.Square, t_x, accum_out=small[:, i:i + 1])
        t = A.act(small[:, 12:16], small[:, 0:4], ACT.Sqrt, t_eps, bias=eps[:, 0:1], scale=1.0 / D)
        modulation_columns(0)
        V.rec(small[:, 24:28], small[:, 12:16], t)
        t_n = [V.ts(ht[i], X[:, i, :], small[:, 24 + i:25 + i], None, ALU.mult, None, t_cs) for i in range(4)]
        modulation_row(2)
        modulation_columns(1)
        for i in range(4):
            f1(i, ht[i], t_n[i])
        modulation_row(3)
        modulation_columns(2)
        modulation_columns(3)
        ar.top = base + 4096 + 512 + 3 * 512 + 64 + 1024
        XA = ar.get(2064, m=4, s=516)
        XC = ar.get(2048, m=4, s=512)
        dead = Arena(A_, 0)
        dead.top = ar.top
        GA = ar.get(2048, m=4, s=512)
        QT = ar.get(2048, m=4, s=512)
        KT = ar.get(2048, m=4, s=512)
        VN = ar.get(2048, t=4, s=512)
        GB = ar.get(2048, t=4, s=512)
        tm = [ar.get(512) for _ in range(6)]
        LNC = ar.get(LNC_N)
        COS, SIN = ar.get(512), ar.get(512)
        dead.n = ar.top
        d_l = dsem()
        wait_r = [V.last(), A.last(), T.last(), *t_m1]
        t_lnc = G.dma(LNC, T_["lnc"], d_l, *wait_r)
        posb = tm[0].bitcast(I32)
        d_p = dsem()
        t_pos = G.dma(posb, T_["positions"][0, :].partition_broadcast(128), d_p, *wait_r)
        ang, kk_, u_ = tm[1], tm[2], tm[3]
        V.cp(ang, posb, t_pos, *wait_r)
        V.ts(ang, ang, C["invf"], None, ALU.mult, None, t_cst)
        V.ts(kk_, ang, 1.0 / (2 * math.pi), 12582912.0, ALU.mult, ALU.add)
        V.ts(kk_, kk_, -12582912.0, None, ALU.add, None)
        c1 = 6.28125
        c2 = float(np.float32(int((2 * math.pi - c1) * 2 ** 17) / 2 ** 17))
        c3 = float(np.float32(2 * math.pi - c1 - c2))
        for c in (c1, c2, c3):
            V.stt(ang, kk_, -c, ang, ALU.mult, ALU.add)
        V.ts(ang, ang, math.pi, -math.pi, ALU.min, ALU.max)
        t = V.ts(u_, ang, -1.0, None, ALU.mult, None)
        t = V.tt(u_, u_, ang, ALU.max)
        t = V.ts(u_, u_, -1.0, math.pi / 2, ALU.mult, ALU.add)
        t_cos = A.act(COS, u_, ACT.Sin, t)
        t = A.act(SIN, ang, ACT.Sin, t)
        t_rope = V.ts(SIN, SIN, C["sgn"], None, ALU.mult, None, t, t_cos)

        class Behind:

            def __init__(self):
                self.pend = []

            def step(self):
                self.pend = [g for g in self.pend if next(g, 0) != 0]

            def add(self, bi, r):
                self.step()
                if isinstance(r, list):
                    banks.give(bi, *r)
                    return

                def run():
                    banks.give(bi, *(yield from r))
                g = run()
                if next(g, 0) != 0:
                    self.pend.append(g)

            def drain(self):
                while self.pend:
                    self.step()

        behind = Behind()

        def proj_t(ci, n_m, rhs, t_rhs, width, sink):
            ws, wb, wt = chunk(ci)
            w = wb.rearrange("p (k n) -> p k n", k=8)
            toks = []
            for m in range(n_m):
                bi, b, bf = banks.take()
                t = T.mm([(b[:, 0:width], w[:, k, m * 128:(m + 1) * 128], rhs(k), k == 0, k == 7) for k in range(8)],
                         wt, *t_rhs, *bf)
                if m == n_m - 1:
                    W.give(ws, t)
                behind.add(bi, sink(m, b[:, 0:width], t))

        def proj_n(ci, tiles, sink, t_in):
            ws, wb, wt = chunk(ci)
            w = wb.rearrange("p (k n) -> p k n", k=8)
            for i, lhs in enumerate(tiles):
                bi, b, bf = banks.take()
                t = T.mm([(b, lhs(k), w[:, k, :], k == 0, k == 7) for k in range(8)], wt, *t_in, *bf)
                if i == len(tiles) - 1:
                    W.give(ws, t)
                behind.add(bi, sink(i, b, t))

        hr = lambda k: HT[:, k, :]
        t_pad = V.zero(XA[:, :, 0:4])
        toks = {}

        def sink_xa(m, b, t):
            toks["xa", m] = A.act(XA[:, m, 4:516], b, ACT.Copy, t, *wait_r)
            return [toks["xa", m]]

        proj_t(6, 4, hr, t_ht, 512, sink_xa)

        def sink_ga(m, b, t):
            t = A.act(GA[:, m, :], b, ACT.Sigmoid, t, *wait_r)
            toks["ga", m] = V.tt(GA[:, m, :], GA[:, m, :], b, ALU.mult, t)
            return [toks["ga", m]]

        proj_t(7, 4, hr, t_ht, 512, sink_ga)

        def sink_rope(name, dst):
            def f(m, b, t):
                o, raw, tmp = dst[:, m, :], tm[m % 2], tm[2]
                t = V.cp(raw, b, t, T.last())
                yield
                bi, b2, bf = banks.take()
                tp = T.mm([(b2, C["perm1"], raw, True, True)], t, t_cst, *bf)
                V.tt(o, raw, COS, ALU.mult, t_rope)
                t2 = V.tt(tmp, b2, SIN, ALU.mult, tp)
                banks.give(bi, t2)
                toks[name, m] = V.tt(o, o, tmp, ALU.add)
                return [t]
            return f

        proj_t(8, 4, hr, t_ht, 512, sink_rope("q", QT))
        proj_t(9, 4, hr, t_ht, 512, sink_rope("k", KT))
        tl = [lambda k, i=i: HT[:, k, i * 128:(i + 1) * 128] for i in range(4)]

        def sink_v(i, b, t):
            toks["v", i] = A.act(VN[:, i, :], b, ACT.Copy, t, *wait_r)
            return [toks["v", i]]

        proj_n(10, tl, sink_v, t_ht)

        def sink_gb(i, b, t):
            t = A.act(GB[:, i, :], b, ACT.Sigmoid, t, *wait_r)
            toks["gb", i] = V.tt(GB[:, i, :], GB[:, i, :], b, ALU.mult, t)
            return [toks["gb", i]]

        proj_n(11, tl, sink_gb, t_ht)
        behind.drain()

        lws = ar.get(32)
        lw = [lws[:, 4 * i:4 * i + 4] for i in range(8)]
        lam = P["lam"]
        V.ts(lw[0], lam, -1.0, None, ALU.mult, None)
        t = V.tt(lw[1], lam, lw[0], ALU.min)
        t = A.act(lw[2], lw[1], ACT.Exp, t)
        V.ts(lw[3], lw[2], 2.0, None, ALU.add, None, t)
        V.rec(lw[3], lw[3])
        V.tt(lw[2], lw[2], lw[3], ALU.mult)
        V.tt(lw[4], lw[2], lw[2], ALU.mult)
        V.zero(lw[5], value=1.0 / 19)
        for n in range(8, -1, -1):
            V.tt(lw[5], lw[5], lw[4], ALU.mult)
            V.ts(lw[5], lw[5], 1.0 / (2 * n + 1), None, ALU.add, None)
        V.stt(lw[5], lw[5], 2.0, lw[2], ALU.mult, ALU.mult)
        V.stt(lw[5], lw[0], 0.0, lw[5], ALU.max, ALU.add)
        t_sp = V.ts(lw[6], lw[5], 8.0, None, ALU.mult, None)
        t_spn = V.ts(lw[7], lw[5], -8.0, None, ALU.mult, None)
        wbd = r0[:, 0:1024]
        d_w = dsem()
        t_wbd = G.dma(wbd, T_["w_rg"], d_w, *wait_r)
        ada2 = (y for j in range(4, 16) for y in modulation(j, mbank))
        mbank = Slots([banks.bufs[7]])
        mbank.give(0, *banks.free[7])
        lbanks = Slots(banks.bufs[0:7])
        for j in range(7):
            lbanks.give(j, *banks.free[j])
        cw = P["conv_w"]
        for m in range(4):
            xc = XC[:, m, :]
            V.ts(xc, XA[:, m, 1:513], cw[:, m:m + 1], P["conv_b"][:, m:m + 1], ALU.mult, ALU.add, toks["xa", m])
            for k in range(1, 4):
                t_xc = V.stt(xc, XA[:, m, 1 + k:513 + k], cw[:, 4 * k + m:4 * k + m + 1], xc, ALU.mult, ALU.add)
            gates = []
            for j, (bn, tmp) in enumerate((("b_a", tm[0]), ("b_x", tm[1]))):
                bi, b, bf = lbanks.take()
                t = T.mm([(b, wbd[:, (4 * j + m) * 128:(4 * j + m + 1) * 128], xc, True, True)], t_xc, t_wbd, *bf)
                t = A.act(tmp, b, ACT.Sigmoid, t, V.last(), bias=P[bn][:, m:m + 1])
                lbanks.give(bi, t)
            ta = A.act(tm[2], tm[0], ACT.Exp, t_spn, scale=lw[7][:, m:m + 1])
            t_th = A.act(tm[3], tm[0], ACT.Tanh, t_sp, scale=lw[6][:, m:m + 1])
            V.ts(tm[4], tm[3], 1.0, None, ALU.add, None, t_th)
            V.rec(tm[4], tm[4])
            t = V.stt(tm[3], tm[3], 2.0, tm[4], ALU.mult, ALU.mult)
            t = A.act(tm[3], tm[3], ACT.Sqrt, t)
            V.tt(tm[1], tm[1], xc, ALU.mult)
            V.tt(tm[1], tm[1], tm[3], ALU.mult, t)
            V.scan(tm[4], tm[2], tm[1], ta)
            t = V.tt(xc, tm[4], GA[:, m, :], ALU.mult, T.last())
            toks["ya", m] = t
            for _ in range(4):
                next(ada2, None)
        bi, b, bf = lbanks.take()
        for m in range(4):
            t = A.act(tm[m % 2], XC[:, m, :], ACT.Square, toks["ya", 3], T.last())
            t = T.mm([(b, ones, tm[m % 2], m == 0, m == 3)], t, *bf)
        t = A.act(tm[2], b, ACT.Sqrt, t, bias=eps[:, 0:1], scale=1.0 / 512)
        lbanks.give(bi, t)
        t = V.rec(tm[2], tm[2], t)
        t_ya = None
        for m in range(4):
            t_ya = V.stt(XC[:, m, :], XC[:, m, :], P["norm_rec"][:, m:m + 1], tm[2], ALU.mult, ALU.mult)

        sl = [r0[:, 512 * i:512 * (i + 1)] for i in range(8)]
        Sb, Pb, PTb, YB = sl[0:2], [sl[2], sl[3], tm[3]], sl[4:6], sl[6:8]
        free_r0 = [T.last(), A.last()]
        YBT = XA.rearrange("p m s -> p (m s)")[:, 0:2048].rearrange("p (m s) -> p m s", m=4)
        nbb = ar.get(512)
        d_na = dsem()
        t_na = G.dma(nbb, T_["norm_att"].partition_broadcast(128), d_na)
        st = ar.get(64)
        nst = ar.get(64)
        abanks, obanks = Slots(banks.bufs[0:5]), Slots(banks.bufs[5:7])
        for j in range(5):
            abanks.give(j, *lbanks.free[j])
        for j in range(2):
            obanks.give(j, *lbanks.free[5 + j])
        it = [(i, h) for i in range(4) for h in range(8)]
        tS, tP, tPT = {}, {}, {}
        obank = {}
        q_all = [toks["q", m] for m in range(4)] + [toks["k", m] for m in range(4)] + [toks["v", i] for i in range(4)]

        def scores(x):
            i, h = it[x]
            n = 128 * (i + 1)
            hb, m = 64 * (h % 2), h // 2
            bi, b, bf = abanks.take()
            t = T.mm([(b[:, 0:n], QT[hb:hb + 64, m, i * 128:(i + 1) * 128], KT[hb:hb + 64, m, 0:n], True, True)],
                     *q_all, *bf)
            s, p = Sb[x % 2], Pb[x % 3]
            o = LNC_OFF[i]
            t = V.stt(s[:, 0:n], b[:, 0:n], 0.125, LNC[:, o:o + n], ALU.mult, ALU.add, t, t_lnc, tP.get(x - 2), *free_r0)
            abanks.give(bi, t)
            t = V.red(st[:, x % 2:x % 2 + 1], s[:, 0:n], ALU.max, negate=True)
            tP[x] = A.act(p[:, 0:n], s[:, 0:n], ACT.Exp, t, tPT.get(x - 3), bias=st[:, x % 2:x % 2 + 1],
                          accum_out=st[:, 8 + 8 * (i % 2) + h:9 + 8 * (i % 2) + h])

        def turn(x):
            i, h = it[x]
            n = 128 * (i + 1)
            bi, b, bf = abanks.take()
            t = T.tr([(b[:, j * 128:(j + 1) * 128], Pb[x % 3][:, j * 128:(j + 1) * 128]) for j in range(i + 1)],
                     ident, tP[x], *bf)
            tPT[x] = t
            tS[x] = A.act(PTb[x % 2][:, 0:n], b[:, 0:n], ACT.Copy, t, obank.get(("pv", x - 2)))
            abanks.give(bi, tS[x])

        def pv(x):
            i, h = it[x]
            if h == 0:
                obank[i] = obanks.take()
            bi, b, bf = obank[i]
            t = T.mm([(b[:, h * 64:(h + 1) * 64], PTb[x % 2][:, j * 128:(j + 1) * 128], VN[:, j, h * 64:(h + 1) * 64],
                       j == 0, j == i) for j in range(i + 1)], tS[x], *bf)
            obank["pv", x] = t
            if h == 7:
                ri = st[:, 24 + 8 * (i % 2):32 + 8 * (i % 2)]
                V.rec(ri, st[:, 8 + 8 * (i % 2):16 + 8 * (i % 2)], tP[x])
                y = YB[i % 2]
                t = V.tt(y.rearrange("p (h d) -> p h d", h=8), b.rearrange("p (h d) -> p h d", h=8), bc(ri, 64),
                         ALU.mult, t, obank.get(("yt", i - 2)))
                obanks.give(bi, t)
                t = V.tt(y, y, GB[:, i, :], ALU.mult)
                t = A.act(tm[0], y, ACT.Square, t, V.last(), accum_out=st[:, 40 + i:41 + i])
                t = A.act(st[:, 44 + i:45 + i], st[:, 40 + i:41 + i], ACT.Sqrt, bias=eps[:, 0:1], scale=1.0 / 512)
                t = V.rec(st[:, 48 + i:49 + i], st[:, 44 + i:45 + i], t)
                t = V.stt(y, y, st[:, 48 + i:49 + i], nbb, ALU.mult, ALU.mult, t_na)
                late.append((i, y, t))

        def gated_out():
            while late:
                i, y, t = late.pop()
                b2i, b2, b2f = abanks.take()
                t = T.tr([(b2[:, q * 128:(q + 1) * 128], y[:, q * 128:(q + 1) * 128]) for q in range(4)], ident, t, *b2f)
                obank["yt", i] = t
                t = V.cp(YBT[:, :, i * 128:(i + 1) * 128], b2.rearrange("p (q s) -> p q s", q=4), t)
                obank["y", i] = t
                abanks.give(b2i, t)

        late = []
        for x in range(len(it) + 3):
            if x < len(it):
                scores(x)
            if 0 <= x - 2 < len(it):
                turn(x - 2)
            next(ada2, None)
            if x % 8 == 4:
                gated_out()
            if 0 <= x - 3 < len(it):
                pv(x - 3)
        gated_out()
        for _ in ada2:
            pass

        banks.free, banks.i = [*abanks.free, *obanks.free, *mbank.free], 0

        wo = [chunk(12), chunk(13)]
        fA = [T.last(), V.last(), A.last()]
        G1, np_, gsc, shc, n1, gs, sh, sqb = [dead.get(1024) for _ in range(8)]
        msb, ht = [dead.get(1024) for _ in range(2)], [dead.get(1024) for _ in range(2)]
        CX = dead.get(2048, t=2, d=1024)
        HCT = r0[:, 0:2048].rearrange("p (k s) -> p k s", k=8)
        d_g1, d_n1, d_n3 = dsem(), dsem(), dsem()
        t1 = G.dma(G1, mods1[2048:3072].partition_broadcast(128), d_g1, *t_m1, *fA)
        t1 = G.dma(np_, T_["norm_post"].partition_broadcast(128), d_g1, *fA)
        row = lambda v, i: mods2[v, i * 1024:(i + 1) * 1024].partition_broadcast(128)
        for dst, src in ((CX, T_["ctx_2"].rearrange("o (t p) d -> p (o t) d", p=128)), (shc, row(1, 0)), (gsc, row(1, 1)),
                         (n1, T_["norm1_g_2"].partition_broadcast(128))):
            t2 = Y.dma(dst, src, d_n1, *t_m2, *fA)
        for dst, src in ((sh, row(0, 0)), (gs, row(0, 1))):
            t3 = Y.dma(dst, src, d_n3, *t_m2, *fA)
        t_gp = V.tt(G1, G1, np_, ALU.mult, t1)
        t_x1, t_tr, used = [], {}, [None, None]
        f2, f3 = transposed(HCT, fA), transposed(HT, fA)

        def rms(x, q, t, n):
            t = A.act(q, x, ACT.Square, t, accum_out=nst[:, n:n + 1])
            t = A.act(nst[:, 16 + n:17 + n], nst[:, n:n + 1], ACT.Sqrt, bias=eps[:, 0:1], scale=1.0 / D)
            V.rec(nst[:, 32 + n:33 + n], nst[:, 16 + n:17 + n], t)
            return nst[:, 32 + n:33 + n]

        def normed(x, t, n, g, b):
            h = ht[len(t_tr) % 2]
            r = rms(x, sqb, t, n)
            V.stt(h, x, r, g, ALU.mult, ALU.mult, used[len(t_tr) % 2], t3)
            t_tr[n] = (h, V.tt(h, h, b, ALU.add))

        def turned(n):
            h, t = t_tr[n]
            used[list(t_tr).index(n) % 2] = f3(n, h, t) if n < 4 else f2(n - 4, h, t)

        for i in range(4):
            bb = []
            for hf in range(2):
                ws, wb, wt = wo[hf]
                w = wb.rearrange("p (k n) -> p k n", k=8)
                bi, b, bf = banks.take()
                g = []
                for k in range(8):
                    lhs = (XC if k < 4 else YBT)[:, k % 4, i * 128:(i + 1) * 128]
                    g.append((b, lhs, w[:, k, :], k == 0, k == 7))
                t = T.mm(g, wt, obank["y", i], t_ya, *bf)
                if i == 3:
                    W.give(ws, t)
                bb.append((bi, b, t))
            if i == 1:
                turned(0)
            elif i == 2:
                turned(4)
                turned(1)
            elif i == 3:
                turned(5)
                turned(2)
            mx = msb[i % 2]
            te = []
            for hf, eng in ((0, A), (1, V)):
                bi, b, t = bb[hf]
                o = mx[:, hf * 512:(hf + 1) * 512]
                prev = t_x1[i - 2] if i > 1 else None
                te.append(A.act(o, b, ACT.Copy, t, prev, *fA) if hf == 0 else V.cp(o, b, t, *fA))
                banks.give(bi, te[-1])
            r = rms(mx, sqb, te[1], 8 + i)
            V.stt(mx, mx, r, G1, ALU.mult, ALU.mult)
            t_x1.append(V.tt(X[:, i, :], X[:, i, :], mx, ALU.add))
            if i == 0:
                V.stt(gs, gs, 1.0, n1, ALU.add, ALU.mult, t2, t3)
                V.stt(gsc, gsc, 1.0, n1, ALU.add, ALU.mult)
            normed(X[:, i, :], t_x1[i], i, gs, sh)
            if i in (1, 2):
                normed(CX[:, i - 1, :], t2, 3 + i, gsc, shc)
        for j in (16, 17):
            for _ in modulation(j, banks):
                pass
        turned(3)
        t_h2 = f2.done + f3.done

        def fence():
            return [T.last(), V.last(), A.last(), G.last()]

        ar.top = base
        ar.get(2048)
        small = ar.get(64)
        mark2 = ar.top
        f = fence() + t_m2

        TB = ar.get(NROPE)
        d_tb = dsem()
        t_tb = G.dma(TB, T_["ropes"], d_tb, *f)
        RP = {n: TB[:, a:b] for n, (a, b) in ROPES.items()}
        PW = ar.get(512, g=4, d=128)
        t_tb = G.dma(PW, T_["pool_w_2"][0].rearrange("g c d -> c g d"), d_tb, *f)
        lqb = ar.get(256)
        t_tb = G.dma(lqb, T_["lambda_qk_2"][0].rearrange("a b -> (a b)").partition_broadcast(128), d_tb, *f)
        SUB = ar.get(512)
        t_tb = G.dma(SUB, T_["subln"].partition_broadcast(128), d_tb, *f)
        mark3 = ar.top
        PP = ar.get(4 * 528, m=4, s=528)
        pt = [ar.get(528) for _ in range(2)]
        B0 = ar.get(2048, m=4, s=512)
        t_z = V.zero(PP, *f)
        hl = lambda k: HT[:, k, :]
        hc = lambda k: HCT[:, k, :]
        t_b0 = []
        pmm = [None]

        def sink_pool(m, b, t):
            w = 2 << m
            u = PP[:, m, :]
            tA = A.act(u[:, 8:520], b, ACT.Copy, t, t_z)
            src, step = u, 1
            n = 528
            j = 0
            while step < w:
                dst = pt[j % 2]
                n2 = n - step
                V.tt(dst[:, 0:n2], src[:, 0:n2], src[:, step:step + n2], ALU.add, tA, pmm[0])
                src, n, step, j = dst, n2, step * 2, j + 1
            o = 8 - w // 2
            dst = pt[j % 2]
            V.tt(dst[:, 0:512], src[:, o:o + 512], RP["cnt"][:, m * 512:(m + 1) * 512], ALU.mult, t_tb)
            t = V.tt(dst[:, 0:512], dst[:, 0:512], u[:, 8:520], ALU.subtract)
            yield
            bi, b2, bf = banks.take()
            pmm[0] = t = T.mm([(b2, PW[:, m, :], dst[:, 0:512], True, True)], t, t_tb, *bf)
            t = V.ts(B0[:, m, :], b2, P["pscale"][:, m:m + 1], None, ALU.mult, None, t)
            banks.give(bi, t)
            t_b0.append(t)
            return [tA]

        d_sp = dsem()
        G.dma(xd, X.rearrange("p t d -> p (t d)"), d_sp, *t_x1)
        t_xd = G.dma(htd, HT.rearrange("p k s -> p (k s)"), d_sp, *t_h2)
        proj_t(26, 4, hl, t_h2, 512, sink_pool)
        V.tt(lqb[:, 0:64], lqb[:, 0:64], lqb[:, 64:128], ALU.mult, t_tb)
        V.tt(lqb[:, 128:192], lqb[:, 128:192], lqb[:, 192:256], ALU.mult)
        V.red(small[:, 40:41], lqb[:, 0:64], ALU.add)
        t = V.red(small[:, 41:42], lqb[:, 128:192], ALU.add)
        t = A.act(small[:, 42:44], small[:, 40:42], ACT.Exp, t)
        V.tt(lamc, small[:, 42:43], small[:, 43:44], ALU.subtract, t)
        V.ts(lamc, lamc, 0.8 - 0.6 * math.exp(0.0), None, ALU.add, None)

        ar.top = mark3 + 4 * 528 + 2 * 528 + 2048
        QT = ar.get(2048, m=4, s=512)
        KT = ar.get(4 * 768, m=4, s=768)
        VN = ar.get(6 * 512, t=6, s=512)
        tm = [ar.get(512) for _ in range(4)]
        toks = {}

        def qk_norm(b, t, n, g, raw, sq):
            t1 = A.act(sq[:, 0:n], b, ACT.Square, t, *f, V.last(), T.last())
            yield
            bi, b2, bf = banks.take()
            t2 = T.mm([(b2[:, 0:n], C["blk64"], sq[:, 0:n], True, True)], t1, *bf)
            t3 = A.act(sq[:, 0:n], b2[:, 0:n], ACT.Sqrt, t2, bias=eps[:, 0:1], scale=1.0 / 64)
            banks.give(bi, t3)
            V.rec(sq[:, 0:n], sq[:, 0:n], t3)
            return V.stt(raw, b, g, sq[:, 0:n], ALU.mult, ALU.mult, t, T.last(), *f)

        def sink_qk(name, dst, col, off):
            def fn(m, b, t):
                n1_, n2_ = tm[2 * (m % 2)], tm[2 * (m % 2) + 1]
                t0 = yield from qk_norm(b, t, 512, col, n1_, n2_)
                yield
                bi, b2, bf = banks.take()
                tp = T.mm([(b2, C["perm2"], n1_, True, True)], t0, *bf)
                o = dst[:, m, off:off + 512]
                V.tt(o, n1_, RP["cos2"], ALU.mult, t_tb)
                t2 = V.tt(n2_, b2, RP["sin2"], ALU.mult, tp)
                banks.give(bi, t2)
                toks[name, m] = V.tt(o, o, n2_, ALU.add)
                return [t0]
            return fn

        proj_t(27, 4, hl, t_h2, 512, sink_qk("q", QT, P["qn"], 0))
        d_br = dsem()
        t_brd = G.dma(brd[0], B0.rearrange("p m s -> p (m s)"), d_br, *t_b0)


        ws, wb, wt = chunk(28)
        w = wb.rearrange("p (k n) -> p k n", k=8)
        sk = sink_qk("k", KT, P["kn"], 256)

        def context_k(m, b, t):
            toks["kc", m] = yield from qk_norm(b, t, 256, P["kn"], KT[:, m, 0:256], tm[2 * (m % 2)])
            return [toks["kc", m]]

        for m in range(4):
            bi, b, bf = banks.take()
            t = T.mm([(b[:, 0:256], w[:, k, m * 128:(m + 1) * 128], hc(k), k == 0, k == 7) for k in range(8)], wt, *t_h2, *bf)
            behind.add(bi, context_k(m, b[:, 0:256], t))
            bi, b, bf = banks.take()
            t = T.mm([(b, w[:, k, m * 128:(m + 1) * 128], hl(k), k == 0, k == 7) for k in range(8)], *bf)
            if m == 3:
                W.give(ws, t)
            behind.add(bi, sk(m, b, t))
        tl6 = [lambda k, i=i: HCT[:, k, i * 128:(i + 1) * 128] for i in range(2)] + \
              [lambda k, i=i: HT[:, k, i * 128:(i + 1) * 128] for i in range(4)]

        def sink_v2(i, b, t):
            toks["v", i] = A.act(VN[:, i, :], b, ACT.Copy, t, *f)
            return [toks["v", i]]

        proj_n(29, tl6, sink_v2, t_h2)
        behind.drain()
        ar2 = ar.top
        ar.top = mark3
        f4 = fence() + [t_brd]
        Pm = [[ar.get(768) for _ in range(2)] for _ in range(2)]
        AT = [ar.get(768) for _ in range(2)]
        ATN = [tm[0], tm[1]]
        assert ar.top <= mark3 + 4 * 528 + 2 * 528 + 2048
        ar.top = ar2
        B1 = ar.get(2048, m=4, s=512)
        st = ar.get(64)
        Pm.append([ar.get(768) for _ in range(2)])
        it = [(i, h) for i in range(4) for h in range(4)]
        spair = Slots([PSUM[:, 0:2, :].rearrange("p a b -> p (a b)"), PSUM[:, 2:4, :].rearrange("p a b -> p (a b)")])
        tpair = Slots([PSUM[:, 4:6, :].rearrange("p a b -> p (a b)")])
        for j in range(2):
            spair.give(j, *banks.free[2 * j], *banks.free[2 * j + 1])
        tpair.give(0, *banks.free[4], *banks.free[5])
        fp = f4
        qkv = list(toks.values())
        tA, tTR, tAT, tPV, tE = {}, {}, {}, {}, {}

        def d_scores(x):
            i, h = it[x]
            o = 4 * (x % 2)
            for mp in range(2):
                bi, b, bf = spair.take()
                lhs = QT[64 * mp:64 * mp + 64, h, i * 128:(i + 1) * 128]
                t = T.mm([(b[:, 0:512], lhs, KT[64 * mp:64 * mp + 64, h, 0:512], True, True),
                          (b[:, 512:768], lhs, KT[64 * mp:64 * mp + 64, h, 512:768], True, True)], *qkv, *bf)
                V.red(st[:, o + mp:o + mp + 1], b[:, 0:768], ALU.max, t, tE.get((x - 2, mp)))
                t = V.ts(st[:, o + mp:o + mp + 1], st[:, o + mp:o + mp + 1], -0.125, None, ALU.mult, None)
                t = A.act(Pm[x % 3][mp], b[:, 0:768], ACT.Exp, t, *fp, tTR.get(x - 3), bias=st[:, o + mp:o + mp + 1],
                          scale=0.125, accum_out=st[:, 8 + o + mp:9 + o + mp])
                spair.give(bi, t)
                tE[x, mp] = t

        def d_mix(x):
            o = 4 * (x % 2)
            rc = st[:, 16 + o:18 + o]
            V.rec(rc, st[:, 8 + o:10 + o], tE[x, 1])
            V.tt(rc[:, 1:2], rc[:, 1:2], lamc, ALU.mult)
            V.ts(Pm[x % 3][1], Pm[x % 3][1], rc[:, 1:2], None, ALU.mult, None)
            tA[x] = V.stt(Pm[x % 3][0], Pm[x % 3][0], rc[:, 0:1], Pm[x % 3][1], ALU.mult, ALU.subtract)

        def d_turn(x):
            bi, b, bf = tpair.take()
            t = T.tr([(b[:, j * 128:(j + 1) * 128], Pm[x % 3][0][:, j * 128:(j + 1) * 128]) for j in range(6)], ident, tA[x], *bf)
            tTR[x] = t
            tAT[x] = A.act(AT[x % 2], b[:, 0:768], ACT.Copy, t, *fp, tPV.get(x - 2))
            tpair.give(bi, tAT[x])

        ob = Slots([PSUM[:, 6, :]])
        tb = Slots([PSUM[:, 7, :]])
        ob.give(0, *banks.free[6])
        tb.give(0, *banks.free[7])
        t_b1 = []
        hold = {}

        def d_pv(x):
            i, h = it[x]
            if h == 0:
                hold["o"] = ob.take()
            bi, b, bf = hold["o"]
            tPV[x] = t = T.mm([(b[:, h * 128:(h + 1) * 128], AT[x % 2][:, j * 128:(j + 1) * 128],
                                VN[:, j, h * 128:(h + 1) * 128], j == 0, j == 5) for j in range(6)], tAT[x], *bf)
            if h == 3:
                y, sq = ATN[i % 2], tm[2]
                t = A.act(y, b, ACT.Copy, t, hold.get(i - 2), V.last())
                ob.give(0, t)
                for q in range(4):
                    qs = slice(128 * q, 128 * q + 128)
                    A.act(sq[:, qs], y[:, qs], ACT.Square, accum_out=st[:, 32 + q:33 + q])
                t = A.act(st[:, 36:40], st[:, 32:36], ACT.Sqrt, bias=eps[:, 0:1], scale=1.0 / 128)
                V.rec(st[:, 40:44], st[:, 36:40], t)
                V.tt(y.rearrange("p (h d) -> p h d", h=4), y.rearrange("p (h d) -> p h d", h=4), bc(st[:, 40:44], 128), ALU.mult)
                t = V.stt(y, y, 1.0 - (0.8 - 0.6 * math.exp(0.0)), SUB, ALU.mult, ALU.mult)
                late.append((i, y, t))

        def mixed_out():
            while late:
                i, y, t = late.pop()
                b2i, b2, b2f = tb.take()
                t = T.tr([(b2[:, q * 128:(q + 1) * 128], y[:, q * 128:(q + 1) * 128]) for q in range(4)], ident, t, *b2f)
                hold[i] = t
                t = V.cp(B1[:, :, i * 128:(i + 1) * 128], b2.rearrange("p (q s) -> p q s", q=4), t)
                tb.give(0, t)
                t_b1.append(t)

        for x in range(len(it) + 3):
            if x < len(it):
                d_scores(x)
            if 0 <= x - 1 < len(it):
                d_mix(x - 1)
            if 0 <= x - 2 < len(it):
                d_turn(x - 2)
            if x % 4 == 0:
                mixed_out()
            if 0 <= x - 3 < len(it):
                d_pv(x - 3)
        mixed_out()
        t_brd = G.dma(brd[1], B1.rearrange("p m s -> p (m s)"), d_br, *t_b1)

        f = fence() + [t_brd, t_xd]
        banks.free = [*[fr for fr in spair.free for _ in range(2)], *[tpair.free[0]] * 2, ob.free[0], tb.free[0]]
        ar.top = mark2
        R = ar.get(2048, m=4, s=512)
        K = ar.get(3072, m=4, s=768)
        VR = ar.get(3072, t=6, s=512)
        WL, AL = ar.get(768), ar.get(768)
        SG = ar.get(512)
        KK = ar.get(3072, m=4, s=768)
        YS = ar.get(2048, t=4, s=512)
        W2, A2, G2 = ar.get(512), ar.get(512), ar.get(512)
        mk_top = ar.top
        MK = ar.get(NMASK)
        IRK = ar.get(32, m=4, h=8)
        COEF = ar.get(32, t=4, h=8)
        STG = ar.get(64)
        MM = {n: MK[:, a:b] for n, (a, b) in MASKS.items()}
        d_rw = dsem()
        for dst, n in ((W2, "decay_w2"), (A2, "aaa_a2"), (G2, "gate_w2"), (MK, "masks")):
            t_rw = G.dma(dst, T_[n], d_rw, *f)
        V.tt(IRK, C["ind"].rearrange("p (m h) -> p m h", m=4), bc(P["r_k"], 8), ALU.mult, *f)
        mark4 = ar.top
        PR = [ar.get(772) for _ in range(2)]
        vt = [ar.get(768) for _ in range(2)]
        kt = [ar.get(768) for _ in range(2)]
        m01 = ar.get(16)
        t_pz = None
        for z in PR:
            t_pz = V.zero(z, *f)
        V.tt(m01[:, 0:15], P["mu0"], P["mu1"], ALU.add)
        V.ts(m01[:, 0:15], m01[:, 0:15], -1.0, 1.0, ALU.mult, ALU.add)
        shifted = {}
        rd = [None, None]
        ti = 0

        def values(fi, ti, v_, t):
            for hf in range(2):
                nb_ = 4 if hf == 0 else 2
                bi, b, bf = banks.take()
                t2 = T.tr([(b[:, q * 128:(q + 1) * 128], v_[:, (4 * hf + q) * 128:(4 * hf + q + 1) * 128])
                           for q in range(nb_)], ident, t, *bf)
                t3 = A.act(VR[:, 4 * hf:4 * hf + nb_, (fi - 8) * 128:(fi - 7) * 128],
                           b[:, 0:nb_ * 128].rearrange("p (q s) -> p q s", q=nb_), ACT.Copy, t2, *f)
                banks.give(bi, t3)
                shifted["vt%d" % (ti % 2)] = t2
                shifted["vr", fi, hf] = t3
            return
            yield

        def keys(m, t):
            kc, q_ = KK[:, m, :], kt[m % 2]
            t_k = V.ts(kc, K[:, m, :], P["k_k"][:, m:m + 1], None, ALU.mult, None, t, *f)
            t = A.act(q_, kc, ACT.Square, t_k, V.last())
            yield
            for o, n in ((0, 512), (512, 256)):
                bi, b, bf = banks.take()
                t2 = T.mm([(b[:, 0:n], C["blk64"], q_[:, o:o + n], True, True)], t, *bf)
                t2 = A.act(q_[:, o:o + n], b[:, 0:n], ACT.Sqrt, t2, bias=eps[:, 2:3])
                banks.give(bi, t2)
            V.ts(q_, q_, 1e-12, None, ALU.max, None, t2)
            V.rec(q_, q_)
            V.tt(kc, kc, q_, ALU.mult)

        for ci, n_m, f0 in ((30, 4, 0), (31, 4, 4), (32, 4, 8), (33, 3, 12)):
            ws, wb, wt = chunk(ci)
            w = wb.rearrange("p (k n) -> p k n", k=8)
            for m in range(n_m):
                fi = f0 + m
                pr = PR[ti % 2]
                has_c = fi not in (0, 1, 2, 3, 14)
                tc = None
                if has_c:
                    bi, b, bf = banks.take()
                    t = T.mm([(b[:, 0:256], w[:, k, m * 128:(m + 1) * 128], hc(k), k == 0, k == 7) for k in range(8)], wt, *bf)
                    tc = A.act(pr[:, 1:257], b[:, 0:256], ACT.Copy, t, t_pz, rd[ti % 2])
                    banks.give(bi, tc)
                bi, b, bf = banks.take()
                t = T.mm([(b, w[:, k, m * 128:(m + 1) * 128], hl(k), k == 0, k == 7) for k in range(8)], wt, *bf)
                if m == n_m - 1:
                    W.give(ws, t)
                behind.step()
                tl_ = A.act(pr[:, 258:770], b, ACT.Copy, t, t_pz, rd[ti % 2])
                banks.give(bi, tl_)
                if fi < 4:
                    dl, dc = R[:, fi, :], None
                elif fi < 8:
                    dl, dc = K[:, fi - 4, 256:768], K[:, fi - 4, 0:256]
                elif fi < 12:
                    v_ = vt[ti % 2]
                    dl, dc = v_[:, 256:768], v_[:, 0:256]
                elif fi < 14:
                    q_ = (WL, AL)[fi - 12]
                    dl, dc = q_[:, 256:768], q_[:, 0:256]
                else:
                    dl, dc = SG, None
                wv = shifted.get("vt%d" % (ti % 2)) if 8 <= fi < 12 else None
                for dst, o, n in ((dl, 258, 512), (dc, 1, 256)):
                    if dst is None:
                        continue
                    V.ts(dst, pr[:, o:o + n], m01[:, fi:fi + 1], None, ALU.mult, None, tl_, tc, wv)
                    V.stt(dst, pr[:, o - 1:o - 1 + n], P["mu0"][:, fi:fi + 1], dst, ALU.mult, ALU.add)
                    t = V.stt(dst, pr[:, o + 1:o + 1 + n], P["mu1"][:, fi:fi + 1], dst, ALU.mult, ALU.add)
                rd[ti % 2] = t
                if 4 <= fi < 8:
                    g = keys(fi - 4, t)
                    next(g)
                    behind.pend.append(g)
                if 8 <= fi < 12:
                    behind.pend.append(values(fi, ti, v_, t))
                ti += 1
        behind.drain()
        t = V.last()
        t_wl = A.act(WL, WL, ACT.Tanh, t)
        t_sg = A.act(SG, SG, ACT.Sigmoid, t)
        t_vr = [v for k_, v in shifted.items() if isinstance(k_, tuple)]
        def region(a, b):
            r = Arena(A_, b)
            r.top = a
            return r

        def place(first, w, **dims):
            for r in (*first, ar):
                if r.top + w <= r.n:
                    return r.get(w, **dims)
            raise AssertionError("no room")

        f6 = f5 = fence() + t_vr + [t_wl, t_sg, t_rw]
        opened = set()
        ends_of = {}
        row3 = lambda o: K[:, :, o:o + 128]
        GW, GBi, t_gn = row3(0), row3(128), []
        t_b2 = []
        B2 = R

        def finish(c, ring, q_, st, t):
            i = c - 2
            if not t_gn:
                for dst, n in ((GW, "gn_w_2"), (GBi, "gn_b_2")):
                    t_gn[:] = [Y.dma(dst, T_[n][0, :].partition_broadcast(128).rearrange("p (m s) -> p m s", m=4), d_gn, V.last())]
            y = YS[:, i, :]
            y3, y4, q3 = [a.rearrange("p (h d) -> p h d", h=n) for a, n in ((y, 8), (y, 4), (q_, 8))]
            V.red(st[:, 0:8], y3, ALU.add)
            V.ts(st[:, 0:8], st[:, 0:8], 1.0 / 64, None, ALU.mult, None)
            V.tt(y3, y3, bc(st[:, 0:8], 64), ALU.subtract)
            yield
            V.tt(q3, y3, y3, ALU.mult, t)
            t = V.red(st[:, 8:16], q3, ALU.add)
            t = A.act(st[:, 16:24], st[:, 8:16], ACT.Sqrt, t, bias=eps[:, 1:2], scale=1.0 / 64)
            yield
            V.rec(st[:, 24:32], st[:, 16:24], t)
            V.tt(y3, y3, bc(st[:, 24:32], 64), ALU.mult)
            V.tt(y4, y4, GW, ALU.mult, *t_gn)
            yield
            V.tt(y4, y4, GBi, ALU.add)
            V.tt(q3, VR[:, c, :].rearrange("p (h d) -> p h d", h=8), bc(COEF[:, i, :], 64), ALU.mult)
            V.tt(y, y, q_, ALU.add)
            yield
            bi, b, bf = ring.take()
            t = T.mm([(b, SG[:, i * 128:(i + 1) * 128], G2, True, True)], t_sg, t_rw, *bf)
            t_y = V.tt(y, y, b, ALU.mult, t)
            ring.give(bi, t_y)
            yield
            bi, b, bf = ring.take()
            t = T.tr([(b[:, q * 128:(q + 1) * 128], y[:, q * 128:(q + 1) * 128]) for q in range(4)], ident, t_y, *bf)
            t = A.act(B2[:, :, i * 128:(i + 1) * 128], b.rearrange("p (q s) -> p q s", q=4), ACT.Copy, t, t_y)
            ring.give(bi, t)
            t_b2.append(t)
            yield

        d_gn = dsem()
        last_one = []

        def accumulate(key, dst, b, t):
            if key in opened:
                return V.tt(dst, dst, b, ALU.add, t)
            opened.add(key)
            return V.cp(dst, b, t)

        def recurrence(d, region, ring):
            g_ = lambda w, **dims: place(region, w, **dims)
            GBm, GKm = g_(2048, h=8, n=256), g_(2048, h=8, n=256)
            AR = g_(1024, m=4, j=2, s=128)
            KB = g_(1024, j=2, m=4, s=128)
            KNB = g_(1024, j=2, n=512)
            TI, TT, NL, XB = [g_(1024, h=8, n=128) for _ in range(4)]
            tmp = [g_(512, m=4, s=128) for _ in range(5)]
            MS, MP = [g_(512, m=4, v=128) for _ in range(2)]
            X0, SA = g_(512), g_(512)
            DDs = [ar.get(4) for _ in range(2)]
            stg = STG[:, 32 * d:32 * d + 32]
            sig, ag, L, ex, e2 = tmp
            t_z = [G.zero(GBm, *f6), G.zero(GKm), V.zero(MS, *f6)]
            tri_i = MM["si%d" % d].bitcast(U32)
            lmT = lambda lv: bm(MM["lm%d" % (1 - d)][:, lv * 128:(lv + 1) * 128], 4)
            order = ([0, 1, 2, 3, 4, 5], [1, 0, 5, 4, 3, 2])[d]
            pe_prev, t_d = None, {}
            u = {"prep": None, "co": None, "kb": None, "x0": None}

            def prepare(n):
                c = order[n]
                cs_ = slice(c * 128, (c + 1) * 128)
                DD = DDs[n % 2]
                for dst, wgt, lo, b0 in ((sig, W2, WL, "w0"), (ag, A2, AL, "a0")):
                    bi, b, bf = ring.take()
                    t = T.mm([(b[:, m * 128:(m + 1) * 128], wgt[64 * d:64 * d + 64, m * 128:(m + 1) * 128],
                               lo[64 * d:64 * d + 64, cs_], True, True) for m in range(4)], *f6, *bf)
                    for m in range(4):
                        t = A.act(dst[:, m, :], b[:, m * 128:(m + 1) * 128], ACT.Sigmoid, t, u["prep"], *f6,
                                  bias=P[b0][:, 4 * d + m:4 * d + m + 1])
                    ring.give(bi, t)
                    yield
                for m in range(4):
                    if d == 0:
                        V.scan(L[:, m, :], ones, sig[:, m, :], t)
                    else:
                        V.scan(L[:, m, ::-1], ones, sig[:, m, ::-1], t)
                    if m == 1:
                        yield
                yield
                tot = L[:, :, 127:128] if d == 0 else L[:, :, 0:1]
                V.cp(DD.unsqueeze(2), tot)
                t_dd = V.cp(ex[:, :, 0:1], tot)
                t_d[n] = A.act(DD, DD, ACT.Exp, t_dd, scale=-0.5 * KAPPA)
                V.stt(L, ex[:, :, 0:1].broadcast_to([128, 4, 128]), -0.5, L, ALU.mult, ALU.add)
                t = V.tt(sig, L, sig, ALU.subtract)
                yield
                t = A.act(ex, L, ACT.Exp, t, scale=KAPPA)
                t = A.act(L, L, ACT.Exp, t, scale=-KAPPA)
                u["e"] = A.act(sig, sig, ACT.Exp, t, scale=-KAPPA)
                yield
                V.stt(e2, ag, -1.0, bc(P["k_a"], 128), ALU.add, ALU.mult, u["co"])
                V.stt(e2, e2, 1.0, K[:, :, cs_], ALU.add, ALU.mult)
                yield
                V.tt(ag, ag, KK[:, :, cs_], ALU.mult)
                V.tt(KB[:, 1], ag, ex, ALU.mult, u["e"], u["kb"])
                yield
                V.tt(KB[:, 0], e2, ex, ALU.mult)
                V.stt(AR[:, :, 0, :], KK[:, :, cs_], -1.0, sig, ALU.mult, ALU.mult, u["x0"])
                yield

            for _ in prepare(0):
                yield
            for n, c in enumerate(order):
                lat = c >= 2
                cs_ = slice(c * 128, (c + 1) * 128)
                ls = slice((c - 2) * 128, (c - 1) * 128)
                DD, t_D = DDs[n % 2], t_d[n]
                ahead = prepare(n + 1) if n < 5 else iter(())
                if lat:
                    V.tt(AR[:, :, 1, :], R[:, :, ls], L, ALU.mult, pe_prev)
                t_ar = V.last()
                t_mp = V.tt(MP, MS, bc(DD, 128), ALU.mult, t_D, pe_prev)
                u["prep"] = t_mp
                if lat:
                    u["prep"] = V.tt(e2, e2, R[:, :, ls], ALU.mult)
                w_ = 256 if lat else 128
                tG = {}
                for nm, buf, j in (("b", GBm, 1), ("k", GKm, 0)):
                    for g in range(2):
                        for q in range(2):
                            bi, b, bf = ring.take()
                            bv = b[:, 0:2 * w_].rearrange("p (h n) -> p h n", h=2)
                            grp = []
                            for n_ in range(2):
                                m = 2 * g + n_
                                rhs = AR[64 * q:64 * q + 64, m, :, :].rearrange("p j s -> p (j s)")[:, 0:w_]
                                grp.append((bv[:, n_, :], KB[64 * q:64 * q + 64, j, m, :], rhs, True, True))
                            t = T.mm(grp, t_ar, *bf)
                            t = V.pred(buf[:, 4 * g + q:4 * g + 4:2, 0:w_], bm(tri_i[:, 0:w_], 2), bv, t, pe_prev, *t_z)
                            ring.give(bi, t)
                            tG[nm, g] = t
                        yield
                tT, tTT, tN = {}, {}, {}
                for g in range(2):
                    hs = slice(4 * g, 4 * g + 4)
                    V.tt(TT[:, hs, :], GBm[:, hs, 0:128], lmT(0), ALU.mult, pe_prev)
                    tTT[g] = V.tt(TT[:, hs, :], TT[:, hs, :], bm(ident, 4), ALU.add)
                    tN[g] = G.tt(NL[:, hs, :], GBm[:, hs, 0:128], lmT(1), ALU.mult, tG["b", g], pe_prev)
                    bi, b, bf = ring.take()
                    t = T.tr([(b[:, n_ * 128:(n_ + 1) * 128], TT[:, 4 * g + n_, :]) for n_ in range(4)], ident, tTT[g], *bf)
                    tT[g] = A.act(TI[:, hs, :], b.rearrange("p (h n) -> p h n", h=4), ACT.Copy, t, pe_prev)
                    ring.give(bi, tT[g])
                yield
                bi, b, bf = ring.take()
                grp = []
                for m in range(4):
                    grp.append((b[:, m * 128:(m + 1) * 128], AR[:, m, 0, :], MP[:, m, :], True, False))
                    for h in (2 * m, 2 * m + 1):
                        grp.append((b[:, h * 64:(h + 1) * 64], GKm[:, h, 0:128], VR[:, c, h * 64:(h + 1) * 64],
                                    False, h % 2 == 1))
                u["x0"] = t = T.mm(grp, t_mp, tG["k", 0], tG["k", 1], *bf)
                t_x0 = A.act(X0, b, ACT.Copy, t, pe_prev)
                ring.give(bi, t_x0)
                tU = {}
                for lv in range(1, 7):
                    half = lambda a: a.rearrange("p h (b two m) -> p h b two m", two=2, m=1 << lv)
                    tX = {}
                    for g in range(2):
                        hs = slice(4 * g, 4 * g + 4)
                        bi, b, bf = ring.take()
                        t = T.mm([(b[:, n_ * 128:(n_ + 1) * 128], NL[:, 4 * g + n_, :], TI[:, 4 * g + n_, :], True, True)
                                  for n_ in range(4)], tT[g], tN[g], *bf)
                        if lv < 6:
                            tN[g] = G.tt(NL[:, hs, :], GBm[:, hs, 0:128], lmT(lv + 1), ALU.mult, t)
                        tX[g] = A.act(XB[:, hs, :], b.rearrange("p (h n) -> p h n", h=4), ACT.Copy, t, tU.get(g), pe_prev)
                        ring.give(bi, tX[g])
                    if lv == 1 and lat:
                        bi, b, bf = ring.take()
                        u["co"] = t = T.mm([(b[:, 0:8], e2[:, m, :], IRK[:, m, :], m == 0, m == 3) for m in range(4)],
                                           u["prep"], *bf)
                        ring.give(bi, accumulate(("coef", c), COEF[:, c - 2, :], b[:, 0:8], t))
                    elif lv in (2, 3):
                        bi, b, bf = ring.take()
                        u["kb"] = t = T.tr([(b[:, m * 128:(m + 1) * 128], KB[:, lv - 2, m, :]) for m in range(4)], ident, t_ar, *bf)
                        t_knb = A.act(KNB[:, lv - 2, :], b, ACT.Copy, t, pe_prev)
                        ring.give(bi, t_knb)
                    next(ahead, None)
                    yield
                    for g in range(2):
                        hs = slice(4 * g, 4 * g + 4)
                        bi, b, bf = ring.take()
                        grp = []
                        for n_ in range(4):
                            h = slice(4 * g + n_, 4 * g + n_ + 1)
                            grp.append((b[:, 256 + n_ * 64:320 + n_ * 64], XB[:, 4 * g + n_, :],
                                        half(TT[:, h, :])[:, 0, :, 1 - d, :], True, True))
                        if lv < 6:
                            for n_ in range(4):
                                h = slice(4 * g + n_, 4 * g + n_ + 1)
                                grp.append((b[:, n_ * 64:(n_ + 1) * 64], TT[:, 4 * g + n_, :],
                                            half(XB[:, h, :])[:, 0, :, d, :], True, True))
                        tU[g] = t = T.mm(grp, tX[g], tTT[g], *bf)
                        if lv < 6:
                            o = half(TI[:, hs, :])[:, :, :, d, :]
                            tT[g] = V.tt(o, o, b[:, 0:256].rearrange("p (h b m) -> p h b m", h=4, m=1 << lv), ALU.add, t)
                        o = half(TT[:, hs, :])[:, :, :, 1 - d, :]
                        tTT[g] = V.tt(o, o, b[:, 256:512].rearrange("p (h b m) -> p h b m", h=4, m=1 << lv), ALU.add, t)
                        ring.give(bi, tTT[g])
                    next(ahead, None)
                    yield
                for _ in ahead:
                    pass
                bi, b, bf = ring.take()
                t = T.mm([(b[:, h * 64:(h + 1) * 64], TT[:, h, :], X0[:, h * 64:(h + 1) * 64], True, True) for h in range(8)],
                         t_x0, tTT[0], tTT[1], *bf)
                t_sa = A.act(SA, b, ACT.Copy, t, pe_prev)
                ring.give(bi, t_sa)
                yield
                bi, b, bf = ring.take()
                grp = []
                for m in range(4):
                    o, ms = b[:, m * 128:(m + 1) * 128], slice(m * 128, (m + 1) * 128)
                    grp.append((o, KNB[:, 0, ms], VR[:, c, ms], True, False))
                    grp.append((o, KNB[:, 1, ms], SA[:, ms], False, True))
                pe_prev = t = T.mm(grp, t_sa, t_knb, *bf)
                V.tt(MS, b.rearrange("p (m v) -> p m v", m=4), bm(C["blk64"], 4), ALU.mult, t)
                ring.give(bi, V.last())
                V.tt(MS, MS, MP, ALU.add)
                V.tt(MS, MS, bc(DD, 128), ALU.mult)
                if lat:
                    bi, b, bf = ring.take()
                    grp = []
                    for m in range(4):
                        grp.append((b[:, m * 128:(m + 1) * 128], AR[:, m, 1, :], MP[:, m, :], True, False))
                        for h in (2 * m, 2 * m + 1):
                            o, hs = b[:, h * 64:(h + 1) * 64], slice(h * 64, (h + 1) * 64)
                            grp.append((o, GKm[:, h, 128:256], VR[:, c, hs], False, False))
                            grp.append((o, GBm[:, h, 128:256], SA[:, hs], False, h % 2 == 1))
                    pe_prev = t = T.mm(grp, t_sa, *bf)
                    adds = ("y", c) in opened
                    ring.give(bi, accumulate(("y", c), YS[:, c - 2, :], b, t))
                    if adds:
                        q_ = XB.rearrange("p h n -> p (h n)")[:, 0:512]
                        if (d, n) == (1, 5):
                            last_one.append(finish(c, banks, KK[:, 0, 0:512], stg, t))
                        else:
                            yield
                            yield from finish(c, ring, q_, stg, t)
                yield
            ends_of[d] = [T.last(), V.last(), A.last(), G.last()]

        d_i, d_y0 = dsem(), dsem()
        t_i0 = Y.dma(idxd.rearrange("(r b) o -> r (b o)", b=NB), T_["zeros_i"], d_i)
        t_y0 = Y.dma(ydv[:, 32:32 + OVF, :], T_["zeros"].unsqueeze(1).broadcast_to([128, OVF, D]), d_y0)

        ar.top = mark4
        rings = [Slots(banks.bufs[4 * d:4 * d + 4]) for d in range(2)]
        for r_ in rings:
            for j in range(4):
                r_.give(j, *f6)
        assert W.slots.i % 3 == 1
        own = [[region(4096, 12288), region(mark0 + 4096, mark0 + 8192)],
               [region(0, 4096), region(mark0, mark0 + 4096), region(base, base + 2048)]]
        woven = [recurrence(d, own[d], rings[d]) for d in range(2)]
        for _ in range(LAG):
            next(woven[0])
        while woven:
            for s_ in list(woven):
                if next(s_, 0) == 0:
                    woven.remove(s_)

        f = fence()
        for j in range(8):
            banks.give(j, *f)
        for j in range(3):
            W.give(j, *ends_of[0 if j else 1])
        d_bk, d_xb, d_re = dsem(), dsem(), [dsem(), dsem()]
        t_hb = Y.dma(HT.rearrange("p k s -> p (k s)"), htd, d_bk, *ends_of[0], t_xd)
        t_xb = G.dma(X.rearrange("p t d -> p (t d)"), xd, d_xb, *f, t_xd)
        ar.top = b01_top = mark2 + 10240 + SMALL + 8192
        assert b01_top >= mark4
        B01 = ar.get(4096, b=2, m=4, s=512)
        MG = ar.get(4096, m=8, s=512)
        gt = [MK[:, 512 * i:512 * (i + 1)] for i in range(4)]
        t_re = [A.dma(B01[:, n].rearrange("p m s -> p (m s)"), brd[n], d_re[n], *f, t_brd) for n in range(2)]
        br = [B01[:, 0], B01[:, 1], B2]
        gj = 0
        grd = [None, None, None, None]
        t_mg = {}
        t_b01 = None
        for n in range(3):
            if n == 1:
                f = fence()
                ar.top = mark2 + 10240
                GP, GM = [ar.get(32, t=4, e=8) for _ in range(2)]
                GI, TIx = [ar.get(32, U32, t=4, e=8) for _ in range(2)]
                TV = ar.get(32, t=4, e=8)
                RT = ar.get(4 * 36, t=4, e=36)
                EQ, LE, E1, E2, IN, RK, Q_, QP, DM = [ar.get(128, t=4, e=32) for _ in range(9)]
                EF, DF, Gg = [ar.get(8, t=4, e=2) for _ in range(3)]
                grp, sm_, pg, dif, exd, g1_, g2_ = [ar.get(4) for _ in range(7)]
                gex = ar.get(16, t=4, e=4)
                OVi, OVx, cnt, ov, o1, onesr = [ar.get(32) for _ in range(6)]
                EID = ar.get(8)
                SUM = ar.get(160, t=5, e=32)
                DI = ar.get(8, I32, t=4, e=2)
                TOK = ar.get(4, I32)
                IDX = ar.get(NB, I32)
                keep = ar.top
                assert keep == mark2 + 10240 + SMALL, keep - mark2 - 10240
                rowA, gs, sh, n2 = [ar.get(1024) for _ in range(4)]
                sqb = n2
                WRT = ar.get(288, k=8, e=36)
                assert ar.top <= mk_top
                ar.top = mark2 + 2048
                ht = [ar.get(1024) for _ in range(4)]
                tt_ = [ar.get(512) for _ in range(2)]
                d_r = dsem()
                V.zero(onesr, *f, value=1.0)
                V.zero(GP, value=-3.0e38)
                V.zero(SUM[:, 0, :])
                V.zero(LE, value=-3.0e38)
                for dst, src in ((rowA, mods2[0, 2048:3072].partition_broadcast(128)), (gs, mods2[0, 4096:5120].partition_broadcast(128)),
                                 (sh, mods2[0, 3072:4096].partition_broadcast(128)), (n2, T_["norm2_g_2"].partition_broadcast(128)),
                                 (WRT, T_["w_router"].rearrange("(k p) e -> p k e", p=128)), (TOK, T_["tok"])):
                    t_l = G.dma(dst, src, d_r, *t_m2, *f)
                t_gs = V.stt(gs, gs, 1.0, n2, ALU.add, ALU.mult, t_l)
            g0 = chunk(34 + 2 * n)
            wbr = chunk(40 + n)
            g1 = chunk(35 + 2 * n)
            wb3 = wbr[1].rearrange("p (k n) -> p k n", k=4)
            for m in range(8):
                gs_ = g0 if m < 4 else g1
                wg = gs_[1].rearrange("p (k n) -> p k n", k=8)
                mc = slice((m % 4) * 128, (m % 4 + 1) * 128)
                bi, b, bf = banks.take()
                t = T.mm([(b, wg[:, k, mc], HT[:, k, :], k == 0, k == 7) for k in range(8)], gs_[2], t_hb, *bf)
                t_gates = t
                next(last_one[0], None)
                if m % 4 == 3:
                    W.give(gs_[0], t)
                gg = gt[gj % 4]
                tg = A.act(gg, b, ACT.Sigmoid, t, *f, grd[gj % 4])
                banks.give(bi, tg)
                bi, b, bf = banks.take()
                t = T.mm([(b, wb3[:, k, m * 128:(m + 1) * 128], br[n][:, k, :], k == 0, k == 3) for k in range(4)],
                         wbr[2], *(t_b2 if n == 2 else [t_re[n]]), *bf)
                if m == 7:
                    W.give(wbr[0], t)
                    t_b01 = t if n == 1 else t_b01
                if n == 0:
                    t = V.tt(MG[:, m, :], gg, b, ALU.mult, tg, t, *f)
                    banks.give(bi, t)
                else:
                    t = V.tt(gg, gg, b, ALU.mult, tg, t)
                    banks.give(bi, t)
                    t = V.tt(MG[:, m, :], MG[:, m, :], gg, ALU.add)
                grd[gj % 4] = t
                t_mg[m] = t
                gj += 1
        wo = [chunk(43), chunk(44)]
        fdv = fd.rearrange("(t p) d -> p t d", p=128)
        d_fd = dsem()
        t_fd, t_x2, t_h = [], [], {}
        f5_ = transposed(HT, [t_gates])

        def route(i):
            f5_(i, ht[i], t_h[i])
            bi, b, bf = banks.take()
            o = b[:, 0:36]
            t = T.mm([(o, HT[:, k, i * 128:(i + 1) * 128], WRT[:, k, :], k == 0, k == 7) for k in range(8)],
                     *f5_.done[-2:], t_l, *bf)
            banks.give(bi, V.cp(RT[:, i, :], o, t))
            V.cp(GP[:, i, 0:4], RT[:, i, 0:4])
            V.put([lambda e: e.max(GM[:, i, :], GP[:, i, :])], [])
            V.put([lambda e: e.max_index(GI[:, i, :], GM[:, i, :], GP[:, i, :])], [])
            V.cp(grp[:, i:i + 1], GI[:, i, 0:1])
            V.ts(EQ[:, i, :], C["grp32"], grp[:, i:i + 1], None, ALU.is_equal, None)
            V.pred(LE[:, i, :], EQ[:, i, :].bitcast(U32), RT[:, i, 4:36])
            V.put([lambda e: e.max(TV[:, i, :], LE[:, i, :])], [])
            V.put([lambda e: e.max_index(TIx[:, i, :], TV[:, i, :], LE[:, i, :])], [])
            V.cp(EF[:, i, :], TIx[:, i, 0:2])
            V.ts(E1[:, i, :], C["iota32"], EF[:, i, 0:1], None, ALU.is_equal, None)
            V.ts(E2[:, i, :], C["iota32"], EF[:, i, 1:2], None, ALU.is_equal, None)
            V.tt(IN[:, i, :], E1[:, i, :], E2[:, i, :], ALU.add)
            return V.tt(SUM[:, i + 1, :], SUM[:, i, :], IN[:, i, :], ALU.add)

        ss = small
        for i in range(5):
            if i < 4:
                for hf in range(2):
                    ws, wb, wt = wo[hf]
                    w = wb.rearrange("p (k n) -> p k n", k=8)
                    bi, b, bf = banks.take()
                    t = T.mm([(b, MG[:, k, i * 128:(i + 1) * 128], w[:, k, :], k == 0, k == 7) for k in range(8)],
                             wt, *t_mg.values(), *bf)
                    if i == 3:
                        W.give(ws, t)
                    tq = tt_[hf]
                    t = V.tt(tq, b, rowA[:, hf * 512:(hf + 1) * 512], ALU.mult, t, t_l)
                    banks.give(bi, t)
                    xs = X[:, i, hf * 512:(hf + 1) * 512]
                    t_x2.append(V.tt(xs, xs, tq, ALU.add, t_xb))
                t = A.act(sqb, X[:, i, :], ACT.Square, t_x2[-1], accum_out=ss[:, i:i + 1])
                t = A.act(ss[:, 8 + i:9 + i], ss[:, i:i + 1], ACT.Sqrt, bias=eps[:, 0:1], scale=1.0 / D)
                V.rec(ss[:, 16 + i:17 + i], ss[:, 8 + i:9 + i], t)
                V.stt(ht[i], X[:, i, :], ss[:, 16 + i:17 + i], gs, ALU.mult, ALU.mult)
                t_h[i] = V.tt(ht[i], ht[i], sh, ALU.add)
                t_fd.append(A.dma(fdv[:, i, :], ht[i], d_fd, t_h[i]))
            if i >= 1:
                t = route(i - 1)

        bi, b, bf = banks.take()
        flat = lambda a: a.rearrange("p t e -> p (t e)")
        g_ = [(b[:, 0:128], C["tri"], flat(IN), True, False), (b[:, 0:128], ones, flat(SUM[:, 0:4, :]), False, True),
              (b[:, 128:160], ones, SUM[:, 4, :], True, True)]
        t = T.mm(g_, t, *bf)
        V.cp(RK, b[:, 0:128].rearrange("p (t e) -> p t e", t=4), t)
        t = V.cp(cnt, b[:, 128:160])
        banks.give(bi, t)
        V.ts(ov, cnt, 128.5, None, ALU.is_ge, None)
        for th in (256.5, 384.5):
            V.stt(ov, cnt, th, ov, ALU.is_ge, ALU.add)
        V.scan(OVi, onesr, ov)
        V.tt(OVx, OVi, ov, ALU.subtract)
        V.ts(QP, RK, 127.5, None, ALU.is_ge, None)
        V.stt(Q_, RK, 255.5, QP, ALU.is_ge, ALU.add)
        V.stt(Q_, RK, 383.5, Q_, ALU.is_ge, ALU.add)
        V.stt(RK, Q_, -128.0, RK, ALU.mult, ALU.add)
        V.tt(DM, Q_, bm(OVx, 4), ALU.add)
        V.stt(DM, DM, 31.0, bm(C["iota32"], 4), ALU.add, ALU.subtract)
        V.tt(DM, DM, QP, ALU.mult)
        V.tt(DM, DM, bm(C["iota32"], 4), ALU.add)
        V.stt(DM, RK, float(NB), DM, ALU.mult, ALU.add)
        for j, E_ in enumerate((E1, E2)):
            V.tt(E_, E_, DM, ALU.mult)
            V.red(DF[:, :, j:j + 1], E_, ALU.add)
        t_di = V.cp(DI, DF)
        d_s = dsem()
        for i in range(4):
            for j in range(2):
                tok = d_s.add()
                G.items.append(([lambda e, i=i, j=j: e.indirect_dma_start(
                    idxd, bass.IndirectOffsetOnAxis(ap=DI[:, i, j:j + 1], axis=0), TOK[:, i:i + 1], None)],
                    [t_di, t_i0, t_l], (d_s.sem, 16)))
        d_ix = dsem()
        t_idx = G.dma(IDX, idxd.rearrange("(r b) o -> r (b o)", b=NB), d_ix, tok)
        t_iov = V.cp(iovn, OVi[:, 31:32])
        for j in range(OVF):
            V.ts(o1, OVi, j + 0.5, None, ALU.is_le, None)
            V.red(EID[:, j:j + 1], o1, ALU.add)
        V.ts(EID[:, 0:OVF], EID[:, 0:OVF], 31.0, None, ALU.min, None)
        t_iov = V.cp(iov[:, 0:OVF], EID[:, 0:OVF])
        V.ts(pg.unsqueeze(2), GM[:, :, 0:1], -1.0, None, ALU.mult, None)
        t = V.tt(gex, RT[:, :, 0:4], bc(pg, 4), ALU.add)
        t = A.act(gex, gex, ACT.Exp, t)
        V.red(sm_, gex, ALU.add, t)
        V.rec(pg, sm_)
        t = V.tt(dif.unsqueeze(2), TV[:, :, 1:2], TV[:, :, 0:1], ALU.subtract)
        t = A.act(exd, dif, ACT.Exp, t)
        V.ts(g1_, exd, 1.0, None, ALU.add, None, t)
        V.rec(g1_, g1_)
        V.tt(g1_, g1_, pg, ALU.mult)
        V.tt(g2_, g1_, exd, ALU.mult)
        V.cp(Gg[:, :, 0], g1_)
        t_gate = V.cp(Gg[:, :, 1], g2_)

        f = fence() + [t_fd[-1], t_y0, t_i0, t_idx]
        ar.top = mark2 + 8192
        YO = [ar.get(1024) for _ in range(2)]
        ar.top = keep
        rest = [ar.get(4096) for _ in range(2)]
        assert ar.top == b01_top
        ar.top += 4096
        rest += [ar.get(4096), HT.rearrange("p k s -> p (k s)")]
        ar.top = mark2
        XG = [ar.get(1024) for _ in range(2)]
        XT = [ar.get(1024, k=8, s=128) for _ in range(2)]
        SGm = [ar.get(512) for _ in range(2)]
        AC = [ar.get(512) for _ in range(2)]
        ACT_T = [ar.get(512, k=4, s=128) for _ in range(2)]
        rowC = ar.get(1024)
        assert ar.top <= mark2 + 8192
        j = W.slots.i % 3
        WE = Stream()
        for k in (j, None, (j + 1) % 3, (j + 2) % 3):
            if k is None:
                WE.grow([B01.rearrange("p b m s -> p (b m s)")], t_b01)
            else:
                WE.grow([W.slots.bufs[k]], *W.slots.free[k])
        t_rc = mod_load(rowC, 2, 5, f)
        d_xg = [dsem() for _ in range(2)]
        d_yo = [dsem() for _ in range(2)]

        class Experts:
            def __init__(self, L, W_, f, dx, dy):
                self.L, self.W, self.f = L, W_, f
                self.s = {}
                self.dx, self.dy = dx, dy
                self.done = []

            def gather(self, e, idx_ap):
                p, tok = e % 2, self.dx[e % 2].add()
                self.L["G"].items.append(([lambda eng: eng.indirect_dma_start(
                    XG[p], None, fd, bass.IndirectOffsetOnAxis(ap=idx_ap, axis=0))],
                    [t_idx, *t_fd, *self.f, self.s.get(("tr", e - 2))], (self.dx[p].sem, 16)))
                self.s["xg", e] = tok

            def weights(self, e, src):
                self.s["w", e] = [self.W.load(src(j), self.L["Y"]) for j in range(3)]

            def turn(self, e):
                T, V, s, p = self.L["T"], self.L["V"], self.s, e % 2
                for half in range(2):
                    bi, b, bf = banks.take()
                    t = T.tr([(b[:, q * 128:(q + 1) * 128], XG[p][:, (4 * half + q) * 128:(4 * half + q + 1) * 128])
                              for q in range(4)], ident, s["xg", e], *bf)
                    o = XT[p][:, 4 * half:4 * half + 4, :]
                    te = V.cp(o, b.rearrange("p (q s) -> p q s", q=4), t, s.get(("up", e - 2)), *self.f)
                    banks.give(bi, te)
                    s["xt", e, half] = te
                s["tr", e] = t

            def enter(self, e, j):
                T, V, A, s, p = self.L["T"], self.L["V"], self.L["A"], self.s, e % 2
                ws, wb, wt = s["w", e][j]
                wv = wb.rearrange("p (k n) -> p k n", k=8)
                bi, b, bf = banks.take()
                t = T.mm([(b, XT[p][:, k, :], wv[:, k, :], k == 0, k == 7) for k in range(8)],
                         wt, s["xt", e, 0], s["xt", e, 1], *bf)
                self.W.give(ws, t)
                if j == 0:
                    t = A.act(SGm[p], b, ACT.Sigmoid, t, s.get(("ac", e - 2)), *self.f)
                    t = V.tt(SGm[p], SGm[p], b, ALU.mult, t)
                else:
                    s["up", e] = t
                    s["ac", e] = t = V.tt(AC[p], SGm[p], b, ALU.mult, t, s.get(("at", e - 2)))
                banks.give(bi, t)

            def turn_back(self, e):
                T, A, s, p = self.L["T"], self.L["A"], self.s, e % 2
                bi, b, bf = banks.take()
                s["at", e] = t = T.tr([(b[:, q * 128:(q + 1) * 128], AC[p][:, q * 128:(q + 1) * 128]) for q in range(4)],
                                      ident, s["ac", e], *bf)
                s["act", e] = t = A.act(ACT_T[p], b.rearrange("p (q s) -> p q s", q=4), ACT.Copy, t,
                                        s.get(("dn", e - 2)), *self.f)
                banks.give(bi, t)

            def leave(self, e, blk):
                T, A, s, p = self.L["T"], self.L["A"], self.s, e % 2
                ws, wb, wt = s["w", e][2]
                wv = wb.rearrange("p (k n) -> p k n", k=4)
                for hf in range(2):
                    bi, b, bf = banks.take()
                    td = T.mm([(b, ACT_T[p][:, k, :], wv[:, k, hf * 512:(hf + 1) * 512], k == 0, k == 3) for k in range(4)],
                              wt, s["act", e], *bf)
                    o = YO[p][:, hf * 512:(hf + 1) * 512]
                    ty = A.act(o, b, ACT.Copy, td, s.get(("yo", e - 2)), *self.f)
                    banks.give(bi, ty)
                s["dn", e] = td
                self.W.give(ws, td)
                s["yo", e] = A.dma(ydv[:, blk, :], YO[p], self.dy[p], ty, t_y0)
                self.done.append(s["yo", e])

            def run(self, n, first_block, src, gathered=lambda: None):
                idx = lambda e: IDX[:, first_block + e:first_block + e + 1]
                self.gather(0, idx(0))
                self.gather(1, idx(1))
                gathered()
                self.weights(0, src(0))
                self.turn(0)
                for e in range(n + 1):
                    if e < n:
                        if e and e + 1 < n:
                            self.gather(e + 1, idx(e + 1))
                        self.enter(e, 0)
                    if e >= 1:
                        self.turn_back(e - 1)
                    if e < n:
                        self.enter(e, 1)
                    if e + 1 < n:
                        self.turn(e + 1)
                    if e >= 1:
                        self.leave(e - 1, first_block + e - 1)
                    if e + 1 < n:
                        self.weights(e + 1, src(e + 1))

        ex = Experts(main, WE, f, d_xg, d_yo)
        ex.run(32, 0, lambda e: lambda j: T_["w"][45 + 3 * e + j], lambda: WE.grow(rest, *f, ex.s["xg", 1]))
        t_yd = ex.done[-2:]

        f = fence() + t_yd
        ovl = {n: Lane(sem(f"o_{n}"), n in "VAG") for n in "TVAGY"}
        saved = (banks.free, banks.i)
        banks.free = [[] for _ in banks.bufs]

        WO = Stream()
        WO.grow(WE.slots.bufs[0:6])
        ev = {}
        oex = Experts(ovl, WO, [], [dsem(), dsem()], [dsem(), dsem()])
        for n in "TVAGY":
            ovl[n].items.append(([], f, None))
        regs = {}

        def load(s_, lane):
            j, q = s_
            k, buf, free = WO.slots.take()
            tok = WO.d[k].add()

            def go(e):
                if q == 0:
                    regs[j] = e.value_load(iov[0:1, j:j + 1], min_val=0, max_val=31)
                return e.dma_start(buf, T_["w"][bass.ds(regs[j] * 3 + (45 + q), 1)][0])
            lane.items.append(([go], free, (WO.d[k].sem, 16)))
            return k, buf, tok
        WO.load = load
        oex.run(OVF, 32, lambda j: lambda q: (j, q))
        ovl["A"].items.append(([], oex.done[-2:], None))
        ovl["G"].items.append(([], oex.done[-2:] + [ovl["T"].last(), ovl["V"].last(), ovl["A"].last()], None))
        banks.free, banks.i = saved

        tail = {n: Lane(sem(f"t_{n}"), n in "VAG") for n in "TVAGY"}
        V2, G2_, A2_, Y2 = [tail[n] for n in "VGAY"]
        t_out = []
        y12 = [[WE.slots.bufs[i // 2][:, 1024 * (2 * (i % 2) + j):1024 * (2 * (i % 2) + j + 1)] for j in range(2)] for i in range(4)]
        d_y = [dsem() for _ in range(4)]
        d_o = dsem()
        t_all = [*t_yd, t_y0, T.last(), V.last(), A.last()]
        for i in range(4):
            for j in range(2):
                d_y[i].add()
                G2_.items.append(([lambda e, i=i, j=j: e.indirect_dma_start(
                    y12[i][j], None, yd, bass.IndirectOffsetOnAxis(ap=DI[:, i, j:j + 1], axis=0))],
                    t_all, (d_y[i].sem, 16)))
        for i in range(4):
            bufs, ty = y12[i], (d_y[i].sem, d_y[i].n)
            t = A2_.act(bufs[0], bufs[0], ACT.Identity, ty, t_gate, scale=Gg[:, i, 0:1])
            V2.stt(bufs[0], bufs[1], Gg[:, i, 1:2], bufs[0], ALU.mult, ALU.add, t, ty, t_rc)
            t = V2.tt(bufs[0], bufs[0], rowC, ALU.mult)
            if i % 2:
                t = V2.tt(X[:, i, :], X[:, i, :], bufs[0], ALU.add)
            else:
                t = G2_.tt(X[:, i, :], X[:, i, :], bufs[0], ALU.add, t)
            t_out.append(Y2.dma(out_d[:, i, :], X[:, i, :], d_o, t))
        Y2.items.append(([], t_out[-1:], None))

        block = ctx.enter_context(nc.Block())

        def program(eng, n):
            seen = {}
            main[n].run(eng, seen)
            eng.wait_ge(V.sem, t_iov[1])
            r = eng.value_load(iovn[0:1, 0:1], min_val=0, max_val=OVF)
            with eng.If(r > 0):
                ovl[n].run(eng, dict(seen))
            tail[n].run(eng, dict(seen))

        @block.sync
        def _(e):
            program(e, "Y")

        @block.gpsimd
        def _(e):
            program(e, "G")

        @block.scalar
        def _(e):
            program(e, "A")

        @block.vector
        def _(e):
            program(e, "V")

        @block.tensor
        def _(e):
            program(e, "T")


def chunks(i):
    def cut(w, k, n):
        r, c = w.shape
        return [w[:, j * n:(j + 1) * n].reshape(k, 128, n).transpose(1, 0, 2).reshape(128, k * n) for j in range(c // n)]

    w2 = i["w_in_2"][0]
    mid = np.zeros((1024, 512), np.float32)
    mid[:, 0:384] = w2[:, 3584:3968]
    out = np.empty((141, 128, 4096), np.float32)
    at = 0
    parts = [(i["w_ada"][0], 8, 512), (i["w_in"][0], 8, 512), (i["w_out"][0], 8, 512), (i["w_ada_2"][0], 8, 512),
             (w2[:, 0:3584], 8, 512), (mid, 8, 512), (w2[:, 3968:7040], 8, 512)]
    parts += [(i["w_br_2"][0, n], 4, 1024) for n in range(3)] + [(i["w_out_2"][0], 8, 512)]
    for e in range(32):
        parts += [(i["w_exp_gate_2"][0, e], 8, 512), (i["w_exp_up_2"][0, e], 8, 512), (i["w_exp_down_2"][0, e], 4, 1024)]
    for w, k, n in parts:
        for c in cut(w, k, n):
            out[at] = c
            at += 1
    assert at == 141
    return out


def params(i):
    def col(v):
        return np.ascontiguousarray(v, np.float32).reshape(-1, 128).T

    p = {
        "c": col(i["c"]), "c2": col(i["c_2"]), "cc": col(i["c_ctx_2"]), "conv_w": col(i["conv_w"][0]),
        "conv_b": col(i["conv_b"]), "b_a": col(i["b_rg_a"]), "b_x": col(i["b_rg_x"]), "lam": col(i["lru_lambda"]),
        "norm_rec": col(i["norm_rec"]), "qn": col(np.tile(i["q_norm_g_2"][0], 2)), "kn": col(np.tile(i["k_norm_g_2"][0], 2)),
        "mu0": col(i["shift_mu_2"][0, 0]), "mu1": col(i["shift_mu_2"][0, 1]), "w0": col(i["decay_w0_2"][0]),
        "a0": col(i["aaa_a0_2"][0]), "k_k": col(i["k_k_2"]), "k_a": col(i["k_a_2"]), "r_k": col(i["r_k_2"]),
        "pscale": col(i["pool_scale_2"]), "b_mod": col(i["b_ada"][0, 0:2048]), "npre": col(i["norm_pre"][0]),
    }
    return np.concatenate([p[n] for n, _ in COL_SPEC], 1)


def lru_weights(i):
    out = np.zeros((128, 8, 128), np.float32)
    for j, n in enumerate(("w_rg_a", "w_rg_x")):
        for h in range(8):
            o = 64 * (h % 2)
            out[o:o + 64, 4 * j + h // 2, o:o + 64] = i[n][0, h]
    return out.reshape(128, 1024)


def constants():
    p = np.arange(128)
    c = {n: np.zeros((128, w), np.float32) for n, w in CONST_SPEC}
    c["ident"][:] = np.eye(128)
    c["ones"][:] = 1
    c["blk64"][:] = (p[:, None] // 64 == p[None] // 64)
    s1 = (p // 64) * 64 + (p % 64 + 32) % 64
    c["perm1"][s1, p] = 1
    s2 = (p // 32) * 32 + (p % 32 + 16) % 32
    c["perm2"][s2, p] = 1
    c["tri"][:] = p[:, None] < p[None]
    for j in range(18):
        c["selp"][j, 2 * j:2 * j + 2] = 1
    f = (10000.0 ** (-np.arange(32) / 32.0)).astype(np.float32)
    c["invf"][:, 0] = f[p % 32]
    c["sgn"][:, 0] = np.where(p % 64 < 32, -1, 1)
    c["iota32"][:] = np.arange(32)
    c["grp32"][:] = np.arange(32) // 8
    for m in range(4):
        c["ind"][p, 8 * m + 2 * m + p // 64] = 1
    return np.concatenate([c[n] for n, _ in CONST_SPEC], 1)


def mask_constants():
    p = np.arange(128)
    t, s = p[:, None], p[None]
    c = {}
    for d in range(2):
        lv = []
        for b in range(7):
            m = 1 << b
            same = t // (2 * m) == s // (2 * m)
            tb, sb_ = (t // m) % 2, (s // m) % 2
            lv.append(same & ((tb == 1) & (sb_ == 0) if d == 0 else (tb == 0) & (sb_ == 1)))
        c["lm%d" % d] = np.concatenate(lv, 1)
        before = (t < s) if d == 0 else (t > s)
        c["si%d" % d] = np.concatenate([before, before | (t == s)], 1)
        c["sb%d" % d] = (s < t) if d == 0 else (s > t)
    return np.concatenate([c[n] for n, _ in MASK_SPEC], 1).astype(np.float32)


def rope_constants():
    tok = np.arange(S)
    f = (10000.0 ** (-np.arange(16) / 16.0)).astype(np.float32)
    rows, cols = (tok // 64).astype(np.float32), (tok % 64).astype(np.float32)
    p = np.arange(128)
    pos = np.where(((p % 64) < 32)[:, None], rows[None], cols[None])
    ang = (pos * f[p % 16][:, None]).astype(np.float32).astype(np.float64)
    sgn = np.where(p % 32 < 16, -1.0, 1.0)[:, None]
    cnt = []
    for w in (2, 4, 8, 16):
        lo = np.clip(tok - w // 2, 0, S - 1)
        hi = np.clip(tok + w // 2 - 1, 0, S - 1)
        cnt.append(np.broadcast_to(1.0 / (hi - lo + 1), (128, S)))
    return np.concatenate([np.cos(ang), np.sin(ang) * sgn] + cnt, 1).astype(np.float32)


def multiplicities():
    out = []
    for i in range(4):
        q = np.arange(128)[:, None] + 128 * i
        k = np.arange(128 * (i + 1))[None]
        dist = q - k
        n = ((dist >= 0) & (dist <= 128)).astype(int) + ((dist >= 0) & (dist % 4 == 0)) + ((dist >= 0) & (dist % 16 == 0))
        out.append(np.where(n > 0, np.log(np.maximum(n, 1)), -1e30))
    return np.concatenate(out, 1).astype(np.float32)


def arrays_of(i):
    i = {k: np.asarray(v) for k, v in i.items()}
    a = {
        "w": chunks(i), "params": params(i), "consts": constants(), "masks": mask_constants(), "ropes": rope_constants(),
        "lnc": multiplicities(), "w_rg": lru_weights(i),
        "bias": np.concatenate([i["b_ada"][0].reshape(6, 512), i["b_ada_2"][0].reshape(12, 512)], 0),
        "x": i["x"], "positions": i["positions"].astype(np.int32) if i["positions"].dtype != np.int32 else i["positions"],
        "norm_pre": i["norm_pre"][0], "norm_post": i["norm_post"][0], "norm_att": i["norm_att"][0],
        "ctx_2": i["ctx_2"], "norm1_g_2": i["norm1_g_2"][0], "norm2_g_2": i["norm2_g_2"][0],
        "pool_w_2": i["pool_w_2"], "lambda_qk_2": i["lambda_qk_2"], "subln": np.tile(i["subln_g_2"][0], 4),
        "decay_w2": i["decay_w2_2"][0].reshape(128, 512), "aaa_a2": i["aaa_a2_2"][0].reshape(128, 512),
        "gate_w2": i["gate_w2_2"][0], "gn_w_2": i["gn_w_2"], "gn_b_2": i["gn_b_2"],
        "w_router": np.concatenate([i["w_router_group_2"][0], i["w_router_expert_2"][0]], 1),
        "zeros": np.zeros((128, 1024), np.float32), "zeros_i": np.zeros((128, NB), np.int32),
        "tok": (np.arange(4)[None] * 128 + np.arange(128)[:, None]).astype(np.int32),
    }
    return {k: np.ascontiguousarray(v) for k, v in a.items()}


def kernel(**inputs):
    import concourse.bacc as bacc
    from concourse.bass_utils import run_bass_kernel_spmd

    nc = bacc.Bacc("TRN2", target_bir_lowering=False, num_devices=1)
    a = arrays_of(inputs)
    t = {n: nc.dram_tensor(f"in_{n}", v.shape, mybir.dt.from_np(v.dtype), kind="ExternalInput").ap() for n, v in a.items()}
    t["out"] = nc.dram_tensor("out", (1, S, D), F, kind="ExternalOutput").ap()
    build(nc, t)
    r = run_bass_kernel_spmd(nc, [{f"in_{n}": v for n, v in a.items()}], core_ids=[0])
    return r.results[0]["out"]
```
